# Optimizing a Trainium2 kernel written in Bass

```python
import jax, jax.numpy as jnp
from jax import lax
import numpy as np
import math

D_MODEL = 1024
BATCH = 1
SEQ = 512
DEPTH = 1

HEAD_DIM = 64
N_HEADS_A = 8
N_KV_A = 2
N_HEADS_B = 8
N_KV_B = 2
WIDTH_A = N_HEADS_A * HEAD_DIM
WIDTH_B = N_HEADS_B * HEAD_DIM
MIX_WIDTH = WIDTH_A + WIDTH_B
Q_BLOCK = 128
WINDOW = 128
GRID_W = 64
ROPE_THETA = 10000.0
EPS = 1e-6
D_FF = ((8 * D_MODEL + 3 * 256 - 1) // (3 * 256)) * 256
IN_COLS = (N_HEADS_A + 2 * N_KV_A + N_HEADS_B + 2 * N_KV_B) * HEAD_DIM
SPLITS = tuple(int(s) for s in np.cumsum([WIDTH_A, N_KV_A * HEAD_DIM, N_KV_A * HEAD_DIM,
                                           WIDTH_B, N_KV_B * HEAD_DIM])[:])


def rms_norm(x, g):
    xf = x.astype(jnp.float32)
    y = xf * lax.rsqrt(jnp.mean(xf * xf, axis=-1, keepdims=True) + EPS)
    return (y * g.astype(jnp.float32)).astype(x.dtype)

def apply_rope(x, ang):
    cos = jnp.cos(ang)[None, :, None, :].astype(x.dtype)
    sin = jnp.sin(ang)[None, :, None, :].astype(x.dtype)
    x1, x2 = jnp.split(x, 2, axis=-1)
    return jnp.concatenate([x1 * cos - x2 * sin, x2 * cos + x1 * sin], axis=-1)

def global_attention(q, k, v):
    B, S, Hq, D = q.shape
    Hkv = k.shape[2]
    G = Hq // Hkv
    nb = S // Q_BLOCK
    qb = q.reshape(B, nb, Q_BLOCK, Hkv, G, D).transpose(1, 0, 2, 3, 4, 5)
    scale = D ** -0.5

    def one_block(qi):
        s = jnp.einsum('bqkgd,bskd->bkgqs', qi, k).astype(jnp.float32) * scale
        p = jax.nn.softmax(s, axis=-1).astype(v.dtype)
        return jnp.einsum('bkgqs,bskd->bqkgd', p, v)

    o = lax.map(one_block, qb)
    return o.transpose(1, 0, 2, 3, 4, 5).reshape(B, S, Hq * D)

def window_attention(q, k, v, sink):
    B, S, Hq, D = q.shape
    Hkv = k.shape[2]
    G = Hq // Hkv
    nb = S // Q_BLOCK
    C = 3 * Q_BLOCK
    qb = q.reshape(B, nb, Q_BLOCK, Hkv, G, D)
    pad = ((0, 0), (Q_BLOCK, Q_BLOCK), (0, 0), (0, 0))
    kp = jnp.pad(k, pad).reshape(B, nb + 2, Q_BLOCK, Hkv, D)
    vp = jnp.pad(v, pad).reshape(B, nb + 2, Q_BLOCK, Hkv, D)
    kb = jnp.concatenate([kp[:, :-2], kp[:, 1:-1], kp[:, 2:]], axis=2)
    vb = jnp.concatenate([vp[:, :-2], vp[:, 1:-1], vp[:, 2:]], axis=2)
    scale = D ** -0.5
    s = jnp.einsum('bnqkgd,bnckd->bnkgqc', qb, kb).astype(jnp.float32) * scale
    blk = jnp.arange(nb)[:, None, None]
    qpos = blk * Q_BLOCK + jnp.arange(Q_BLOCK)[None, :, None]
    kpos = (blk - 1) * Q_BLOCK + jnp.arange(C)[None, None, :]
    valid = (jnp.abs(kpos - qpos) <= WINDOW) & (kpos >= 0) & (kpos < S)
    s = jnp.where(valid[None, :, None, None], s, -jnp.inf)
    sink_l = sink.astype(jnp.float32).reshape(1, 1, Hkv, G, 1, 1)
    m = jnp.maximum(jnp.max(s, axis=-1, keepdims=True), sink_l)
    e = jnp.exp(s - m)
    den = jnp.sum(e, axis=-1, keepdims=True) + jnp.exp(sink_l - m)
    p = (e / den).astype(v.dtype)
    o = jnp.einsum('bnkgqc,bnckd->bnqkgd', p, vb)
    return o.reshape(B, S, Hq * D)

def first_inputs(seed: int = 0) -> dict:
    key = jax.random.key(seed)
    ks = jax.random.split(key, 16)
    f32 = jnp.float32

    def gain(k, n):
        return 1.0 + 0.05 * jax.random.normal(k, (DEPTH, n), f32)

    def dense(k, fan_in, fan_out):
        return jax.random.normal(k, (DEPTH, fan_in, fan_out), f32) * fan_in ** -0.5

    return {
        "x": jax.random.normal(ks[0], (BATCH, SEQ, D_MODEL), f32),
        "norm_mix_pre": gain(ks[1], D_MODEL),
        "w_in": dense(ks[2], D_MODEL, IN_COLS),
        "q_norm_a": gain(ks[3], HEAD_DIM),
        "k_norm_a": gain(ks[4], HEAD_DIM),
        "sink_b": 0.5 * jax.random.normal(ks[5], (DEPTH, N_HEADS_B), f32),
        "group_norm_a": gain(ks[6], WIDTH_A),
        "group_norm_b": gain(ks[7], WIDTH_B),
        "w_out": dense(ks[8], MIX_WIDTH, D_MODEL),
        "norm_mix_post": gain(ks[9], D_MODEL),
        "norm_ffn_pre": gain(ks[10], D_MODEL),
        "w_gate": dense(ks[11], D_MODEL, D_FF),
        "w_up": dense(ks[12], D_MODEL, D_FF),
        "w_down": dense(ks[13], D_FF, D_MODEL),
        "norm_ffn_post": gain(ks[14], D_MODEL),
    }

def first_block(x, norm_mix_pre, w_in, q_norm_a, k_norm_a, sink_b, group_norm_a, group_norm_b,
              w_out, norm_mix_post, norm_ffn_pre, w_gate, w_up, w_down, norm_ffn_post):
    B, S, _ = x.shape
    rows = S // GRID_W
    t = jnp.arange(S, dtype=jnp.float32)
    row = jnp.broadcast_to(jnp.arange(rows, dtype=jnp.float32)[:, None], (rows, GRID_W)).reshape(S)
    col = jnp.broadcast_to(jnp.arange(GRID_W, dtype=jnp.float32)[None, :], (rows, GRID_W)).reshape(S)
    ax_pairs = HEAD_DIM // 4
    freq_ax = ROPE_THETA ** (-jnp.arange(ax_pairs, dtype=jnp.float32) / ax_pairs)
    ang_axial = jnp.concatenate([row[:, None] * freq_ax[None, :], col[:, None] * freq_ax[None, :]], axis=-1)
    n_pairs = HEAD_DIM // 2
    freq_1d = ROPE_THETA ** (-jnp.arange(n_pairs, dtype=jnp.float32) / n_pairs)
    ang_1d = t[:, None] * freq_1d[None, :]

    for l in range(DEPTH):
        h = rms_norm(x, norm_mix_pre[l])
        proj = h @ w_in[l]
        qa, ka, va, qb, kb, vb = jnp.split(proj, SPLITS, axis=-1)

        qa = apply_rope(rms_norm(qa.reshape(B, S, N_HEADS_A, HEAD_DIM), q_norm_a[l]), ang_axial)
        ka = apply_rope(rms_norm(ka.reshape(B, S, N_KV_A, HEAD_DIM), k_norm_a[l]), ang_axial)
        va = va.reshape(B, S, N_KV_A, HEAD_DIM)
        out_a = global_attention(qa, ka, va)

        qb = apply_rope(qb.reshape(B, S, N_HEADS_B, HEAD_DIM), ang_1d)
        kb = apply_rope(kb.reshape(B, S, N_KV_B, HEAD_DIM), ang_1d)
        vb = vb.reshape(B, S, N_KV_B, HEAD_DIM)
        out_b = window_attention(qb, kb, vb, sink_b[l])

        mixed = jnp.concatenate([rms_norm(out_a, group_norm_a[l]),
                                 rms_norm(out_b, group_norm_b[l])], axis=-1) @ w_out[l]
        x = x + rms_norm(mixed, norm_mix_post[l])

        h = rms_norm(x, norm_ffn_pre[l])
        f = (jax.nn.silu(h @ w_gate[l]) * (h @ w_up[l])) @ w_down[l]
        x = x + rms_norm(f, norm_ffn_post[l])
    return x


PLE_DIM = 256
D_POOL = D_MODEL // 2
POOL_WINDOWS = (2, 4, 8, 16)
N_POOL_GROUPS = len(POOL_WINDOWS)
POOL_GROUP_DIM = D_POOL // N_POOL_GROUPS
SB_HEADS = 8
SB_HEAD_DIM = 64
D_SB = SB_HEADS * SB_HEAD_DIM
D_FF_2 = ((8 * D_MODEL // 3 + 255) // 256) * 256
D_IN = D_POOL + 3 * D_SB + 2 * D_MODEL
RMS_EPS = 1e-6


def rms_norm_2(x, gain):
    xf = x.astype(jnp.float32)
    inv = lax.rsqrt(jnp.mean(xf * xf, axis=-1, keepdims=True) + RMS_EPS)
    return (xf * inv * gain.astype(jnp.float32)).astype(x.dtype)

def pool_mixer(u, w_pool, pool_scale):
    B, S, _ = u.shape
    uf = u.astype(jnp.float32)
    csum = jnp.cumsum(uf, axis=1)
    t = jnp.arange(S, dtype=jnp.int32)
    outs = []
    for g, w in enumerate(POOL_WINDOWS):
        sl = slice(g * POOL_GROUP_DIM, (g + 1) * POOL_GROUP_DIM)
        cg = csum[..., sl]
        prev = jnp.pad(cg, ((0, 0), (w, 0), (0, 0)))[:, :S]
        count = jnp.minimum(t + 1, w).astype(jnp.float32)[None, :, None]
        outs.append((cg - prev) / count - uf[..., sl])
    pooled = jnp.stack(outs, axis=2).astype(u.dtype)
    mixed = jnp.einsum('bsgc,gcd->bsgd', pooled, w_pool).reshape(B, S, D_POOL)
    return mixed * pool_scale

def stick_breaking_attention(q, k, v):
    B, H, S, dh = q.shape
    n_blk = S // Q_BLOCK
    scale = 1.0 / math.sqrt(dh)
    q_blocks = q.reshape(B, H, n_blk, Q_BLOCK, dh).transpose(2, 0, 1, 3, 4)
    starts = jnp.arange(n_blk, dtype=jnp.int32) * Q_BLOCK
    k_pos = jnp.arange(S, dtype=jnp.int32)

    def one_block(args):
        q_i, start = args
        z = jnp.einsum('bhqd,bhkd->bhqk', q_i, k).astype(jnp.float32) * scale
        t_pos = start + jnp.arange(Q_BLOCK, dtype=jnp.int32)
        mask = k_pos[None, :] < t_pos[:, None]
        log_fail = jnp.where(mask, jax.nn.log_sigmoid(-z), 0.0)
        suffix = lax.cumsum(log_fail, axis=3, reverse=True) - log_fail
        a = jnp.where(mask, jnp.exp(jax.nn.log_sigmoid(z) + suffix), 0.0)
        return jnp.einsum('bhqk,bhkd->bhqd', a.astype(v.dtype), v)

    out = lax.map(one_block, (q_blocks, starts))
    return out.transpose(1, 2, 0, 3, 4).reshape(B, H, S, dh)

def second_inputs(seed: int = 0) -> dict:
    key = jax.random.key(seed)
    ks = jax.random.split(key, 20)
    f32 = jnp.float32

    def nrm(k, shape, fan_in):
        return jax.random.normal(k, shape, f32) * (fan_in ** -0.5)

    def gain(k, shape):
        return jnp.ones(shape, f32) + 0.02 * jax.random.normal(k, shape, f32)

    return {
        "x": jax.random.normal(ks[0], (BATCH, SEQ, D_MODEL), f32),
        "p": jax.random.normal(ks[1], (DEPTH, BATCH, SEQ, PLE_DIM), f32),
        "norm_mix": gain(ks[2], (DEPTH, D_MODEL)),
        "w_in": nrm(ks[3], (DEPTH, D_MODEL, D_IN), D_MODEL),
        "w_pool": nrm(ks[4], (DEPTH, N_POOL_GROUPS, POOL_GROUP_DIM, POOL_GROUP_DIM), POOL_GROUP_DIM),
        "pool_scale": gain(ks[5], (DEPTH, D_POOL)),
        "w_branch_a": nrm(ks[6], (DEPTH, D_POOL, D_MODEL), D_POOL),
        "w_branch_b": nrm(ks[7], (DEPTH, D_SB, D_MODEL), D_SB),
        "w_out": nrm(ks[8], (DEPTH, D_MODEL, D_MODEL), D_MODEL),
        "norm_ffn": gain(ks[9], (DEPTH, D_MODEL)),
        "w_ffn_gate": nrm(ks[10], (DEPTH, D_MODEL, D_FF_2), D_MODEL),
        "w_ffn_up": nrm(ks[11], (DEPTH, D_MODEL, D_FF_2), D_MODEL),
        "w_ffn_down": nrm(ks[12], (DEPTH, D_FF_2, D_MODEL), D_FF_2),
        "norm_ple": gain(ks[13], (DEPTH, D_MODEL)),
        "w_ple_gate": nrm(ks[14], (DEPTH, D_MODEL, D_MODEL), D_MODEL),
        "w_ple_proj": nrm(ks[15], (DEPTH, PLE_DIM, D_MODEL), PLE_DIM),
        "norm_final": gain(ks[16], (D_MODEL,)),
    }

def second_block(x, p, norm_mix, w_in, w_pool, pool_scale, w_branch_a, w_branch_b, w_out,
              norm_ffn, w_ffn_gate, w_ffn_up, w_ffn_down, norm_ple, w_ple_gate, w_ple_proj,
              norm_final):
    B, S, _ = x.shape
    split_at = [D_POOL, D_POOL + D_SB, D_POOL + 2 * D_SB, D_POOL + 3 * D_SB,
                D_POOL + 3 * D_SB + D_MODEL]
    for i in range(DEPTH):
        h = rms_norm_2(x, norm_mix[i])
        proj = h @ w_in[i]
        u_pool, q, k, v, g_a, g_b = jnp.split(proj, split_at, axis=-1)
        y_a = pool_mixer(u_pool, w_pool[i], pool_scale[i])
        to_heads = lambda t: t.reshape(B, S, SB_HEADS, SB_HEAD_DIM).transpose(0, 2, 1, 3)
        y_b = stick_breaking_attention(to_heads(q), to_heads(k), to_heads(v))
        y_b = y_b.transpose(0, 2, 1, 3).reshape(B, S, D_SB)
        merged = (jax.nn.sigmoid(g_a) * (y_a @ w_branch_a[i])
                  + jax.nn.sigmoid(g_b) * (y_b @ w_branch_b[i]))
        x = x + merged @ w_out[i]
        h = rms_norm_2(x, norm_ffn[i])
        x = x + (jax.nn.silu(h @ w_ffn_gate[i]) * (h @ w_ffn_up[i])) @ w_ffn_down[i]
        gate = jax.nn.sigmoid(rms_norm_2(x, norm_ple[i]) @ w_ple_gate[i])
        x = x + gate * (p[i] @ w_ple_proj[i])
    return rms_norm_2(x, norm_final)


def setup_inputs(seed=0):
    out = dict(first_inputs(seed))
    for name, value in second_inputs(seed + 1).items():
        if name != "x":
            out[name + "_2"] = value
    return out


def reference(
    x, norm_mix_pre, w_in, q_norm_a, k_norm_a, sink_b, group_norm_a, group_norm_b, w_out,
    norm_mix_post, norm_ffn_pre, w_gate, w_up, w_down, norm_ffn_post, p_2, norm_mix_2, w_in_2,
    w_pool_2, pool_scale_2, w_branch_a_2, w_branch_b_2, w_out_2, norm_ffn_2, w_ffn_gate_2,
    w_ffn_up_2, w_ffn_down_2, norm_ple_2, w_ple_gate_2, w_ple_proj_2, norm_final_2,
):
    x = first_block(
        x, norm_mix_pre, w_in, q_norm_a, k_norm_a, sink_b, group_norm_a, group_norm_b, w_out,
        norm_mix_post, norm_ffn_pre, w_gate, w_up, w_down, norm_ffn_post,
    )
    return second_block(
        x, p_2, norm_mix_2, w_in_2, w_pool_2, pool_scale_2, w_branch_a_2, w_branch_b_2, w_out_2,
        norm_ffn_2, w_ffn_gate_2, w_ffn_up_2, w_ffn_down_2, norm_ple_2, w_ple_gate_2,
        w_ple_proj_2, norm_final_2,
    )


_drawn_inputs = setup_inputs


def setup_inputs(seed=0):
    import zlib

    import numpy as np

    out = dict(_drawn_inputs(seed))
    spreads = {}
    factors = {'sink_b': 8.0,
     'norm_mix_2': 7.882,
     'pool_scale_2': 8.0,
     'norm_ffn_2': 19.236,
     'norm_ple_2': 64.0,
     'norm_final_2': 7.431,
     'p_2': 3.765,
     'w_ple_gate_2': 5.641,
     'w_ple_proj_2': 3.772}
    for name, (base, spread) in spreads.items():
        noise = np.random.default_rng([zlib.crc32(name.encode()), seed]).standard_normal(out[name].shape)
        drawn = base * np.exp(spread * noise) if base else spread * noise
        out[name] = __import__('jax').numpy.asarray(drawn.astype(out[name].dtype))
    for name, factor in factors.items():
        out[name] = (out[name] * factor).astype(out[name].dtype)
    return out
```

```python
D = 1024
S = 512
P = 128
KD = D // P
FF = 2816
KF = FF // P
HD = 64
NH = 8
NB = S // P
EPS = 1e-6
SCALE = HD ** -0.5
POOL_WINDOWS = (2, 4, 8, 16)
PADW = 16
RAW = 2048
NEG = -3.0e38

DOWN_TILES = KF // 2
UNITS_IN1, UNITS_OUT1 = 6, 4
UNITS_FF, UNITS_DOWN = 2 * (KF // 2), 2 * KD
UNITS_IN2, UNITS_POOL, UNITS_BRANCH, UNITS_OUT2 = 16, 2, 2, 4
U_IN1 = 0
U_OUT1 = U_IN1 + UNITS_IN1
U_FF1 = U_OUT1 + UNITS_OUT1
U_DOWN1 = U_FF1 + UNITS_FF
U_IN2 = U_DOWN1 + UNITS_DOWN
U_POOL = U_IN2 + UNITS_IN2
U_BRA = U_POOL + UNITS_POOL
U_BRB = U_BRA + UNITS_BRANCH
U_OUT2 = U_BRB + UNITS_BRANCH
U_FF2 = U_OUT2 + UNITS_OUT2
U_DOWN2 = U_FF2 + UNITS_FF
U_PLEP = U_DOWN2 + UNITS_DOWN
U_PLEG = U_PLEP + 1
N_UNITS = U_PLEG + 4

GAINS = ["norm_mix_pre", "norm_mix_post", "norm_ffn_pre", "norm_ffn_post", "norm_mix_2", "norm_ffn_2",
         "norm_ple_2", "norm_final_2", "group_norm_a", "group_norm_b", "pool_scale_2"]
GAIN_W = [KD] * 8 + [4] * 3
GAIN_AT = {n: sum(GAIN_W[:i]) for i, n in enumerate(GAINS)}
G_QN = sum(GAIN_W)
G_KN = G_QN + 1
G_SINK = G_QN + 2
G_COLS = G_SINK + NH

C_ID, C_ONE, C_HONE, C_ROT, C_TRI, C_NEG1, C_SMASK = (P * i for i in range(7))
C_MASK = 7 * P
C_COSA, C_SINA, C_COSB, C_SINB = (10 * P + S * i for i in range(4))
C_INVC = 10 * P + 4 * S
C_COLS = C_INVC + 4 * PADW


ORDER1 = [4, 5, 0, 1, 2, 3, 10, 11, 6, 7, 8, 9]
V1 = [5, 11]
NORMED = [4, 0, 1, 2, 3]
ROPED = [c for c in ORDER1 if c not in V1]
ORDER2 = [*range(8, 12), *range(4, 8), *range(12, 16), *range(0, 4), *range(16, 32)]
STEPS = [(0, h, b, 0, NB) for h in range(NH) for b in range(NB)] + [
    (1, h, b, max(b - 1, 0), min(b + 2, NB)) for h in range(NH) for b in range(NB)]


def build(nc, xT, pT, weights, gains, consts, outT, stop=None):
    import concourse.bass as bass
    from concourse import mybir
    from contextlib import ExitStack

    f32, f32r = mybir.dt.float32, mybir.dt.float32r
    ACT = mybir.ActivationFunctionType
    ALU = mybir.AluOpType
    AX = mybir.AxisListType

    ctx = ExitStack()
    with ctx:
        def sb(name, shape, dt=f32, stack=ctx):
            return stack.enter_context(nc.sbuf_tensor(name, shape, dt))

        def sem(name):
            return ctx.enter_context(nc.semaphore(name))

        X = sb("X", [P, KD, S])
        w_raw = [sb(f"w_raw{i}", [P, RAW]) for i in range(2)]
        w_hi = [sb(f"w_hi{i}", [P, RAW], f32r) for i in range(2)]
        w_lo = [sb(f"w_lo{i}", [P, RAW], f32r) for i in range(2)]
        p_hi = sb("p_hi", [P, 2, S], f32r)
        p_lo = sb("p_lo", [P, 2, S], f32r)
        ident = sb("ident", [P, P])
        ones = sb("ones", [P, P])
        gain = sb("gain", [P, G_COLS])
        sq = sb("sq", [P, 2, S])
        hf = sb("hf", [P, 2, S])
        sqsum = sb("sqsum", [P, S])
        diag = sb("diag", [P, NB, P])
        stat = sb("stat", [P, 5, NB])

        with ExitStack() as lowpart:
            h_lo = sb("h_lo", [P, KD, S], f32r, lowpart)
        F = sb("F", [P, KD, S])
        h_hi = sb("h_hi", [P, KD, S], f32r)

        with ExitStack() as st:
            with ExitStack() as st2:
                F1 = sb("F1", [P, KD, S], stack=st2)
            QA = sb("QA", [P, 4, S], stack=st)
            QB = sb("QB", [P, 4, S], stack=st)
            KDA = sb("KDA", [P, 2, S], stack=st)
            KDB = sb("KDB", [P, 2, S], stack=st)
            VA = sb("VA", [P, NB, P], stack=st)
            VB = sb("VB", [P, NB, P], stack=st)
            c1 = sb("c1", [P, C_COLS], stack=st)
            with ExitStack() as st2:
                OT = sb("OT", [P, 8, S], stack=st2)
            y = sb("y", [P, 2, S], stack=st)
            ysq = sb("ysq", [P, 2, S], stack=st)
            rt = sb("rt", [P, 6, S], stack=st)
            sm = sb("sm", [P, 2, 3 * P], stack=st)
            prob = sb("prob", [P, 2, S], stack=st)
            PT = sb("PT", [P, 2, NB, S], stack=st)
            nmax = sb("nmax", [P, 64], stack=st)
            bmax = sb("bmax", [P, 64], stack=st)
            den = sb("den", [P, 64], stack=st)
            esink = sb("esink", [P, 64], stack=st)
            rden = sb("rden", [P, 64], stack=st)
        with ExitStack() as st:
            mid_hi = sb("mid_hi", [P, KF, S], f32r, st)
            mid_lo = sb("mid_lo", [P, KF, S], f32r, st)
        with ExitStack() as st:
            with ExitStack() as st2:
                Q2 = sb("Q2", [P, 4, S], stack=st2)
                K2 = sb("K2", [P, 4, S], stack=st2)
                V2 = sb("V2", [P, NB, S], stack=st2)
                E2 = sb("E2", [P, 1280], stack=st2)
                A2 = sb("A2", [P, 2, 1280], stack=st2)
            with ExitStack() as st2:
                pl_hi = sb("pl_hi", [P, 4, S], f32r, st2)
                pl_lo = sb("pl_lo", [P, 4, S], f32r, st2)
            with ExitStack() as st2:
                m_hi = sb("m_hi", [P, KD, S], f32r, st2)
                m_lo = sb("m_lo", [P, KD, S], f32r, st2)
            sb("behind", [P, 9984], stack=st)
            GA = sb("GA", [P, KD, S], stack=st)
            GB = sb("GB", [P, KD, S], stack=st)
            UP = sb("UP", [P, 4, S], stack=st)
            OB = sb("OB", [P, 4, S], stack=st)
            c2 = sb("c2", [P, 3 * P + 4 * PADW], stack=st)
        with ExitStack() as st:
            PP = sb("PP", [P, KD, S], stack=st)
            OUT = sb("OUT", [P, KD, S], stack=st)

        ps = ctx.enter_context(nc.psum_tensor("ps", [P, 8, S], f32))
        R_BANK, SS_BANK = 4, 5

        raw_landed = [sem(f"raw_landed{i}") for i in range(2)]
        hi_ready, lo_ready = sem("hi_ready"), sem("lo_ready")
        group_done = sem("group_done")
        evac_act, evac_dve = sem("evac_act"), sem("evac_dve")
        x_landed = [sem(f"x_landed{i}") for i in range(4)]
        gain_landed, c0_landed, c1_landed, c2_landed, p_landed = (
            sem(n) for n in ("gain_landed", "c0_landed", "c1_landed", "c2_landed", "p_landed"))
        p_hi_ready, p_lo_ready = sem("p_hi_ready"), sem("p_lo_ready")
        dve_self, act_self, pool_self = sem("dve_self"), sem("act_self"), sem("pool_self")
        ysq_ready, rot_done, hsum_done, hvar_ready, hguess_ready, rope_done, v_ready = (
            sem(n) for n in ("ysq_ready", "rot_done", "hsum_done", "hvar_ready", "hguess_ready", "rope_done",
                             "v_ready"))
        vtr_done = sem("vtr_done")
        s_done, nmax_ready, masked, exp_done, es_done, pn_ready, tr_done, pt_ready, av_done, ot_ready = (
            sem(n) for n in ("scores_done", "negmax_ready", "scores_masked", "exp_done", "sink_exp_done",
                             "prob_normed", "transposed", "pt_ready", "av_done", "ot_ready"))
        z_done, ln_done, sp_ready, sp_masked, cum_done, a_done, av2_done, ob_ready = (
            sem(n) for n in ("z_done", "ln_done", "sp_ready", "sp_masked", "cum_done", "a_done", "av2_done", "ob_ready"))
        v2tr_done, v2_ready = sem("v2tr_done"), sem("v2_ready")
        pooled, pl_hi_ready, pl_lo_ready = sem("pooled"), sem("pl_hi_ready"), sem("pl_lo_ready")
        ya_ready, ya_hi, ya_lo, yb_hi, yb_lo = (sem(n) for n in ("ya_ready", "ya_hi", "ya_lo", "yb_hi", "yb_lo"))
        sig_ready, merged, m_hi_ready, m_lo_ready = (sem(n) for n in ("sig_ready", "merged", "m_hi_ready", "m_lo_ready"))
        x_new = [sem(f"x_new{i}") for i in range(3)]
        prod_hi, prod_lo = sem("mid_hi_ready"), sem("mid_lo_ready")
        out_ready, out_stored = sem("out_ready"), sem("out_stored")

        class Count:

            def __init__(self, sem, base=0):
                self.sem, self.base = sem, base

            def __call__(self, n):
                return self.sem, self.base + n

        NORM_EVENTS = ("squares",
                       "summed",
                       "total",
                       "var",
                       "guess",
                       "diag",
                       "factor",
                       "f32",
                       "hi",
                       "lo")
        norm_sems = {e: sem("norm_" + e) for e in NORM_EVENTS}
        norm_counts = dict.fromkeys(NORM_EVENTS, 0)

        class Norm:

            def __init__(self, n, kind, before):
                self.n, self.before = n, before
                (self.squares, self.summed, self.total, self.var, self.guess, self.diag, self.factor, self.f32,
                 self.hi, self.lo) = (Count(norm_sems[e], norm_counts[e]) for e in NORM_EVENTS)
                for e in NORM_EVENTS:
                    norm_counts[e] += (n if e in ("squares", "summed") or e == "f32" and kind != "final"
                                       or e in ("hi", "lo") and kind == "split" else
                                       0 if e in ("f32", "hi", "lo") else 1)

        norms = []
        for n, kind in ((KD, "split"), (4, "split"), (4, "split"), (KD, "added"), (KD, "split"), (KD, "added"),
                        (KD, "split"), (KD, "split"), (KD, "split"), (KD, "final")):
            norms.append(Norm(n, kind, norms[-1] if norms else None))
        (n_mix_pre, n_group_a, n_group_b, n_mix_post, n_ffn_pre, n_ffn_post, n_mix2, n_ffn2, n_ple,
         n_final) = norms

        PHASES = [("in1", 12, "A", 4, 1), ("out1", KD, "A", 4, 1), ("ff1", 2 * KF, "AADD", 4, 1),
                  ("down1", KD, "A", 2, 2), ("in2", 32, "A", 4, 1), ("pool", 4, "A", 4, 1),
                  ("bra", KD, "D", 4, 1), ("brb", KD, "D", 4, 1), ("out2", KD, "D", 4, 1),
                  ("ff2", 2 * KF, "AADD", 4, 1), ("down2", KD, "D", 2, 2), ("plep", KD, "A", 4, 1),
                  ("pleg", KD, "A", 4, 1)]
        GROUP, EVAC, BEFORE, BASE = {}, {}, {}, {}
        counts, groups, users = {"A": 0, "D": 0}, 0, {}
        for phase, n, engines, banks, parts in PHASES:
            BASE[phase] = (groups, counts["A"], counts["D"])
            for j in range(n):
                e = engines[j % len(engines)]
                groups += parts
                counts[e] += 1
                GROUP[phase, j] = groups
                EVAC[phase, j] = (e, counts[e])
                BEFORE[phase, j] = users.get(j % banks)
                users[j % banks] = (e, counts[e])

        USED = []
        for phase, n, engines, banks, parts in PHASES:
            per = {"pool": 2, "bra": 4, "brb": 4, "plep": 8}.get(phase, 2)
            if parts == 2:
                USED += [g for j in range(n) for g in (GROUP[phase, j] - 1, GROUP[phase, j])]
            else:
                USED += [GROUP[phase, j + per - 1] for j in range(0, n, per)]
        assert len(USED) == N_UNITS

        block = ctx.enter_context(nc.Block())

        def gcol(name, k):
            c = GAIN_AT[name] + k
            return gain[:, c:c + 1]

        def tiles_of(u):
            if U_DOWN1 <= u < U_IN2 or U_DOWN2 <= u < U_PLEP:
                return DOWN_TILES
            return 2 if U_POOL <= u < U_BRA else 16

        @block.sync
        def _(sp):
            def load(u, slot, width, first=False):
                if not first:
                    sp.wait_ge(lo_ready, u - 1)
                sp.dma_start(w_raw[slot][:, 0:width * P], weights[bass.ds(u, 1), :, 0:width * P]
                             if not isinstance(u, int) else weights[u, :, 0:width * P]
                             ).then_inc(raw_landed[slot], 16)

            for i in range(4):
                sp.dma_start(X[:, 2 * i:2 * i + 2, :],
                             xT[i * 2 * P:(i + 1) * 2 * P, :].rearrange("(k p) s -> p k s", p=P)
                             ).then_inc(x_landed[i], 16)
            load(0, 0, 16, True)
            load(1, 1, 16, True)

            def run(start, n):
                with sp.Fori(0, n // 2) as i:
                    for slot in range(2):
                        u = i * 2 + (start + slot)
                        sp.wait_ge(lo_ready, u - 1)
                        sp.dma_start(w_raw[slot][:, 0:tiles_of(start) * P],
                                     weights[bass.ds(u, 1), :, 0:tiles_of(start) * P]
                                     ).then_inc(raw_landed[slot], 16)

            run(2, U_DOWN1 - 2)
            run(U_DOWN1, UNITS_DOWN)
            run(U_IN2, UNITS_IN2)
            run(U_POOL, UNITS_POOL)
            run(U_BRA, U_DOWN2 - U_BRA)
            run(U_DOWN2, UNITS_DOWN)
            for u in range(U_PLEP, N_UNITS):
                load(u, u % 2, 16)
            for k in range(KD):
                sp.wait_ge(out_ready, k + 1)
                sp.dma_start(outT[k * P:(k + 1) * P, :], OUT[:, k, :]).then_inc(out_stored, 16)
            sp.wait_ge(out_stored, 16 * KD)

        @block.gpsimd
        def _(pool):
            def sum_squares(nm):
                if nm.before is not None:
                    pool.wait_ge(*nm.before.total(1))
                nc.gpsimd.memset(sqsum[:, :], 0.0).then_inc(nm.summed.sem, 1)
                for j in range(nm.n - 1):
                    pool.wait_ge(*nm.squares(j + 1))
                    pool.wait_ge(*nm.summed(j + 1))
                    nc.gpsimd.tensor_tensor(sqsum[:, :], sqsum[:, :], sq[:, j % 2, :], ALU.add
                                            ).then_inc(nm.summed.sem, 1)

            def zero_masked(t):
                for at in (0, 512, 896, 1024):
                    v = t[:, at:at + P]
                    last = nc.gpsimd.affine_select(out=v, in_=v, compare_op=ALU.is_gt, fill=0.0, base=0,
                                                   pattern=[[1, P]], channel_multiplier=-1)
                return last

            for nm in norms[:7]:
                sum_squares(nm)
            for h in range(NH):
                pool.wait_ge(sp_ready, h + 1)
                zero_masked(E2[:, :]).then_inc(sp_masked, 1)
            for nm in norms[7:]:
                sum_squares(nm)

        @block.tensor
        def _(pe):
            def mm(out, lhsT, rhs, start=True, stop=True, loose=False):
                return nc.tensor.matmul(out, lhsT, rhs, start=start, stop=stop, skip_group_check=loose)

            def three(bank, slot, t, hi, lo, start, stop):
                whi, wlo = w_hi[slot][:, t * P:(t + 1) * P], w_lo[slot][:, t * P:(t + 1) * P]
                mm(ps[:, bank, :], whi, hi, start, False)
                mm(ps[:, bank, :], whi, lo, False, False)
                return mm(ps[:, bank, :], wlo, hi, False, stop)

            def wait_bank(phase, j):
                if BEFORE[phase, j]:
                    e, n = BEFORE[phase, j]
                    pe.wait_ge(evac_act if e == "A" else evac_dve, n)

            def group(slot, t0, ks, bank, hi, lo, start=True, stop=True, ready=None):
                for n, k in enumerate(ks):
                    if ready is not None:
                        pe.wait_ge(ready[0], ready[1] + k + 1)
                    last = three(bank, slot, t0 + n, hi[:, k, :], lo[:, k, :], start and n == 0,
                                 stop and n == len(ks) - 1)
                last.then_inc(group_done, 1)

            def first_units(phase, u, nchunks, ks, hi, lo, ready, per=2):
                for j in range(nchunks):
                    wait_bank(phase, j)
                for n in range(nchunks // per):
                    pe.wait_ge(lo_ready, u + n + 1)
                for n, k in enumerate(ks):
                    pe.wait_ge(*ready(k + 1))
                    for j in range(nchunks):
                        last = three(j % 4, (u + j // per) % 2, (j % per) * len(ks) + n, hi[:, k, :], lo[:, k, :],
                                     n == 0, n == len(ks) - 1)
                        if n == len(ks) - 1:
                            last.then_inc(group_done, 1)

            def unit(phase, u, j0, nchunks, ks, hi, lo, after=None):
                pe.wait_ge(lo_ready, u + 1)
                for c in range(nchunks):
                    wait_bank(phase, j0 + c)
                    group(u % 2, c * len(ks), ks, (j0 + c) % 4, hi, lo)
                    if after:
                        after(j0 + c)

            def total(nm):
                for src, ready, n in ((sqsum[:, :], nm.summed, nm.n), (sq[:, (nm.n - 1) % 2, :], nm.squares, nm.n)):
                    pe.wait_ge(*ready(n))
                    for b in range(NB):
                        last = mm(ps[:, SS_BANK, b:b + 1], src[:, b * P:(b + 1) * P], ones[:, 0:1],
                                  ready is nm.summed and b == 0, True, loose=True)
                last.then_inc(nm.total.sem, 1)

            def factor(nm):
                pe.wait_ge(*nm.diag(1))
                if nm.before is not None:
                    pe.wait_ge(*nm.before.f32(nm.before.n))
                mm(ps[:, R_BANK, :], ones[:, :], diag[:, :, :]).then_inc(nm.factor.sem, 1)

            KS = range(KD)
            pe.wait_ge(c0_landed, 32)
            total(n_mix_pre)
            factor(n_mix_pre)

            def free_item(j):
                if j >= 0:
                    if ORDER1[j] in V1:
                        pe.wait_ge(v_ready, V1.index(ORDER1[j]) + 1)
                    else:
                        pe.wait_ge(rope_done, ROPED.index(ORDER1[j]) + 1)

            def item(j):
                if j < 0:
                    return
                c = ORDER1[j]
                free_item(j - 2)
                if j == 0:
                    pe.wait_ge(*n_mix_pre.lo(KD))
                    pe.wait_ge(c1_landed, 16)
                pe.wait_ge(evac_act, EVAC["in1", j][1])
                if c in V1:
                    for b in range(NB):
                        last = nc.tensor.transpose(ps[:, 4 + j % 2, b * P:(b + 1) * P],
                                                   y[:, j % 2, b * P:(b + 1) * P], ident[:, :])
                    last.then_inc(vtr_done, 1)
                    return
                mm(ps[:, 4 + j % 2, :], c1[:, C_ROT:C_ROT + P], y[:, j % 2, :]).then_inc(rot_done, 1)
                if c in NORMED:
                    pe.wait_ge(ysq_ready, NORMED.index(c) + 1)
                    mm(ps[:, 6 + j % 2, :], c1[:, C_HONE:C_HONE + P], ysq[:, j % 2, :]).then_inc(hsum_done, 1)

            first_units("in1", 0, 4, KS, h_hi, h_lo, n_mix_pre.lo)
            for j in range(3):
                item(j)
            for u in range(2, UNITS_IN1):
                unit("in1", u, 2 * u, 2, KS, h_hi, h_lo, after=lambda j: item(j - 1))
            item(11)

            pe.wait_ge(rope_done, len(ROPED))
            pe.wait_ge(v_ready, 2)
            pe.wait_ge(evac_act, EVAC["in1", 11][1])

            def scores(s):
                if s >= 64:
                    return
                kind, h, b, k0, k1 = STEPS[s]
                if s >= 3:
                    pe.wait_ge(exp_done if s - 3 < 32 else masked, s - 2 if s - 3 < 32 else s - 3 - 32 + 1)
                q, kd = (QA, KDA) if kind == 0 else (QB, KDB)
                r = HD * (h % 2)
                mm(ps[:, s % 3, 0:(k1 - k0) * P], q[r:r + HD, h // 2, b * P:(b + 1) * P],
                   kd[r:r + HD, h // 4, k0 * P:k1 * P]).then_inc(s_done, 1)

            def weighted(g):
                c = g // 2
                if c >= 2 and g % 2 == 0:
                    pe.wait_ge(ot_ready, c - 1)
                r, v = HD * (g % 2), (VA if g < NH else VB)
                kv = (g % NH) // 4
                pe.wait_ge(pt_ready, 4 * (g + 1))
                order = ([(kb, 0, NB) for kb in range(NB)] if g < NH else
                         [(1, 0, 3), (0, 0, 2), (2, 1, 4), (3, 2, 4)])
                for n, (kb, q0, q1) in enumerate(order):
                    last = mm(ps[r:r + HD, 5 + c % 2, q0 * P:q1 * P], v[:, kb, kv * HD:(kv + 1) * HD],
                              PT[:, g % 2, kb, q0 * P:q1 * P], n == 0, n == len(order) - 1, loose=True)
                last.then_inc(av_done, 1)

            scores(0)
            scores(1)
            for s, (kind, h, b, k0, k1) in enumerate(STEPS):
                scores(s + 2)
                pe.wait_ge(pn_ready, s + 1)
                if s >= 2:
                    pe.wait_ge(pt_ready, s - 1)
                for kb in range(k0, k1):
                    last = nc.tensor.transpose(ps[:, 3 + s % 2, (kb - k0) * P:(kb - k0 + 1) * P],
                                               prob[:, s % 2, (kb - k0) * P:(kb - k0 + 1) * P], ident[:, :])
                last.then_inc(tr_done, 1)
                if s and s % 4 == 0:
                    weighted(s // 4 - 1)
            weighted(15)
            pe.wait_ge(ot_ready, 8)
            pe.wait_ge(pt_ready, 64)
            for nm in (n_group_a, n_group_b):
                total(nm)
                factor(nm)

            for j in range(4):
                wait_bank("out1", j)
            pe.wait_ge(lo_ready, U_OUT1 + 2)
            for k in KS:
                pe.wait_ge(*(n_group_a.lo if k < 4 else n_group_b.lo)(k % 4 + 1))
                for j in range(4):
                    last = three(j, j // 2, (j % 2) * KD + k, h_hi[:, k, :], h_lo[:, k, :], k == 0, k == KD - 1)
                    if k == KD - 1:
                        last.then_inc(group_done, 1)
            for u in range(2, UNITS_OUT1):
                unit("out1", U_OUT1 + u, 2 * u, 2, KS, h_hi, h_lo)

            def ffn(phase, down, u_ff, u_down, nm, mids0):
                g0, a0, d0 = BASE[phase]
                first_units(phase, u_ff, 4, KS, h_hi, h_lo, nm.lo)
                with pe.Fori(1, KF // 2) as i:
                    for c in range(2):
                        pe.wait_ge(lo_ready, i * 2 + (u_ff + 1))
                        pe.wait_ge(evac_act, i * 2 + (a0 - 1 + c))
                        group(0, c * KD, KS, c, h_hi, h_lo)
                    for c in range(2):
                        pe.wait_ge(lo_ready, i * 2 + (u_ff + 2))
                        pe.wait_ge(evac_dve, i * 2 + (d0 - 1 + c))
                        group(1, c * KD, KS, 2 + c, h_hi, h_lo)
                g0, a0, d0 = BASE[down]
                pe.wait_ge(evac_act, a0)

                def chunk(j, c, ready=None):
                    for part in range(2):
                        pe.wait_ge(lo_ready, j * 2 + (u_down + part + 1))
                        group(part, 0, range(part * DOWN_TILES, (part + 1) * DOWN_TILES), c, mid_hi, mid_lo,
                              part == 0, part == 1, ready)

                chunk(0, 0, (prod_lo, mids0))
                chunk(1, 1)
                evac, e0 = (evac_act, a0) if down == "down1" else (evac_dve, d0)
                with pe.Fori(1, KD // 2) as i:
                    for c in range(2):
                        pe.wait_ge(evac, i * 2 + (e0 - 1 + c))
                        chunk(i * 2 + c, c)

            total(n_mix_post)
            factor(n_mix_post)
            total(n_ffn_pre)
            factor(n_ffn_pre)
            ffn("ff1", "down1", U_FF1, U_DOWN1, n_ffn_pre, 0)
            total(n_ffn_post)
            factor(n_ffn_post)
            total(n_mix2)
            factor(n_mix2)

            def vee(i):
                pe.wait_ge(evac_act, EVAC["in2", 8 + i][1])
                if i >= 2:
                    pe.wait_ge(v2_ready, i - 1)
                for b in range(NB):
                    last = nc.tensor.transpose(ps[:, 4 + i % 2, b * P:(b + 1) * P],
                                               hf[:, i % 2, b * P:(b + 1) * P], ident[:, :])
                last.then_inc(v2tr_done, 1)

            first_units("in2", U_IN2, 4, KS, h_hi, h_lo, n_mix2.lo)
            for u in range(2, 8):
                unit("in2", U_IN2 + u, 2 * u, 2, KS, h_hi, h_lo,
                     after=lambda j: vee(j - 9) if 9 <= j < 13 else None)
            Z = ps[:, 4:7, :].rearrange("p b s -> p (b s)")
            ZAT = [0, 512, 1024, 896]
            pe.wait_ge(v2_ready, 4)
            pe.wait_ge(c2_landed, 32)
            for h in range(NH):
                r = HD * (h % 2)
                if h:
                    pe.wait_ge(a_done, h)
                for kb in range(NB):
                    w = S - kb * P
                    last = mm(Z[:, ZAT[kb]:ZAT[kb] + w], K2[r:r + HD, h // 2, kb * P:(kb + 1) * P],
                              Q2[r:r + HD, h // 2, kb * P:S], kb < 3, True, loose=True)
                last.then_inc(z_done, 1)
                u = 8 + h
                pe.wait_ge(lo_ready, U_IN2 + u + 1)
                wait_bank("in2", 2 * u)
                group(u % 2, 0, KS, (2 * u) % 4, h_hi, h_lo)
                pe.wait_ge(sp_masked, h + 1)
                for kb in range(NB):
                    for later in range(kb, NB):
                        w = S - later * P
                        o = ZAT[kb] + (later - kb) * P
                        last = mm(Z[:, o:o + w], c2[:, 0:P] if later == kb else c2[:, P:2 * P],
                                  E2[:, ZAT[later]:ZAT[later] + w], False, True, loose=True)
                    last = mm(Z[:, ZAT[kb]:ZAT[kb] + P], ident[:, :], c2[:, 2 * P:3 * P], False, True, loose=True)
                last.then_inc(cum_done, 1)
                wait_bank("in2", 2 * u + 1)
                group(u % 2, KD, KS, (2 * u + 1) % 4, h_hi, h_lo)
                pe.wait_ge(a_done, h + 1)
                if h % 2 == 0 and h:
                    pe.wait_ge(ob_ready, h // 2)
                for kb in range(NB):
                    w = S - kb * P
                    last = mm(ps[r:r + HD, 7, kb * P:S], V2[:, kb, h * HD:(h + 1) * HD],
                              A2[:, h % 2, ZAT[kb]:ZAT[kb] + w], kb == 0, kb == 3, loose=True)
                last.then_inc(av2_done, 1)

            for u in range(UNITS_POOL):
                pe.wait_ge(lo_ready, U_POOL + u + 1)
                for c in range(2):
                    j = 2 * u + c
                    wait_bank("pool", j)
                    pe.wait_ge(pl_lo_ready, j + 1)
                    group(u % 2, c, range(j, j + 1), j % 4, pl_hi, pl_lo)
            pe.wait_ge(ya_lo, 4)
            for u in range(UNITS_BRANCH):
                unit("bra", U_BRA + u, 4 * u, 4, range(4), h_hi, h_lo)
            pe.wait_ge(yb_lo, 4)
            for u in range(UNITS_BRANCH):
                unit("brb", U_BRB + u, 4 * u, 4, range(4, 8), h_hi, h_lo)
            first_units("out2", U_OUT2, 4, KS, m_hi, m_lo, Count(m_lo_ready))
            for u in range(2, UNITS_OUT2):
                unit("out2", U_OUT2 + u, 2 * u, 2, KS, m_hi, m_lo)
            total(n_ffn2)
            factor(n_ffn2)
            ffn("ff2", "down2", U_FF2, U_DOWN2, n_ffn2, KF)

            total(n_ple)
            pe.wait_ge(p_lo_ready, 1)
            unit("plep", U_PLEP, 0, KD, range(2), p_hi, p_lo)
            factor(n_ple)
            first_units("pleg", U_PLEG, 4, KS, h_hi, h_lo, n_ple.lo)
            for u in range(2, 4):
                unit("pleg", U_PLEG + u, 2 * u, 2, KS, h_hi, h_lo)
            total(n_final)
            factor(n_final)

        @block.scalar
        def _(act):
            n_self = [0]

            def link(ins):
                n_self[0] += 1
                ins.then_inc(act_self, 1)
                act.wait_ge(act_self, n_self[0])

            def af(out, in_, func, **kw):
                return nc.scalar.activation(out, in_, func, **kw)

            def split(u, slot=None, width=None):
                slot = u % 2 if slot is None else slot
                width = tiles_of(u) if width is None else width
                half = u // 2 if isinstance(u, int) else None
                act.wait_ge(raw_landed[slot], 16 * (half + 1))
                if u >= 2:
                    act.wait_ge(group_done, USED[u - 2])
                af(w_hi[slot][:, 0:width * P], w_raw[slot][:, 0:width * P], ACT.Copy).then_inc(hi_ready, 1)

            def square(nm, j, src):
                if j >= 2:
                    act.wait_ge(*nm.summed(j))
                af(sq[:, j % 2, :], src, ACT.Square).then_inc(nm.squares.sem, 1)

            def guess(nm):
                act.wait_ge(*nm.var(1))
                link(af(stat[:, 1, :], stat[:, 0, :], ACT.Ln))
                af(stat[:, 2, :], stat[:, 1, :], ACT.Exp, scale=-0.5).then_inc(nm.guess.sem, 1)

            def high(nm, dst, n0=0):
                for k in range(nm.n):
                    act.wait_ge(*nm.f32(k + 1))
                    af(dst[:, n0 + k, :], hf[:, k % 2, :], ACT.Copy).then_inc(nm.hi.sem, 1)

            act.dma_start(gain[:, :], gains[:, :]).then_inc(gain_landed, 16)
            act.dma_start(ident[:, :], consts[:, C_ID:C_ID + P]).then_inc(c0_landed, 16)
            act.dma_start(ones[:, :], consts[:, C_ONE:C_ONE + P]).then_inc(c0_landed, 16)
            act.dma_start(hf[:, :, :], pT.rearrange("(k p) s -> p k s", p=P)).then_inc(p_landed, 16)
            act.dma_start(c1[:, :], consts[:, :]).then_inc(c1_landed, 16)
            act.wait_ge(gain_landed, 16)
            for k in range(KD):
                act.wait_ge(x_landed[k // 2], 16)
                square(n_mix_pre, k, X[:, k, :])
            act.wait_ge(p_landed, 16)
            af(p_hi[:, :, :], hf[:, :, :], ACT.Copy).then_inc(p_hi_ready, 1)
            guess(n_mix_pre)
            split(0)
            split(1)
            high(n_mix_pre, h_hi)

            def free_item(j):
                if j >= 0:
                    if ORDER1[j] in V1:
                        act.wait_ge(v_ready, V1.index(ORDER1[j]) + 1)
                    else:
                        act.wait_ge(rope_done, ROPED.index(ORDER1[j]) + 1)

            def finish(j):
                c = ORDER1[j]
                if c in V1:
                    act.wait_ge(vtr_done, V1.index(c) + 1)
                    af((VA if c == 5 else VB)[:, :, :], ps[:, 4 + j % 2, :].rearrange("p (b c) -> p b c", b=NB),
                       ACT.Copy).then_inc(v_ready, 1)
                elif c in NORMED:
                    act.wait_ge(hvar_ready, NORMED.index(c) + 1)
                    link(af(rt[:, 4, :], rt[:, 3, :], ACT.Ln))
                    af(rt[:, 4, :], rt[:, 4, :], ACT.Exp, scale=-0.5).then_inc(hguess_ready, 1)

            for j in range(12):
                c = ORDER1[j]
                act.wait_ge(group_done, GROUP["in1", j])
                free_item(j - 2)
                if c in NORMED:
                    af(ysq[:, j % 2, :], ps[:, j % 4, :], ACT.Square).then_inc(ysq_ready, 1)
                    g = gain[:, G_KN:G_KN + 1] if c == 4 else gain[:, G_QN:G_QN + 1]
                    af(y[:, j % 2, :], ps[:, j % 4, :], ACT.Copy, scale=g).then_inc(evac_act, 1)
                else:
                    af(y[:, j % 2, :], ps[:, j % 4, :], ACT.Copy).then_inc(evac_act, 1)
                if j % 2:
                    split(j // 2 + 2)
                if j:
                    finish(j - 1)
            finish(11)

            def copy_pt(s):
                kind, h, b, k0, k1 = STEPS[s]
                g = s // 4
                act.wait_ge(tr_done, s + 1)
                if g >= 2 and s % 4 == 0:
                    act.wait_ge(av_done, g - 1)
                n = k1 - k0
                af(PT[:, g % 2, k0:k1, b * P:(b + 1) * P],
                   ps[:, 3 + s % 2, 0:n * P].rearrange("p (b c) -> p b c", b=n), ACT.Copy).then_inc(pt_ready, 1)

            def copy_out(c):
                act.wait_ge(av_done, 2 * c + 2)
                af(OT[:, c, :], ps[:, 5 + c % 2, :], ACT.Copy).then_inc(ot_ready, 1)

            for s, (kind, h, b, k0, k1) in enumerate(STEPS):
                w = (k1 - k0) * P
                act.wait_ge(nmax_ready, s + 1)
                if s >= 2:
                    act.wait_ge(tr_done, s - 1)
                src = ps[:, s % 3, 0:w] if kind == 0 else sm[:, s % 2, 0:w]
                af(prob[:, s % 2, 0:w], src, ACT.Exp, bias=nmax[:, s:s + 1],
                   accum_out=den[:, s:s + 1]).then_inc(exp_done, 1)
                if kind:
                    af(esink[:, s:s + 1], gain[:, G_SINK + h:G_SINK + h + 1], ACT.Exp,
                       bias=nmax[:, s:s + 1]).then_inc(es_done, 1)
                if s:
                    copy_pt(s - 1)
                if s % 8 == 2 and s > 8:
                    copy_out(s // 8 - 1)
            copy_pt(63)
            copy_out(7)
            for nm, c0 in ((n_group_a, 0), (n_group_b, 4)):
                for j in range(4):
                    act.wait_ge(ot_ready, c0 + j + 1)
                    square(nm, j, OT[:, c0 + j, :])
                guess(nm)
                high(nm, h_hi, c0)

            for j in range(KD):
                act.wait_ge(group_done, GROUP["out1", j])
                square(n_mix_post, j, ps[:, j % 4, :])
                af(F1[:, j, :], ps[:, j % 4, :], ACT.Copy).then_inc(evac_act, 1)
                if j % 2:
                    split(U_OUT1 + j // 2 + 2)
            guess(n_mix_post)
            for k in range(KD):
                act.wait_ge(x_new[0], k + 1)
                square(n_ffn_pre, k, X[:, k, :])
            guess(n_ffn_pre)
            high(n_ffn_pre, h_hi)

            def ffn(phase, u_ff, mids0):
                g0, a0, d0 = BASE[phase]

                def turn(i, last=False):
                    for c in range(2):
                        act.wait_ge(group_done, i * 4 + (g0 + 1 + c))
                        if mids0 or not isinstance(i, int) or i:
                            act.wait_ge(evac_dve, i * 2 + (d0 - 1 + c))
                        af(sq[:, c, :], ps[:, c, :], ACT.Silu).then_inc(evac_act, 1)
                    for half in range(2):
                        u = i * 2 + (u_ff + 2 + half)
                        if half:
                            for c in range(2):
                                act.wait_ge(evac_dve, i * 2 + (d0 + 1 + c))
                                af(mid_hi[:, bass.ds(i * 2 + c, 1), :] if not isinstance(i, int)
                                   else mid_hi[:, 2 * i + c, :], hf[:, c, :], ACT.Copy).then_inc(prod_hi, 1)
                        if last:
                            split(u_ff + 2 * i + 2 + half)
                        else:
                            act.wait_ge(raw_landed[half], i * 16 + 16 * (u_ff // 2 + 2))
                            act.wait_ge(group_done, i * 4 + (g0 + 2 + 2 * half))
                            af(w_hi[half][:, :], w_raw[half][:, :], ACT.Copy).then_inc(hi_ready, 1)

                turn(0)
                with act.Fori(1, KF // 2 - 1) as i:
                    turn(i)
                turn(KF // 2 - 1, True)

            ffn("ff1", U_FF1, 0)

            def down_chunk(phase, u0, j, epilogue):
                act.wait_ge(group_done, GROUP[phase, j] - 1)
                split(u0 + 2 * j + 2)
                act.wait_ge(group_done, GROUP[phase, j])
                epilogue(j)
                split(u0 + 2 * j + 3)

            def down1(j):
                square(n_ffn_post, j, ps[:, j % 2, :])
                af(F[:, j, :], ps[:, j % 2, :], ACT.Copy).then_inc(evac_act, 1)

            for j in range(KD):
                down_chunk("down1", U_DOWN1, j, down1)
            act.dma_start(c2[:, 0:3 * P], consts[:, C_TRI:C_TRI + 3 * P]).then_inc(c2_landed, 16)
            act.dma_start(c2[:, 3 * P:], consts[:, C_INVC:C_INVC + 4 * PADW]).then_inc(c2_landed, 16)
            guess(n_ffn_post)
            for k in range(KD):
                act.wait_ge(x_new[0], KD + k + 1)
                square(n_mix2, k, X[:, k, :])
            guess(n_mix2)
            high(n_mix2, h_hi)

            def finish_vee(i):
                act.wait_ge(v2tr_done, i + 1)
                af(V2[:, :, i * P:(i + 1) * P], ps[:, 4 + i % 2, :].rearrange("p (b c) -> p b c", b=NB),
                   ACT.Copy).then_inc(v2_ready, 1)

            def chunk2(j):
                act.wait_ge(group_done, GROUP["in2", j])
                bank = ps[:, j % 4, :]
                if j < 4:
                    af(K2[:, j, :], bank, ACT.Copy).then_inc(evac_act, 1)
                elif j < 8:
                    af(Q2[:, j - 4, :], bank, ACT.Copy, scale=SCALE).then_inc(evac_act, 1)
                elif j < 12:
                    if j >= 10:
                        act.wait_ge(v2_ready, j - 9)
                    af(hf[:, j % 2, :], bank, ACT.Copy).then_inc(evac_act, 1)
                elif j < 16:
                    af(UP[:, j - 12, :], bank, ACT.Copy).then_inc(evac_act, 1)
                else:
                    dst = GA if j < 24 else GB
                    af(dst[:, j % 8, :], bank, ACT.Copy).then_inc(evac_act, 1)

            for j in range(16):
                chunk2(j)
                if j % 2:
                    split(U_IN2 + j // 2 + 2)
                if 9 <= j < 13:
                    finish_vee(j - 9)

            Z = ps[:, 4:7, :].rearrange("p b s -> p (b s)")[:, 0:1280]

            def copy_ob(c):
                act.wait_ge(av2_done, 2 * c + 2)
                af(OB[:, c, :], ps[:, 7, :], ACT.Copy).then_inc(ob_ready, 1)

            for h in range(NH):
                act.wait_ge(z_done, h + 1)
                if h:
                    act.wait_ge(cum_done, h)
                link(af(E2[:, :], Z, ACT.Abs))
                link(af(E2[:, :], E2[:, :], ACT.Exp, scale=-1.0))
                af(E2[:, :], E2[:, :], ACT.Ln, bias=1.0).then_inc(ln_done, 1)
                if h % 2 == 0 and h:
                    copy_ob(h // 2 - 1)
                chunk2(16 + 2 * h)
                act.wait_ge(cum_done, h + 1)
                if h >= 2:
                    act.wait_ge(av2_done, h - 1)
                af(A2[:, h % 2, :], Z, ACT.Exp).then_inc(a_done, 1)
                chunk2(17 + 2 * h)
                split(U_IN2 + 8 + h + 2)
            copy_ob(3)

            act.wait_ge(pooled, 4)
            act.wait_ge(av2_done, NH)
            for i in range(4):
                af(pl_hi[:, i, :], UP[:, i, :], ACT.Copy).then_inc(pl_hi_ready, 1)
            for i in range(4):
                act.wait_ge(ob_ready, i + 1)
                af(h_hi[:, 4 + i, :], OB[:, i, :], ACT.Copy).then_inc(yb_hi, 1)
            for j in range(4):
                act.wait_ge(group_done, GROUP["pool", j])
                if j >= 2:
                    act.wait_ge(ya_lo, j - 1)
                af(hf[:, j % 2, :], ps[:, j % 4, :], ACT.Copy, scale=gcol("pool_scale_2", j)
                   ).then_inc(evac_act, 1)
                act.wait_ge(evac_act, EVAC["pool", j][1])
                af(h_hi[:, j, :], hf[:, j % 2, :], ACT.Copy).then_inc(ya_hi, 1)
                if j % 2:
                    split(U_POOL + j // 2 + 2)
            for j in range(0, KD, 2):
                af(GA[:, j:j + 2, :], GA[:, j:j + 2, :], ACT.Sigmoid).then_inc(sig_ready, 1)
            for j in range(0, KD, 2):
                af(GB[:, j:j + 2, :], GB[:, j:j + 2, :], ACT.Sigmoid).then_inc(sig_ready, 1)
            split(U_BRA + 2)
            split(U_BRA + 3)
            for j in range(KD):
                act.wait_ge(merged, j + 1)
                af(m_hi[:, j, :], GB[:, j, :], ACT.Copy).then_inc(m_hi_ready, 1)
                if j % 4 == 3:
                    split(U_BRB + j // 4 + 2)
            for j in range(KD):
                act.wait_ge(evac_dve, EVAC["out2", j][1])
                square(n_ffn2, j, X[:, j, :])
                if j % 2:
                    split(U_OUT2 + j // 2 + 2)
            guess(n_ffn2)
            high(n_ffn2, h_hi)
            ffn("ff2", U_FF2, KF)

            def down2(j):
                act.wait_ge(evac_dve, EVAC["down2", j][1])
                square(n_ple, j, X[:, j, :])

            for j in range(KD):
                down_chunk("down2", U_DOWN2, j, down2)
            guess(n_ple)
            for j in range(KD):
                act.wait_ge(group_done, GROUP["plep", j])
                af(PP[:, j, :], ps[:, j % 4, :], ACT.Copy).then_inc(evac_act, 1)
            high(n_ple, h_hi)
            split(U_PLEP + 2)
            for j in range(KD):
                act.wait_ge(group_done, GROUP["pleg", j])
                if j >= 2:
                    act.wait_ge(x_new[1], j - 1)
                af(hf[:, j % 2, :], ps[:, j % 4, :], ACT.Sigmoid).then_inc(evac_act, 1)
                if j % 2 and U_PLEG + j // 2 + 2 < N_UNITS:
                    split(U_PLEG + j // 2 + 2)
                if j:
                    act.wait_ge(x_new[1], j)
                    square(n_final, j - 1, X[:, j - 1, :])
            act.wait_ge(x_new[1], KD)
            square(n_final, KD - 1, X[:, KD - 1, :])
            guess(n_final)

        @block.vector
        def _(dve):
            n_self = [0]

            def mark(ins):
                n_self[0] += 1
                ins.then_inc(dve_self, 1)
                return n_self[0]

            def link(ins):
                dve.wait_ge(dve_self, mark(ins))

            def tt(out, a, b, op):
                return nc.vector.tensor_tensor(out, a, b, op)

            def ts(out, a, s1, op0, s2=None, op1=None):
                return (nc.vector.tensor_scalar(out, a, s1, s2, op0, op1) if op1 is not None
                        else nc.vector.tensor_scalar(out, a, s1, None, op0))

            def stt(out, a, s, b, op0, op1):
                return nc.vector.scalar_tensor_tensor(out=out, in0=a, scalar=s, in1=b, op0=op0, op1=op1)

            def low(out, full, hi):
                return tt(out, full, hi.bitcast(f32), ALU.subtract)

            def split(u):
                slot, width = u % 2, tiles_of(u)
                dve.wait_ge(hi_ready, u + 1)
                low(w_lo[slot][:, 0:width * P], w_raw[slot][:, 0:width * P], w_hi[slot][:, 0:width * P]
                    ).then_inc(lo_ready, 1)

            def refine(out, v, r0):
                link(stt(out, v, -0.5, r0, ALU.mult, ALU.mult))
                link(tt(out, out, r0, ALU.mult))
                return stt(out, out, 1.5, r0, ALU.add, ALU.mult)

            def factors(nm, width):
                dve.wait_ge(*nm.total(1))
                ts(stat[:, 0, :], ps[:, SS_BANK, 0:NB], 1.0 / width, ALU.mult, EPS, ALU.add).then_inc(nm.var.sem, 1)
                dve.wait_ge(*nm.guess(1))
                link(refine(stat[:, 3, :], stat[:, 0, :], stat[:, 2, :]))
                for b in range(NB):
                    last = ts(diag[:, b, :], ident[:, :], stat[:, 3, b:b + 1], ALU.mult)
                last.then_inc(nm.diag.sem, 1)

            def apply(nm, src, name, dst_hi, dst_lo, n0=0):
                dve.wait_ge(*nm.factor(1))
                for k in range(nm.n + 1):
                    if k < nm.n:
                        if k >= 2:
                            dve.wait_ge(*nm.lo(k - 1))
                        stt(hf[:, k % 2, :], src[:, k, :], gcol(name, k), ps[:, R_BANK, :], ALU.mult, ALU.mult
                            ).then_inc(nm.f32.sem, 1)
                    if k:
                        dve.wait_ge(*nm.hi(k))
                        low(dst_lo[:, n0 + k - 1, :], hf[:, (k - 1) % 2, :], dst_hi[:, n0 + k - 1, :]
                            ).then_inc(nm.lo.sem, 1)

            def apply_post(nm, f, name, added):
                dve.wait_ge(*nm.factor(1))
                for k in range(KD + 1):
                    if k < KD:
                        if k >= 2:
                            dve.wait_ge(x_new[0], added + k - 1)
                        stt(hf[:, k % 2, :], f[:, k, :], gcol(name, k), ps[:, R_BANK, :], ALU.mult, ALU.mult
                            ).then_inc(nm.f32.sem, 1)
                    if k:
                        dve.wait_ge(*nm.f32(k))
                        tt(X[:, k - 1, :], X[:, k - 1, :], hf[:, (k - 1) % 2, :], ALU.add).then_inc(x_new[0], 1)

            dve.wait_ge(p_hi_ready, 1)
            low(p_lo[:, :, :], hf[:, :, :], p_hi[:, :, :]).then_inc(p_lo_ready, 1)
            dve.wait_ge(c0_landed, 32)
            dve.wait_ge(gain_landed, 16)
            factors(n_mix_pre, D)
            split(0)
            split(1)
            apply(n_mix_pre, X, "norm_mix_pre", h_hi, h_lo)
            dve.wait_ge(c1_landed, 16)

            def rope(j):
                c = ORDER1[j]
                if c in V1:
                    return
                normed, key = c in NORMED, c in (4, 10)
                cos, sin = (C_COSA, C_SINA) if normed else (C_COSB, C_SINB)
                scale = 1.0 if normed or key else SCALE
                i_roped = ROPED.index(c)
                if i_roped:
                    dve.wait_ge(rope_done, i_roped)
                dve.wait_ge(rot_done, i_roped + 1)
                stt(rt[:, 0, :], y[:, j % 2, :], scale, c1[:, cos:cos + S], ALU.mult, ALU.mult)
                m = mark(stt(rt[:, 1, :], ps[:, 4 + j % 2, :], scale, c1[:, sin:sin + S], ALU.mult, ALU.mult))
                if normed:
                    dve.wait_ge(hsum_done, NORMED.index(c) + 1)
                    ts(rt[:, 3, :], ps[:, 6 + j % 2, :], 1.0 / HD, ALU.mult, EPS, ALU.add).then_inc(hvar_ready, 1)
                dve.wait_ge(dve_self, m)
                if normed:
                    link(tt(rt[:, 2, :], rt[:, 0, :], rt[:, 1, :], ALU.add))
                    dve.wait_ge(hguess_ready, NORMED.index(c) + 1)
                    link(refine(rt[:, 5, :], rt[:, 3, :], rt[:, 4, :]))
                if not key:
                    if normed:
                        last = stt(QA[:, c, :], rt[:, 2, :], SCALE, rt[:, 5, :], ALU.mult, ALU.mult)
                    else:
                        last = tt(QB[:, c - 6, :], rt[:, 0, :], rt[:, 1, :], ALU.add)
                else:
                    for kv in range(2):
                        for half in range(2):
                            i = slice(HD * kv, HD * kv + HD)
                            o = slice(HD * half, HD * half + HD)
                            if normed:
                                last = tt(KDA[o, kv, :], rt[i, 2, :], rt[i, 5, :], ALU.mult)
                            else:
                                last = tt(KDB[o, kv, :], rt[i, 0, :], rt[i, 1, :], ALU.add)
                last.then_inc(rope_done, 1)

            for u in range(UNITS_IN1):
                if u:
                    rope(2 * u - 1)
                split(u + 2)
                rope(2 * u)
            rope(11)

            def negmax(s):
                if s >= 64:
                    return
                kind, h, b, k0, k1 = STEPS[s]
                w = (k1 - k0) * P
                dve.wait_ge(s_done, s + 1)
                if kind == 0:
                    nc.vector.tensor_reduce(nmax[:, s:s + 1], ps[:, s % 3, 0:w], AX.X, ALU.max, negate=True
                                            ).then_inc(nmax_ready, 1)
                    return
                m0 = C_MASK + (k0 - b + 1) * P
                if s >= 34:
                    dve.wait_ge(exp_done, s - 1)
                tt(sm[:, s % 2, 0:w], ps[:, s % 3, 0:w], c1[:, m0:m0 + w], ALU.add).then_inc(masked, 1)
                dve.wait_ge(masked, s - 32 + 1)
                link(nc.vector.tensor_reduce(bmax[:, s:s + 1], sm[:, s % 2, 0:w], AX.X, ALU.max))
                ts(nmax[:, s:s + 1], bmax[:, s:s + 1], gain[:, G_SINK + h:G_SINK + h + 1], ALU.max, -1.0, ALU.mult
                   ).then_inc(nmax_ready, 1)

            negmax(0)
            for s, (kind, h, b, k0, k1) in enumerate(STEPS):
                negmax(s + 1)
                w = (k1 - k0) * P
                dve.wait_ge(exp_done, s + 1)
                total = den
                if kind:
                    dve.wait_ge(es_done, s - 32 + 1)
                    link(tt(bmax[:, s:s + 1], den[:, s:s + 1], esink[:, s:s + 1], ALU.add))
                    total = bmax
                link(nc.vector.reciprocal(rden[:, s:s + 1], total[:, s:s + 1]))
                ts(prob[:, s % 2, 0:w], prob[:, s % 2, 0:w], rden[:, s:s + 1], ALU.mult).then_inc(pn_ready, 1)

            for nm, c0, name in ((n_group_a, 0, "group_norm_a"), (n_group_b, 4, "group_norm_b")):
                factors(nm, 4 * P)
                apply(nm, OT[:, c0:c0 + 4, :], name, h_hi, h_lo, c0)
            for u in range(UNITS_OUT1):
                split(U_OUT1 + u + 2)
            factors(n_mix_post, D)
            apply_post(n_mix_post, F1, "norm_mix_post", 0)
            factors(n_ffn_pre, D)
            apply(n_ffn_pre, X, "norm_ffn_pre", h_hi, h_lo)

            def ffn(phase, u_ff, mids0):
                g0, a0, d0 = BASE[phase]

                def turn(i, last=False):
                    for half in range(2):
                        if half:
                            for c in range(2):
                                dve.wait_ge(group_done, i * 4 + (g0 + 3 + c))
                                dve.wait_ge(evac_act, i * 2 + (a0 + 1 + c))
                                if not isinstance(i, int) or i:
                                    dve.wait_ge(prod_lo, i * 2 + (mids0 - 1 + c))
                                tt(hf[:, c, :], sq[:, c, :], ps[:, 2 + c, :], ALU.mult).then_inc(evac_dve, 1)
                            for c in range(2):
                                dve.wait_ge(prod_hi, i * 2 + (mids0 + 1 + c))
                                at = 2 * i + c if isinstance(i, int) else bass.ds(i * 2 + c, 1)
                                low(mid_lo[:, at, :], hf[:, c, :], mid_hi[:, at, :]).then_inc(prod_lo, 1)
                        if last:
                            split(u_ff + 2 * i + 2 + half)
                        else:
                            dve.wait_ge(hi_ready, i * 2 + (u_ff + 3 + half))
                            low(w_lo[half][:, :], w_raw[half][:, :], w_hi[half][:, :]).then_inc(lo_ready, 1)

                turn(0)
                with dve.Fori(1, KF // 2 - 1) as i:
                    turn(i)
                turn(KF // 2 - 1, True)

            ffn("ff1", U_FF1, 0)
            for u in range(UNITS_DOWN):
                split(U_DOWN1 + u + 2)
            factors(n_ffn_post, D)
            apply_post(n_ffn_post, F, "norm_ffn_post", KD)
            factors(n_mix2, D)
            apply(n_mix2, X, "norm_mix_2", h_hi, h_lo)

            for u in range(8):
                split(U_IN2 + u + 2)

            def pool_group(g):
                w, u = POOL_WINDOWS[g], UP[:, g, :]
                src, step, n = u, 1, 0
                if g:
                    dve.wait_ge(pooled, g)
                while step < w:
                    dst = hf[:, n % 2, :]
                    nc.vector.tensor_copy(dst[:, 0:step], src[:, 0:step])
                    link(tt(dst[:, step:S], src[:, step:S], src[:, 0:S - step], ALU.add))
                    src, step, n = dst, 2 * step, n + 1
                tmp = hf[:, n % 2, 0:PADW]
                link(tt(tmp, src[:, 0:PADW], c2[:, 3 * P + g * PADW:3 * P + (g + 1) * PADW], ALU.mult))
                tt(u[:, 0:PADW], tmp, u[:, 0:PADW], ALU.subtract)
                stt(u[:, PADW:S], src[:, PADW:S], 1.0 / w, u[:, PADW:S], ALU.mult, ALU.subtract
                    ).then_inc(pooled, 1)

            dve.wait_ge(evac_act, EVAC["in2", 15][1])
            dve.wait_ge(v2tr_done, 4)
            dve.wait_ge(c2_landed, 32)
            Z = ps[:, 4:7, :].rearrange("p b s -> p (b s)")[:, 0:1280]
            for h in range(NH):
                dve.wait_ge(ln_done, h + 1)
                stt(E2[:, :], Z, 0.0, E2[:, :], ALU.max, ALU.add).then_inc(sp_ready, 1)
                if h < 4:
                    pool_group(h)
                split(U_IN2 + 8 + h + 2)

            for i in range(4):
                dve.wait_ge(pl_hi_ready, i + 1)
                low(pl_lo[:, i, :], UP[:, i, :], pl_hi[:, i, :]).then_inc(pl_lo_ready, 1)
            for i in range(4):
                dve.wait_ge(yb_hi, i + 1)
                low(h_lo[:, 4 + i, :], OB[:, i, :], h_hi[:, 4 + i, :]).then_inc(yb_lo, 1)
            for j in range(4):
                dve.wait_ge(ya_hi, j + 1)
                low(h_lo[:, j, :], hf[:, j % 2, :], h_hi[:, j, :]).then_inc(ya_lo, 1)
                if j % 2:
                    split(U_POOL + j // 2 + 2)
            for j in range(KD):
                dve.wait_ge(sig_ready, j // 2 + 1)
                dve.wait_ge(group_done, GROUP["bra", j])
                tt(GA[:, j, :], GA[:, j, :], ps[:, j % 4, :], ALU.mult).then_inc(evac_dve, 1)
                if j % 4 == 3:
                    split(U_BRA + j // 4 + 2)
            for j in range(KD):
                dve.wait_ge(sig_ready, 4 + j // 2 + 1)
                dve.wait_ge(group_done, GROUP["brb", j])
                tt(GB[:, j, :], GB[:, j, :], ps[:, j % 4, :], ALU.mult).then_inc(evac_dve, 1)
                dve.wait_ge(evac_dve, EVAC["brb", j][1])
                tt(GB[:, j, :], GB[:, j, :], GA[:, j, :], ALU.add).then_inc(merged, 1)
                dve.wait_ge(m_hi_ready, j + 1)
                low(m_lo[:, j, :], GB[:, j, :], m_hi[:, j, :]).then_inc(m_lo_ready, 1)
                if j % 4 == 3:
                    split(U_BRB + j // 4 + 2)
            for j in range(KD):
                dve.wait_ge(group_done, GROUP["out2", j])
                tt(X[:, j, :], X[:, j, :], ps[:, j % 4, :], ALU.add).then_inc(evac_dve, 1)
                if j % 2:
                    split(U_OUT2 + j // 2 + 2)
            factors(n_ffn2, D)
            apply(n_ffn2, X, "norm_ffn_2", h_hi, h_lo)
            ffn("ff2", U_FF2, KF)
            for j in range(KD):
                split(U_DOWN2 + 2 * j + 2)
                dve.wait_ge(group_done, GROUP["down2", j])
                tt(X[:, j, :], X[:, j, :], ps[:, j % 2, :], ALU.add).then_inc(evac_dve, 1)
                split(U_DOWN2 + 2 * j + 3)
            factors(n_ple, D)
            apply(n_ple, X, "norm_ple_2", h_hi, h_lo)
            split(U_PLEP + 2)
            for j in range(KD):
                dve.wait_ge(evac_act, EVAC["pleg", j][1])
                link(tt(hf[:, j % 2, :], hf[:, j % 2, :], PP[:, j, :], ALU.mult))
                tt(X[:, j, :], X[:, j, :], hf[:, j % 2, :], ALU.add).then_inc(x_new[1], 1)
                if j % 2 and U_PLEG + j // 2 + 2 < N_UNITS:
                    split(U_PLEG + j // 2 + 2)
            factors(n_final, D)
            dve.wait_ge(*n_final.factor(1))
            for k in range(KD):
                stt(OUT[:, k, :], X[:, k, :], gcol("norm_final_2", k), ps[:, R_BANK, :], ALU.mult, ALU.mult
                    ).then_inc(out_ready, 1)


def constants():
    import numpy as np

    c = np.zeros((P, C_COLS), np.float32)
    i = np.arange(P)
    c[:, C_ID:C_ID + P] = np.eye(P)
    c[:, C_ONE:C_ONE + P] = 1.0
    c[:, C_HONE:C_HONE + P] = i[:, None] // HD == i[None, :] // HD
    half = HD // 2
    for m in range(P):
        if m % HD < half:
            c[m + half, C_ROT + m] = -1.0
        else:
            c[m - half, C_ROT + m] = 1.0
    c[:, C_TRI:C_TRI + P] = np.where(i[:, None] >= i[None, :], -1.0, 0.0)
    c[:, C_NEG1:C_NEG1 + P] = -1.0
    c[:, C_SMASK:C_SMASK + P] = np.where(i[:, None] >= i[None, :], NEG, 0.0)
    c[:, C_MASK:C_MASK + P] = np.where(i[None, :] >= i[:, None], 0.0, NEG)
    c[:, C_MASK + 2 * P:C_MASK + 3 * P] = np.where(i[None, :] <= i[:, None], 0.0, NEG)
    t = np.arange(S, dtype=np.float32)
    row, col = np.floor(t / 64).astype(np.float32), (t % 64).astype(np.float32)
    quarter = HD // 4
    f_ax = np.float32(10000.0) ** (-np.arange(quarter, dtype=np.float32) / np.float32(quarter))
    f_1d = np.float32(10000.0) ** (-np.arange(half, dtype=np.float32) / np.float32(half))
    ang_a = np.concatenate([row[None, :] * f_ax[:, None], col[None, :] * f_ax[:, None]])
    ang_b = t[None, :] * f_1d[:, None]
    for ang, cos, sin in ((ang_a, C_COSA, C_SINA), (ang_b, C_COSB, C_SINB)):
        ang = np.concatenate([ang.astype(np.float32)] * 4).astype(np.float64)
        c[:, cos:cos + S], c[:, sin:sin + S] = np.cos(ang), np.sin(ang)
    for g, w in enumerate(POOL_WINDOWS):
        c[:, C_INVC + g * PADW:C_INVC + (g + 1) * PADW] = 1.0 / np.minimum(np.arange(PADW) + 1.0, w)
    return c


def tiles(w, order=None):
    k, n = w.shape
    t = w.reshape(k // P, P, n // P, P).transpose(2, 0, 1, 3)
    return t if order is None else t[order]


def pack(ts, per):
    import numpy as np

    ts = ts.reshape(-1, per, P, P).transpose(0, 2, 1, 3).reshape(-1, P, per * P)
    return np.pad(ts, ((0, 0), (0, 0), (0, RAW - per * P)))


def pack_pairs(a, b):
    import numpy as np

    return np.stack([pack(tiles(a), 16), pack(tiles(b), 16)], 1).reshape(-1, P, RAW)


def kernel(**inputs):
    import numpy as np
    import concourse.bacc as bacc
    from concourse import mybir
    from concourse.bass_utils import run_bass_kernel_spmd

    a = {n: np.asarray(v) for n, v in inputs.items()}
    weights = np.concatenate([
        pack(tiles(a["w_in"][0], ORDER1), 16),
        pack(tiles(a["w_out"][0]), 16),
        pack_pairs(a["w_gate"][0], a["w_up"][0]),
        pack(tiles(a["w_down"][0]), DOWN_TILES),
        pack(tiles(a["w_in_2"][0], ORDER2), 16),
        pack(a["w_pool_2"][0], 2),
        pack(tiles(a["w_branch_a_2"][0]), 16),
        pack(tiles(a["w_branch_b_2"][0]), 16),
        pack(tiles(a["w_out_2"][0]), 16),
        pack_pairs(a["w_ffn_gate_2"][0], a["w_ffn_up_2"][0]),
        pack(tiles(a["w_ffn_down_2"][0]), DOWN_TILES),
        pack(tiles(a["w_ple_proj_2"][0]), 16),
        pack(tiles(a["w_ple_gate_2"][0]), 16),
    ])
    cols = [a[n].reshape(-1, P).T for n in GAINS]
    cols += [np.concatenate([a[n].reshape(-1)] * 2)[:, None] for n in ("q_norm_a", "k_norm_a")]
    cols.append(np.broadcast_to(a["sink_b"].reshape(1, NH), (P, NH)))
    arrays = {
        "x_t": np.ascontiguousarray(a["x"][0].T),
        "p_t": np.ascontiguousarray(a["p_2"][0, 0].T),
        "weights": np.ascontiguousarray(weights),
        "gains": np.ascontiguousarray(np.concatenate(cols, 1)),
        "constants": constants(),
    }
    nc = bacc.Bacc("TRN2", target_bir_lowering=False, num_devices=1)
    args = [nc.dram_tensor(n, v.shape, mybir.dt.from_np(v.dtype), kind="ExternalInput").ap()
            for n, v in arrays.items()]
    args.append(nc.dram_tensor("out_t", (D, S), mybir.dt.float32, kind="ExternalOutput").ap())
    build(nc, *args)
    r = run_bass_kernel_spmd(nc, [arrays], core_ids=[0])
    return r.results[0]["out_t"].T.reshape(1, S, D)
```

```python
D = 1024
S = 512
P = 128
KD = D // P
FF = 2816
KF = FF // P
HD = 64
NH = 8
NB = S // P
EPS = 1e-6
SCALE = HD ** -0.5
POOL_WINDOWS = (2, 4, 8, 16)
PADW = 16
RAW = 2048
NEG = -3.0e38

DOWN_TILES = KF // 2
UNITS_IN1, UNITS_OUT1 = 6, 4
UNITS_FF, UNITS_DOWN = 2 * (KF // 2), 2 * KD
UNITS_IN2, UNITS_POOL, UNITS_BRANCH, UNITS_OUT2 = 16, 2, 2, 4
U_IN1 = 0
U_OUT1 = U_IN1 + UNITS_IN1
U_FF1 = U_OUT1 + UNITS_OUT1
U_DOWN1 = U_FF1 + UNITS_FF
U_IN2 = U_DOWN1 + UNITS_DOWN
U_POOL = U_IN2 + UNITS_IN2
U_BRA = U_POOL + UNITS_POOL
U_BRB = U_BRA + UNITS_BRANCH
U_OUT2 = U_BRB + UNITS_BRANCH
U_FF2 = U_OUT2 + UNITS_OUT2
U_DOWN2 = U_FF2 + UNITS_FF
U_PLEP = U_DOWN2 + UNITS_DOWN
U_PLEG = U_PLEP + 1
N_UNITS = U_PLEG + 4

NORM_A_STEP = 38

LN_EXP, SILU, SIGMOID = "natural_log_exp_and_others", "silu_and_others", "sigmoid_and_others"

GAINS = ["norm_mix_pre", "norm_mix_post", "norm_ffn_pre", "norm_ffn_post", "norm_mix_2", "norm_ffn_2",
         "norm_ple_2", "norm_final_2", "group_norm_a", "group_norm_b", "pool_scale_2"]
GAIN_W = [KD] * 8 + [4] * 3
GAIN_AT = {n: sum(GAIN_W[:i]) for i, n in enumerate(GAINS)}
G_QN = sum(GAIN_W)
G_KN = G_QN + 1
G_SINK = G_QN + 2
G_COLS = G_SINK + NH

C_ID, C_ONE, C_HONE, C_ROT, C_TRI, C_NEG1, C_SMASK = (P * i for i in range(7))
C_MASK = 7 * P
C_COSA, C_SINA, C_COSB, C_SINB = (9 * P + S * i for i in range(4))
C_INVC = 9 * P + 4 * S
C_COLS = C_INVC + 4 * PADW


ORDER1 = [4, 5, 0, 1, 2, 3, 10, 11, 6, 7, 8, 9]
V1 = [5, 11]
NORMED = [4, 0, 1, 2, 3]
ROPED = [c for c in ORDER1 if c not in V1]
ORDER2 = [*range(8, 12), *range(4, 8), *range(12, 16), *range(0, 4), *range(16, 32)]
STEPS = [(0, h, b, 0, NB) for h in range(NH) for b in range(NB)] + [
    (1, h, b, max(b - 1, 0), min(b + 2, NB)) for h in range(NH) for b in range(NB)]


def build(nc, xT, pT, weights, gains, consts, outT):
    import concourse.bass as bass
    from concourse import mybir
    from contextlib import ExitStack

    f32, f32r = mybir.dt.float32, mybir.dt.float32r
    ACT = mybir.ActivationFunctionType
    ALU = mybir.AluOpType
    AX = mybir.AxisListType

    ctx = ExitStack()
    with ctx:
        def sb(name, shape, dt=f32, stack=ctx):
            return stack.enter_context(nc.sbuf_tensor(name, shape, dt))

        def sem(name):
            return ctx.enter_context(nc.semaphore(name))

        X = sb("X", [P, KD, S])
        w_raw = [sb(f"w_raw{i}", [P, RAW]) for i in range(2)]
        w_hi = [sb(f"w_hi{i}", [P, RAW], f32r) for i in range(2)]
        w_lo = [sb(f"w_lo{i}", [P, RAW], f32r) for i in range(2)]
        p_hi = sb("p_hi", [P, 2, S], f32r)
        p_lo = sb("p_lo", [P, 2, S], f32r)
        ident = sb("ident", [P, P])
        ones = sb("ones", [P, P])
        gain = sb("gain", [P, G_COLS])
        sq = sb("sq", [P, 2, S])
        hf = sb("hf", [P, 2, S])
        sqsum = sb("sqsum", [P, S])
        with ExitStack() as shared:
            diag = sb("diag", [P, NB, P], stack=shared)
        factors_sb = sb("factors_sb", [P, S])
        stat = sb("stat", [P, 5, NB])

        with ExitStack() as lowpart:
            h_lo = sb("h_lo", [P, KD, S], f32r, lowpart)
        F = sb("F", [P, KD, S])
        h_hi = sb("h_hi", [P, KD, S], f32r)

        with ExitStack() as st:
            with ExitStack() as st2:
                F1 = sb("F1", [P, KD, S], stack=st2)
            QA = sb("QA", [P, 4, S], stack=st)
            QB = sb("QB", [P, 4, S], stack=st)
            KDA = sb("KDA", [P, 2, S], stack=st)
            KDB = sb("KDB", [P, 2, S], stack=st)
            VA = sb("VA", [P, NB, P], stack=st)
            VB = sb("VB", [P, NB, P], stack=st)
            c1 = sb("c1", [P, C_COLS], stack=st)
            with ExitStack() as st2:
                OT = sb("OT", [P, 8, S], stack=st2)
            y = sb("y", [P, 2, S], stack=st)
            ysq = sb("ysq", [P, 2, S], stack=st)
            rt = sb("rt", [P, 6, S], stack=st)
            prob = sb("prob", [P, 3, S], stack=st)
            ident_r = sb("ident_r", [P, P], f32r, st)
            mask_r = sb("mask_r", [P, 2, P], f32r, st)
            PT = sb("PT", [P, 2, NB, S], stack=st)
            nmax = sb("nmax", [P, 64], stack=st)
            den = sb("den", [P, 64], stack=st)
            rden = sb("rden", [P, 64], stack=st)
        with ExitStack() as st:
            mid_hi = sb("mid_hi", [P, KF, S], f32r, st)
            mid_lo = sb("mid_lo", [P, KF, S], f32r, st)
        with ExitStack() as st:
            with ExitStack() as st2:
                Q2 = sb("Q2", [P, 4, S], stack=st2)
                K2 = sb("K2", [P, 4, S], stack=st2)
                V2 = sb("V2", [P, NB, S], stack=st2)
                E2 = sb("E2", [P, 1280], stack=st2)
                A2 = sb("A2", [P, 2, 1280], stack=st2)
            with ExitStack() as st2:
                pl_hi = sb("pl_hi", [P, 4, S], f32r, st2)
                pl_lo = sb("pl_lo", [P, 4, S], f32r, st2)
            with ExitStack() as st2:
                m_hi = sb("m_hi", [P, KD, S], f32r, st2)
                m_lo = sb("m_lo", [P, KD, S], f32r, st2)
            sb("behind", [P, 9984], stack=st)
            GA = sb("GA", [P, KD, S], stack=st)
            GB = sb("GB", [P, KD, S], stack=st)
            UP = sb("UP", [P, 4, S], stack=st)
            OB = sb("OB", [P, 4, S], stack=st)
            c2 = sb("c2", [P, 3 * P + 4 * PADW], stack=st)
        with ExitStack() as st:
            PP = sb("PP", [P, KD, S], stack=st)
            OUT = sb("OUT", [P, KD, S], stack=st)

        ps = ctx.enter_context(nc.psum_tensor("ps", [P, 8, S], f32))
        R_BANK, SS_BANK = 4, 5
        GROUP_A_BANK = 7

        raw_landed = [sem(f"raw_landed{i}") for i in range(2)]
        hi_ready, lo_ready = sem("hi_ready"), sem("lo_ready")
        group_done = sem("group_done")
        evac_act, evac_dve = sem("evac_act"), sem("evac_dve")
        x_landed = [sem(f"x_landed{i}") for i in range(4)]
        gain_landed, c0_landed, c1_landed, c2_landed, p_landed = (
            sem(n) for n in ("gain_landed", "c0_landed", "c1_landed", "c2_landed", "p_landed"))
        p_hi_ready, p_lo_ready = sem("p_hi_ready"), sem("p_lo_ready")
        dve_self, act_self, pool_self = sem("dve_self"), sem("act_self"), sem("pool_self")
        ysq_ready, rot_done, hsum_done, hvar_ready, hguess_ready, rope_done, v_ready = (
            sem(n) for n in ("ysq_ready", "rot_done", "hsum_done", "hvar_ready", "hguess_ready", "rope_done",
                             "v_ready"))
        vtr_done = sem("vtr_done")
        masks_ready, s_done, nmax_ready, exp_done, pn_ready, tr_done, pt_ready, av_done, ot_ready = (
            sem(n) for n in ("masks_ready", "scores_done", "negmax_ready", "exp_done", "prob_normed", "transposed",
                             "pt_ready", "av_done", "ot_ready"))
        z_done, ln_done, sp_ready, sp_masked, cum_done, a_done, av2_done, ob_ready = (
            sem(n) for n in ("z_done", "ln_done", "sp_ready", "sp_masked", "cum_done", "a_done", "av2_done", "ob_ready"))
        v2tr_done, v2_ready = sem("v2tr_done"), sem("v2_ready")
        pooled, pl_hi_ready, pl_lo_ready = sem("pooled"), sem("pl_hi_ready"), sem("pl_lo_ready")
        ya_ready, ya_hi, ya_lo, yb_hi, yb_lo = (sem(n) for n in ("ya_ready", "ya_hi", "ya_lo", "yb_hi", "yb_lo"))
        sig_ready, merged, m_hi_ready, m_lo_ready = (sem(n) for n in ("sig_ready", "merged", "m_hi_ready", "m_lo_ready"))
        x_new = [sem(f"x_new{i}") for i in range(3)]
        silu_ready, prod_ready, prod_hi, prod_lo = (
            sem(n) for n in ("silu_ready", "prod_ready", "prod_hi_ready", "prod_lo_ready"))
        out_ready, out_stored = sem("out_ready"), sem("out_stored")

        class Count:

            def __init__(self, sem, base=0):
                self.sem, self.base = sem, base

            def __call__(self, n):
                return self.sem, self.base + n

        NORM_EVENTS = ("squares",
                       "summed",
                       "total",
                       "var",
                       "guess",
                       "diag",
                       "factor",
                       "f32",
                       "hi",
                       "lo")
        norm_sems = {e: sem("norm_" + e) for e in NORM_EVENTS}
        norm_counts = dict.fromkeys(NORM_EVENTS, 0)

        class Norm:

            def __init__(self, n, kind, before):
                self.n, self.before = n, before
                self.r_bank, self.ss_bank = R_BANK, SS_BANK
                (self.squares, self.summed, self.total, self.var, self.guess, self.diag, self.factor, self.f32,
                 self.hi, self.lo) = (Count(norm_sems[e], norm_counts[e]) for e in NORM_EVENTS)
                n_f32 = {"split": n, "late": 1, "added": n, "final": 0}[kind]
                self.factor_used = self.f32(n_f32)
                for e in NORM_EVENTS:
                    norm_counts[e] += (n if e in ("squares", "summed") else n_f32 if e == "f32" else
                                       (n if kind in ("split", "late") else 0) if e in ("hi", "lo") else 1)

        norms = []
        for n, kind in ((KD, "split"), (4, "split"), (4, "split"), (KD, "added"), (KD, "late"), (KD, "added"),
                        (KD, "late"), (KD, "late"), (KD, "split"), (KD, "final")):
            norms.append(Norm(n, kind, norms[-1] if norms else None))
        (n_mix_pre, n_group_a, n_group_b, n_mix_post, n_ffn_pre, n_ffn_post, n_mix2, n_ffn2, n_ple,
         n_final) = norms
        n_group_a.r_bank = n_group_a.ss_bank = GROUP_A_BANK

        PHASES = [("in1", 12, "A", 4, 1), ("out1", KD, "A", 4, 1), ("ff1", 2 * KF, "D", 4, 1),
                  ("down1", KD, "A", 2, 2), ("in2", 32, "D", 4, 1), ("pool", 4, "A", 4, 1),
                  ("bra", KD, "D", 4, 1), ("brb", KD, "D", 4, 1), ("out2", KD, "D", 4, 1),
                  ("ff2", 2 * KF, "D", 4, 1), ("down2", KD, "D", 2, 2), ("plep", KD, "A", 4, 1),
                  ("pleg", KD, "A", 4, 1)]
        GROUP, EVAC, BEFORE, BASE = {}, {}, {}, {}
        counts, groups, users = {"A": 0, "D": 0}, 0, {}
        for phase, n, engines, banks, parts in PHASES:
            BASE[phase] = (groups, counts["A"], counts["D"])
            for j in range(n):
                e = engines[j % len(engines)]
                groups += parts
                counts[e] += 1
                GROUP[phase, j] = groups
                EVAC[phase, j] = (e, counts[e])
                BEFORE[phase, j] = users.get(j % banks)
                users[j % banks] = (e, counts[e])

        USED = []
        for phase, n, engines, banks, parts in PHASES:
            per = {"pool": 2, "bra": 4, "brb": 4, "plep": 8}.get(phase, 2)
            if parts == 2:
                USED += [g for j in range(n) for g in (GROUP[phase, j] - 1, GROUP[phase, j])]
            else:
                USED += [GROUP[phase, j + per - 1] for j in range(0, n, per)]
        assert len(USED) == N_UNITS

        block = ctx.enter_context(nc.Block())

        def gcol(name, k):
            c = GAIN_AT[name] + k
            return gain[:, c:c + 1]

        def tiles_of(u):
            if U_DOWN1 <= u < U_IN2 or U_DOWN2 <= u < U_PLEP:
                return DOWN_TILES
            return 2 if U_POOL <= u < U_BRA else 16

        @block.sync
        def _(sp):
            def load(u, slot, width, first=False):
                if not first:
                    sp.wait_ge(lo_ready, u - 1)
                sp.dma_start(w_raw[slot][:, 0:width * P], weights[bass.ds(u, 1), :, 0:width * P]
                             if not isinstance(u, int) else weights[u, :, 0:width * P]
                             ).then_inc(raw_landed[slot], 16)

            for i in range(4):
                sp.dma_start(X[:, 2 * i:2 * i + 2, :],
                             xT[i * 2 * P:(i + 1) * 2 * P, :].rearrange("(k p) s -> p k s", p=P)
                             ).then_inc(x_landed[i], 16)
            load(0, 0, 16, True)
            load(1, 1, 16, True)

            def run(start, n):
                with sp.Fori(0, n // 2) as i:
                    for slot in range(2):
                        u = i * 2 + (start + slot)
                        sp.wait_ge(lo_ready, u - 1)
                        sp.dma_start(w_raw[slot][:, 0:tiles_of(start) * P],
                                     weights[bass.ds(u, 1), :, 0:tiles_of(start) * P]
                                     ).then_inc(raw_landed[slot], 16)

            run(2, U_DOWN1 - 2)
            run(U_DOWN1, UNITS_DOWN)
            run(U_IN2, UNITS_IN2)
            run(U_POOL, UNITS_POOL)
            run(U_BRA, U_DOWN2 - U_BRA)
            run(U_DOWN2, UNITS_DOWN)
            for u in range(U_PLEP, N_UNITS):
                load(u, u % 2, 16)
            for k in range(KD):
                sp.wait_ge(out_ready, k + 1)
                sp.dma_start(outT[k * P:(k + 1) * P, :], OUT[:, k, :]).then_inc(out_stored, 16)
            sp.wait_ge(out_stored, 16 * KD)

        @block.gpsimd
        def _(pool):
            def sum_squares(nm):
                if nm.before is not None:
                    pool.wait_ge(*nm.before.total(1))
                nc.gpsimd.memset(sqsum[:, :], 0.0).then_inc(nm.summed.sem, 1)
                for j in range(nm.n - 1):
                    pool.wait_ge(*nm.squares(j + 1))
                    pool.wait_ge(*nm.summed(j + 1))
                    nc.gpsimd.tensor_tensor(sqsum[:, :], sqsum[:, :], sq[:, j % 2, :], ALU.add
                                            ).then_inc(nm.summed.sem, 1)

            def zero_masked(t):
                for at in (0, 512, 896, 1024):
                    v = t[:, at:at + P]
                    last = nc.gpsimd.affine_select(out=v, in_=v, compare_op=ALU.is_gt, fill=0.0, base=0,
                                                   pattern=[[1, P]], channel_multiplier=-1)
                return last

            for nm in norms[:7]:
                sum_squares(nm)
            for h in range(NH):
                pool.wait_ge(sp_ready, h + 1)
                zero_masked(E2[:, :]).then_inc(sp_masked, 1)
            for nm in norms[7:]:
                sum_squares(nm)

        @block.tensor
        def _(pe):
            def mm(out, lhsT, rhs, start=True, stop=True, loose=False):
                return nc.tensor.matmul(out, lhsT, rhs, start=start, stop=stop, skip_group_check=loose)

            def three(bank, slot, t, hi, lo, start, stop):
                whi, wlo = w_hi[slot][:, t * P:(t + 1) * P], w_lo[slot][:, t * P:(t + 1) * P]
                mm(ps[:, bank, :], whi, hi, start, False)
                mm(ps[:, bank, :], whi, lo, False, False)
                return mm(ps[:, bank, :], wlo, hi, False, stop)

            def wait_bank(phase, j):
                if BEFORE[phase, j]:
                    e, n = BEFORE[phase, j]
                    pe.wait_ge(evac_act if e == "A" else evac_dve, n)

            def group(slot, t0, ks, bank, hi, lo, start=True, stop=True, ready=None):
                for n, k in enumerate(ks):
                    if ready is not None:
                        pe.wait_ge(ready[0], ready[1] + k + 1)
                    last = three(bank, slot, t0 + n, hi[:, k, :], lo[:, k, :], start and n == 0,
                                 stop and n == len(ks) - 1)
                last.then_inc(group_done, 1)

            def first_unit(phase, u, ks, hi, lo, readies):
                for j in range(2):
                    wait_bank(phase, j)
                pe.wait_ge(lo_ready, u + 1)
                for n, (k, ready) in enumerate(zip(ks, readies)):
                    pe.wait_ge(*ready)
                    for j in range(2):
                        last = three(j, u % 2, j * len(ks) + n, hi[:, k, :], lo[:, k, :], n == 0, n == len(ks) - 1)
                        if n == len(ks) - 1:
                            last.then_inc(group_done, 1)

            def parts_of(count):
                return [count(k + 1) for k in KS]

            def unit(phase, u, j0, nchunks, ks, hi, lo, after=None):
                pe.wait_ge(lo_ready, u + 1)
                for c in range(nchunks):
                    wait_bank(phase, j0 + c)
                    group(u % 2, c * len(ks), ks, (j0 + c) % 4, hi, lo)
                    if after:
                        after(j0 + c)

            def total(nm):
                for src, ready, n in ((sqsum[:, :], nm.summed, nm.n), (sq[:, (nm.n - 1) % 2, :], nm.squares, nm.n)):
                    pe.wait_ge(*ready(n))
                    for b in range(NB):
                        last = mm(ps[:, nm.ss_bank, b:b + 1], src[:, b * P:(b + 1) * P], ones[:, 0:1],
                                  ready is nm.summed and b == 0, True, loose=True)
                last.then_inc(nm.total.sem, 1)

            def factor(nm):
                pe.wait_ge(*nm.diag(1))
                if nm.before is not None:
                    pe.wait_ge(*nm.before.factor_used)
                mm(ps[:, nm.r_bank, :], ones[:, :], diag[:, :, :]).then_inc(nm.factor.sem, 1)

            KS = range(KD)
            pe.wait_ge(c0_landed, 32)
            total(n_mix_pre)
            factor(n_mix_pre)

            def free_item(j):
                if j >= 0:
                    if ORDER1[j] in V1:
                        pe.wait_ge(v_ready, V1.index(ORDER1[j]) + 1)
                    else:
                        pe.wait_ge(rope_done, ROPED.index(ORDER1[j]) + 1)

            def item(j):
                if j < 0:
                    return
                c = ORDER1[j]
                free_item(j - 2)
                if j == 0:
                    pe.wait_ge(*n_mix_pre.lo(KD))
                    pe.wait_ge(c1_landed, 16)
                pe.wait_ge(evac_act, EVAC["in1", j][1])
                if c in V1:
                    for b in range(NB):
                        last = nc.tensor.transpose(ps[:, 4 + j % 2, b * P:(b + 1) * P],
                                                   y[:, j % 2, b * P:(b + 1) * P], ident[:, :])
                    last.then_inc(vtr_done, 1)
                    return
                mm(ps[:, 4 + j % 2, :], c1[:, C_ROT:C_ROT + P], y[:, j % 2, :]).then_inc(rot_done, 1)
                if c in NORMED:
                    pe.wait_ge(ysq_ready, NORMED.index(c) + 1)
                    mm(ps[:, 6 + j % 2, :], c1[:, C_HONE:C_HONE + P], ysq[:, j % 2, :]).then_inc(hsum_done, 1)

            first_unit("in1", 0, KS, h_hi, h_lo, parts_of(n_mix_pre.lo))
            for u in range(1, UNITS_IN1):
                unit("in1", u, 2 * u, 2, KS, h_hi, h_lo,
                     after=lambda j: (item(0) if j == 2 else None, item(j - 1)))
            item(11)

            pe.wait_ge(rope_done, len(ROPED))
            pe.wait_ge(v_ready, 2)
            pe.wait_ge(evac_act, EVAC["in1", 11][1])

            def scores(s):
                if s >= 64:
                    return
                kind, h, b, k0, k1 = STEPS[s]
                if s >= 3:
                    pe.wait_ge(exp_done, s - 2)
                q, kd = (QA, KDA) if kind == 0 else (QB, KDB)
                r, w, bank = HD * (h % 2), (k1 - k0) * P, s % 3
                last = mm(ps[:, bank, 0:w], q[r:r + HD, h // 2, b * P:(b + 1) * P],
                          kd[r:r + HD, h // 4, k0 * P:k1 * P], True, kind == 0, loose=kind == 1)
                if kind:
                    if b:
                        mm(ps[:, bank, 0:P], ident_r[:, :], mask_r[:, 0, :], False, True, loose=True)
                    if b + 1 < NB:
                        mm(ps[:, bank, w - P:w], ident_r[:, :], mask_r[:, 1, :], False, True, loose=True)
                    last = mm(ps[:, bank, w:w + 1], ident[:, :], gain[:, G_SINK + h:G_SINK + h + 1], False, True,
                              loose=True)
                last.then_inc(s_done, 1)

            def weighted(g):
                c = g // 2
                if c >= 2 and g % 2 == 0:
                    pe.wait_ge(ot_ready, c - 1)
                r, v = HD * (g % 2), (VA if g < NH else VB)
                kv = (g % NH) // 4
                pe.wait_ge(pt_ready, 4 * (g + 1))
                order = ([(kb, 0, NB) for kb in range(NB)] if g < NH else
                         [(1, 0, 3), (0, 0, 2), (2, 1, 4), (3, 2, 4)])
                for n, (kb, q0, q1) in enumerate(order):
                    last = mm(ps[r:r + HD, 5 + c % 2, q0 * P:q1 * P], v[:, kb, kv * HD:(kv + 1) * HD],
                              PT[:, g % 2, kb, q0 * P:q1 * P], n == 0, n == len(order) - 1, loose=True)
                last.then_inc(av_done, 1)

            pe.wait_ge(masks_ready, 2)
            scores(0)
            scores(1)
            for s, (kind, h, b, k0, k1) in enumerate(STEPS):
                scores(s + 2)
                pe.wait_ge(pn_ready, s + 1)
                if s >= 2:
                    pe.wait_ge(pt_ready, s - 1)
                for kb in range(k0, k1):
                    last = nc.tensor.transpose(ps[:, 3 + s % 2, (kb - k0) * P:(kb - k0 + 1) * P],
                                               prob[:, s % 3, (kb - k0) * P:(kb - k0 + 1) * P], ident[:, :])
                last.then_inc(tr_done, 1)
                if s % 4 == 2 and s > 2:
                    weighted(s // 4 - 1)
                if s == NORM_A_STEP + 4:
                    total(n_group_a)
                if s == NORM_A_STEP + 8:
                    factor(n_group_a)
            weighted(15)
            pe.wait_ge(ot_ready, 8)
            pe.wait_ge(pt_ready, 64)
            total(n_group_b)
            factor(n_group_b)

            first_unit("out1", U_OUT1, KS, h_hi, h_lo,
                       [nm.lo(k + 1) for nm in (n_group_a, n_group_b) for k in range(4)])
            for u in range(1, UNITS_OUT1):
                unit("out1", U_OUT1 + u, 2 * u, 2, KS, h_hi, h_lo)

            def ffn(phase, down, u_ff, u_down, nm, mids0):
                g0, a0, d0 = BASE[phase]
                first_unit(phase, u_ff, KS, h_hi, h_lo, parts_of(nm.lo))
                total(nm)
                unit(phase, u_ff + 1, 2, 2, KS, h_hi, h_lo, after=lambda j: factor(nm) if j == 2 else None)
                with pe.Fori(1, KF // 2) as i:
                    for half in range(2):
                        for c in range(2):
                            pe.wait_ge(lo_ready, i * 2 + (u_ff + 1 + half))
                            pe.wait_ge(evac_dve, i * 4 + (d0 - 3 + 2 * half + c))
                            group(half, c * KD, KS, 2 * half + c, h_hi, h_lo)
                g0, a0, d0 = BASE[down]
                pe.wait_ge(evac_dve, d0)

                def chunk(j, c, ready=None):
                    for part in range(2):
                        pe.wait_ge(lo_ready, j * 2 + (u_down + part + 1))
                        group(part, 0, range(part * DOWN_TILES, (part + 1) * DOWN_TILES), c, mid_hi, mid_lo,
                              part == 0, part == 1, ready)

                chunk(0, 0, (prod_lo, mids0))
                chunk(1, 1)
                evac, e0 = (evac_act, a0) if down == "down1" else (evac_dve, d0)
                with pe.Fori(1, KD // 2) as i:
                    for c in range(2):
                        pe.wait_ge(evac, i * 2 + (e0 - 1 + c))
                        chunk(i * 2 + c, c)

            total(n_mix_post)
            factor(n_mix_post)
            ffn("ff1", "down1", U_FF1, U_DOWN1, n_ffn_pre, 0)
            total(n_ffn_post)
            factor(n_ffn_post)

            def vee(i):
                pe.wait_ge(evac_dve, EVAC["in2", 8 + i][1])
                if i >= 2:
                    pe.wait_ge(v2_ready, i - 1)
                for b in range(NB):
                    last = nc.tensor.transpose(ps[:, 4 + i % 2, b * P:(b + 1) * P],
                                               hf[:, i % 2, b * P:(b + 1) * P], ident[:, :])
                last.then_inc(v2tr_done, 1)

            first_unit("in2", U_IN2, KS, h_hi, h_lo, parts_of(n_mix2.lo))
            total(n_mix2)
            for u in range(1, 8):
                unit("in2", U_IN2 + u, 2 * u, 2, KS, h_hi, h_lo,
                     after=lambda j: vee(j - 9) if 9 <= j < 13 else factor(n_mix2) if j == 2 else None)
            Z = ps[:, 4:7, :].rearrange("p b s -> p (b s)")
            AHEAD = 4

            def three_rows(slot, t0, bank, k0, k1):
                for k in range(k0, k1):
                    last = three(bank, slot, t0 + k, h_hi[:, k, :], h_lo[:, k, :], k == 0, k == KD - 1)
                return last

            ZAT = [0, 512, 1024, 896]
            pe.wait_ge(v2_ready, 4)
            pe.wait_ge(c2_landed, 32)
            for h in range(NH):
                r = HD * (h % 2)
                if h:
                    pe.wait_ge(a_done, h)
                for kb in range(NB):
                    w = S - kb * P
                    last = mm(Z[:, ZAT[kb]:ZAT[kb] + w], K2[r:r + HD, h // 2, kb * P:(kb + 1) * P],
                              Q2[r:r + HD, h // 2, kb * P:S], kb < 3, True, loose=True)
                last.then_inc(z_done, 1)
                u = 8 + h
                pe.wait_ge(lo_ready, U_IN2 + u + 1)
                wait_bank("in2", 2 * u)
                group(u % 2, 0, KS, (2 * u) % 4, h_hi, h_lo)
                wait_bank("in2", 2 * u + 1)
                three_rows(u % 2, KD, (2 * u + 1) % 4, 0, AHEAD)
                pe.wait_ge(sp_masked, h + 1)
                for kb in range(NB):
                    for later in range(kb, NB):
                        w = S - later * P
                        o = ZAT[kb] + (later - kb) * P
                        last = mm(Z[:, o:o + w], c2[:, 0:P] if later == kb else c2[:, P:2 * P],
                                  E2[:, ZAT[later]:ZAT[later] + w], False, True, loose=True)
                    last = mm(Z[:, ZAT[kb]:ZAT[kb] + P], ident[:, :], c2[:, 2 * P:3 * P], False, True, loose=True)
                last.then_inc(cum_done, 1)
                three_rows(u % 2, KD, (2 * u + 1) % 4, AHEAD, KD).then_inc(group_done, 1)
                pe.wait_ge(a_done, h + 1)
                if h % 2 == 0 and h:
                    pe.wait_ge(ob_ready, h // 2)
                for kb in range(NB):
                    w = S - kb * P
                    last = mm(ps[r:r + HD, 7, kb * P:S], V2[:, kb, h * HD:(h + 1) * HD],
                              A2[:, h % 2, ZAT[kb]:ZAT[kb] + w], kb == 0, kb == 3, loose=True)
                last.then_inc(av2_done, 1)

            for u in range(UNITS_POOL):
                pe.wait_ge(lo_ready, U_POOL + u + 1)
                for c in range(2):
                    j = 2 * u + c
                    wait_bank("pool", j)
                    pe.wait_ge(pl_lo_ready, j + 1)
                    group(u % 2, c, range(j, j + 1), j % 4, pl_hi, pl_lo)
            pe.wait_ge(ya_lo, 4)
            for u in range(UNITS_BRANCH):
                unit("bra", U_BRA + u, 4 * u, 4, range(4), h_hi, h_lo)
            pe.wait_ge(yb_lo, 4)
            for u in range(UNITS_BRANCH):
                unit("brb", U_BRB + u, 4 * u, 4, range(4, 8), h_hi, h_lo)
            first_unit("out2", U_OUT2, KS, m_hi, m_lo, parts_of(Count(m_lo_ready)))
            for u in range(1, UNITS_OUT2):
                unit("out2", U_OUT2 + u, 2 * u, 2, KS, m_hi, m_lo)
            ffn("ff2", "down2", U_FF2, U_DOWN2, n_ffn2, KF)

            total(n_ple)
            pe.wait_ge(p_lo_ready, 1)
            unit("plep", U_PLEP, 0, KD, range(2), p_hi, p_lo)
            factor(n_ple)
            first_unit("pleg", U_PLEG, KS, h_hi, h_lo, parts_of(n_ple.lo))
            for u in range(1, 4):
                unit("pleg", U_PLEG + u, 2 * u, 2, KS, h_hi, h_lo)
            total(n_final)
            factor(n_final)

        @block.scalar
        def _(act):
            n_self = [0]

            def link(ins):
                n_self[0] += 1
                ins.then_inc(act_self, 1)
                act.wait_ge(act_self, n_self[0])

            def af(out, in_, func, **kw):
                return nc.scalar.activation(out, in_, func, **kw)

            def split(u, slot=None, width=None):
                slot = u % 2 if slot is None else slot
                width = tiles_of(u) if width is None else width
                half = u // 2 if isinstance(u, int) else None
                act.wait_ge(raw_landed[slot], 16 * (half + 1))
                if u >= 2:
                    act.wait_ge(group_done, USED[u - 2])
                af(w_hi[slot][:, 0:width * P], w_raw[slot][:, 0:width * P], ACT.Copy).then_inc(hi_ready, 1)

            def square(nm, j, src):
                if j >= 2:
                    act.wait_ge(*nm.summed(j))
                af(sq[:, j % 2, :], src, ACT.Square).then_inc(nm.squares.sem, 1)

            def tables(name):
                nc.scalar.preload_act_table_set(name)

            def guess(nm):
                act.wait_ge(*nm.var(1))
                link(af(stat[:, 1, :], stat[:, 0, :], ACT.Ln))
                af(stat[:, 2, :], stat[:, 1, :], ACT.Exp, scale=-0.5).then_inc(nm.guess.sem, 1)

            def high_one(nm, dst, k, n0):
                act.wait_ge(*nm.f32(k + 1))
                af(dst[:, n0 + k, :], hf[:, k % 2, :], ACT.Copy).then_inc(nm.hi.sem, 1)

            def high(nm, dst, n0=0):
                for k in range(nm.n):
                    high_one(nm, dst, k, n0)

            def late_part(nm, name, k):
                square(nm, k, X[:, k, :])
                af(h_hi[:, k, :], X[:, k, :], ACT.Copy, scale=gcol(name, k)).then_inc(nm.hi.sem, 1)

            def late_factors(nm):
                act.wait_ge(*nm.factor(1))
                af(factors_sb[:, :], ps[:, nm.r_bank, :], ACT.Copy).then_inc(nm.f32.sem, 1)

            tables(LN_EXP)
            act.dma_start(gain[:, :], gains[:, :]).then_inc(gain_landed, 16)
            act.dma_start(ident[:, :], consts[:, C_ID:C_ID + P]).then_inc(c0_landed, 16)
            act.dma_start(ones[:, :], consts[:, C_ONE:C_ONE + P]).then_inc(c0_landed, 16)
            act.dma_start(hf[:, :, :], pT.rearrange("(k p) s -> p k s", p=P)).then_inc(p_landed, 16)
            act.dma_start(c1[:, :], consts[:, :]).then_inc(c1_landed, 16)
            act.wait_ge(gain_landed, 16)
            for k in range(KD):
                act.wait_ge(x_landed[k // 2], 16)
                square(n_mix_pre, k, X[:, k, :])
            act.wait_ge(p_landed, 16)
            af(p_hi[:, :, :], hf[:, :, :], ACT.Copy).then_inc(p_hi_ready, 1)
            guess(n_mix_pre)
            split(0)
            split(1)
            high(n_mix_pre, h_hi)

            def free_item(j):
                if j >= 0:
                    if ORDER1[j] in V1:
                        act.wait_ge(v_ready, V1.index(ORDER1[j]) + 1)
                    else:
                        act.wait_ge(rope_done, ROPED.index(ORDER1[j]) + 1)

            def finish(j):
                c = ORDER1[j]
                if c in V1:
                    act.wait_ge(vtr_done, V1.index(c) + 1)
                    af((VA if c == 5 else VB)[:, :, :], ps[:, 4 + j % 2, :].rearrange("p (b c) -> p b c", b=NB),
                       ACT.Copy).then_inc(v_ready, 1)
                elif c in NORMED:
                    act.wait_ge(hvar_ready, NORMED.index(c) + 1)
                    link(af(rt[:, 4, :], rt[:, 3, :], ACT.Ln))
                    af(rt[:, 4, :], rt[:, 4, :], ACT.Exp, scale=-0.5).then_inc(hguess_ready, 1)

            for j in range(12):
                c = ORDER1[j]
                act.wait_ge(group_done, GROUP["in1", j])
                free_item(j - 2)
                if c in NORMED:
                    af(ysq[:, j % 2, :], ps[:, j % 4, :], ACT.Square).then_inc(ysq_ready, 1)
                    g = gain[:, G_KN:G_KN + 1] if c == 4 else gain[:, G_QN:G_QN + 1]
                    af(y[:, j % 2, :], ps[:, j % 4, :], ACT.Copy, scale=g).then_inc(evac_act, 1)
                else:
                    af(y[:, j % 2, :], ps[:, j % 4, :], ACT.Copy).then_inc(evac_act, 1)
                if j % 2:
                    split(j // 2 + 2)
                if j:
                    finish(j - 1)
            finish(11)

            def copy_pt(s):
                kind, h, b, k0, k1 = STEPS[s]
                g = s // 4
                act.wait_ge(tr_done, s + 1)
                if g >= 2 and s % 4 == 0:
                    act.wait_ge(av_done, g - 1)
                n = k1 - k0
                af(PT[:, g % 2, k0:k1, b * P:(b + 1) * P],
                   ps[:, 3 + s % 2, 0:n * P].rearrange("p (b c) -> p b c", b=n), ACT.Copy).then_inc(pt_ready, 1)

            def copy_out(c):
                act.wait_ge(av_done, 2 * c + 2)
                af(OT[:, c, :], ps[:, 5 + c % 2, :], ACT.Copy).then_inc(ot_ready, 1)

            def square_group(nm, c0, j):
                act.wait_ge(ot_ready, c0 + j + 1)
                square(nm, j, OT[:, c0 + j, :])

            af(ident_r[:, :], ident[:, :], ACT.Copy).then_inc(masks_ready, 1)
            af(mask_r[:, :, :], c1[:, C_MASK:C_MASK + 2 * P].rearrange("p (m c) -> p m c", m=2), ACT.Copy
               ).then_inc(masks_ready, 1)
            for s, (kind, h, b, k0, k1) in enumerate(STEPS):
                w = (k1 - k0) * P + kind
                act.wait_ge(nmax_ready, s + 1)
                if s >= 3:
                    act.wait_ge(tr_done, s - 2)
                af(prob[:, s % 3, 0:w], ps[:, s % 3, 0:w], ACT.Exp, bias=nmax[:, s:s + 1],
                   accum_out=den[:, s:s + 1]).then_inc(exp_done, 1)
                if s >= 2:
                    copy_pt(s - 2)
                if s % 8 == 4 and s > 8:
                    copy_out(s // 8 - 1)
                if NORM_A_STEP <= s < NORM_A_STEP + 4:
                    square_group(n_group_a, 0, s - NORM_A_STEP)
                if s == NORM_A_STEP + 6:
                    guess(n_group_a)
                if NORM_A_STEP + 10 <= s < NORM_A_STEP + 14:
                    high_one(n_group_a, h_hi, s - (NORM_A_STEP + 10), 0)
            copy_pt(62)
            copy_pt(63)
            for j in range(3):
                square_group(n_group_b, 4, j)
            copy_out(7)
            square_group(n_group_b, 4, 3)
            guess(n_group_b)
            high(n_group_b, h_hi, 4)

            for j in range(KD):
                act.wait_ge(group_done, GROUP["out1", j])
                square(n_mix_post, j, ps[:, j % 4, :])
                af(F1[:, j, :], ps[:, j % 4, :], ACT.Copy).then_inc(evac_act, 1)
                if j % 2:
                    split(U_OUT1 + j // 2 + 2)
            guess(n_mix_post)
            for k in range(KD):
                act.wait_ge(x_new[0], k + 1)
                late_part(n_ffn_pre, "norm_ffn_pre", k)
            guess(n_ffn_pre)

            def ffn(phase, u_ff, mids0, nm):
                g0, a0, d0 = BASE[phase]

                def turn(i, last=False):
                    first = isinstance(i, int) and i == 0
                    for half in range(2):
                        if last:
                            split(u_ff + 2 * i + 2 + half)
                        else:
                            act.wait_ge(raw_landed[half], i * 16 + 16 * (u_ff // 2 + 2))
                            act.wait_ge(group_done, i * 4 + (g0 + 2 + 2 * half))
                            af(w_hi[half][:, :], w_raw[half][:, :], ACT.Copy).then_inc(hi_ready, 1)
                        if half:
                            continue
                        if first:
                            late_factors(nm)
                        for c in range(2):
                            act.wait_ge(evac_dve, i * 4 + (d0 + 1 + c))
                            af(sq[:, c, :], sq[:, c, :], ACT.Silu).then_inc(silu_ready, 1)
                        for c in range(2):
                            act.wait_ge(prod_ready, i * 2 + (mids0 + 1 + c))
                            af(mid_hi[:, bass.ds(i * 2 + c, 1), :] if not isinstance(i, int)
                               else mid_hi[:, 2 * i + c, :], hf[:, c, :], ACT.Copy).then_inc(prod_hi, 1)

                turn(0)
                with act.Fori(1, KF // 2 - 1) as i:
                    turn(i)
                turn(KF // 2 - 1, True)

            tables(SILU)
            ffn("ff1", U_FF1, 0, n_ffn_pre)
            tables(LN_EXP)

            def down_chunk(phase, u0, j, epilogue):
                act.wait_ge(group_done, GROUP[phase, j] - 1)
                split(u0 + 2 * j + 2)
                act.wait_ge(group_done, GROUP[phase, j])
                epilogue(j)
                split(u0 + 2 * j + 3)

            def down1(j):
                square(n_ffn_post, j, ps[:, j % 2, :])
                af(F[:, j, :], ps[:, j % 2, :], ACT.Copy).then_inc(evac_act, 1)

            for j in range(KD):
                down_chunk("down1", U_DOWN1, j, down1)
            act.dma_start(c2[:, 0:3 * P], consts[:, C_TRI:C_TRI + 3 * P]).then_inc(c2_landed, 16)
            act.dma_start(c2[:, 3 * P:], consts[:, C_INVC:C_INVC + 4 * PADW]).then_inc(c2_landed, 16)
            guess(n_ffn_post)
            for k in range(KD):
                act.wait_ge(x_new[0], KD + k + 1)
                late_part(n_mix2, "norm_mix_2", k)
            guess(n_mix2)

            def finish_vee(i):
                act.wait_ge(v2tr_done, i + 1)
                af(V2[:, :, i * P:(i + 1) * P], ps[:, 4 + i % 2, :].rearrange("p (b c) -> p b c", b=NB),
                   ACT.Copy).then_inc(v2_ready, 1)

            for u in range(8):
                split(U_IN2 + u + 2)
                if u == 0:
                    late_factors(n_mix2)
                for i in range(4):
                    if (9 + i) // 2 == u:
                        finish_vee(i)

            Z = ps[:, 4:7, :].rearrange("p b s -> p (b s)")[:, 0:1280]

            def copy_ob(c):
                act.wait_ge(av2_done, 2 * c + 2)
                af(OB[:, c, :], ps[:, 7, :], ACT.Copy).then_inc(ob_ready, 1)

            def pl_high(i):
                act.wait_ge(pooled, i + 1)
                af(pl_hi[:, i, :], UP[:, i, :], ACT.Copy).then_inc(pl_hi_ready, 1)

            for h in range(NH):
                act.wait_ge(z_done, h + 1)
                if h:
                    act.wait_ge(cum_done, h)
                link(af(E2[:, :], Z, ACT.Abs))
                link(af(E2[:, :], E2[:, :], ACT.Exp, scale=-1.0))
                af(E2[:, :], E2[:, :], ACT.Ln, bias=1.0).then_inc(ln_done, 1)
                if h == NH - 1:
                    for i in range(4):
                        pl_high(i)
                if h % 2 == 0 and h:
                    copy_ob(h // 2 - 1)
                act.wait_ge(cum_done, h + 1)
                if h >= 2:
                    act.wait_ge(av2_done, h - 1)
                af(A2[:, h % 2, :], Z, ACT.Exp).then_inc(a_done, 1)
                split(U_IN2 + 8 + h + 2)

            def yb_high(i):
                act.wait_ge(ob_ready, i + 1)
                act.wait_ge(group_done, GROUP["in2", 31])
                af(h_hi[:, 4 + i, :], OB[:, i, :], ACT.Copy).then_inc(yb_hi, 1)

            for j in range(4):
                act.wait_ge(group_done, GROUP["pool", j])
                if j >= 2:
                    act.wait_ge(ya_lo, j - 1)
                af(hf[:, j % 2, :], ps[:, j % 4, :], ACT.Copy, scale=gcol("pool_scale_2", j)
                   ).then_inc(evac_act, 1)
                act.wait_ge(evac_act, EVAC["pool", j][1])
                af(h_hi[:, j, :], hf[:, j % 2, :], ACT.Copy).then_inc(ya_hi, 1)
                if j % 2:
                    split(U_POOL + j // 2 + 2)
            copy_ob(3)
            for i in range(4):
                yb_high(i)
            tables(SIGMOID)
            act.wait_ge(evac_dve, EVAC["in2", 31][1])
            for j in range(0, KD, 2):
                af(GA[:, j:j + 2, :], GA[:, j:j + 2, :], ACT.Sigmoid).then_inc(sig_ready, 1)
            for j in range(0, KD, 2):
                af(GB[:, j:j + 2, :], GB[:, j:j + 2, :], ACT.Sigmoid).then_inc(sig_ready, 1)
            tables(LN_EXP)
            split(U_BRA + 2)
            split(U_BRA + 3)
            for j in range(KD):
                act.wait_ge(merged, j + 1)
                af(m_hi[:, j, :], GB[:, j, :], ACT.Copy).then_inc(m_hi_ready, 1)
                if j % 4 == 3:
                    split(U_BRB + j // 4 + 2)
            for j in range(KD):
                act.wait_ge(evac_dve, EVAC["out2", j][1])
                late_part(n_ffn2, "norm_ffn_2", j)
                if j % 2:
                    split(U_OUT2 + j // 2 + 2)
            guess(n_ffn2)
            tables(SILU)
            ffn("ff2", U_FF2, KF, n_ffn2)
            tables(LN_EXP)

            def down2(j):
                act.wait_ge(evac_dve, EVAC["down2", j][1])
                square(n_ple, j, X[:, j, :])

            for j in range(KD):
                down_chunk("down2", U_DOWN2, j, down2)
            guess(n_ple)
            for j in range(KD):
                act.wait_ge(group_done, GROUP["plep", j])
                af(PP[:, j, :], ps[:, j % 4, :], ACT.Copy).then_inc(evac_act, 1)
            tables(SIGMOID)
            high(n_ple, h_hi)
            split(U_PLEP + 2)
            for j in range(KD):
                act.wait_ge(group_done, GROUP["pleg", j])
                if j >= 2:
                    act.wait_ge(x_new[1], j - 1)
                af(hf[:, j % 2, :], ps[:, j % 4, :], ACT.Sigmoid).then_inc(evac_act, 1)
                if j % 2 and U_PLEG + j // 2 + 2 < N_UNITS:
                    split(U_PLEG + j // 2 + 2)
                if j:
                    act.wait_ge(x_new[1], j)
                    square(n_final, j - 1, X[:, j - 1, :])
            tables(LN_EXP)
            act.wait_ge(x_new[1], KD)
            square(n_final, KD - 1, X[:, KD - 1, :])
            guess(n_final)

        @block.vector
        def _(dve):
            n_self = [0]

            def mark(ins):
                n_self[0] += 1
                ins.then_inc(dve_self, 1)
                return n_self[0]

            def link(ins):
                dve.wait_ge(dve_self, mark(ins))

            def tt(out, a, b, op):
                return nc.vector.tensor_tensor(out, a, b, op)

            def ts(out, a, s1, op0, s2=None, op1=None):
                return (nc.vector.tensor_scalar(out, a, s1, s2, op0, op1) if op1 is not None
                        else nc.vector.tensor_scalar(out, a, s1, None, op0))

            def stt(out, a, s, b, op0, op1):
                return nc.vector.scalar_tensor_tensor(out=out, in0=a, scalar=s, in1=b, op0=op0, op1=op1)

            def low(out, full, hi):
                return tt(out, full, hi.bitcast(f32), ALU.subtract)

            def split(u):
                slot, width = u % 2, tiles_of(u)
                dve.wait_ge(hi_ready, u + 1)
                low(w_lo[slot][:, 0:width * P], w_raw[slot][:, 0:width * P], w_hi[slot][:, 0:width * P]
                    ).then_inc(lo_ready, 1)

            def refine(out, v, r0):
                link(stt(out, v, -0.5, r0, ALU.mult, ALU.mult))
                link(tt(out, out, r0, ALU.mult))
                return stt(out, out, 1.5, r0, ALU.add, ALU.mult)

            def variance(nm, width=D):
                dve.wait_ge(*nm.total(1))
                ts(stat[:, 0, :], ps[:, nm.ss_bank, 0:NB], 1.0 / width, ALU.mult, EPS, ALU.add
                   ).then_inc(nm.var.sem, 1)

            def factors(nm):
                dve.wait_ge(*nm.guess(1))
                link(refine(stat[:, 3, :], stat[:, 0, :], stat[:, 2, :]))
                for b in range(NB):
                    last = ts(diag[:, b, :], ident[:, :], stat[:, 3, b:b + 1], ALU.mult)
                last.then_inc(nm.diag.sem, 1)

            def apply_one(nm, src, name, dst_hi, dst_lo, k, n0):
                if k < nm.n:
                    if k == 0:
                        dve.wait_ge(*nm.factor(1))
                    if k >= 2:
                        dve.wait_ge(*nm.lo(k - 1))
                    stt(hf[:, k % 2, :], src[:, k, :], gcol(name, k), ps[:, nm.r_bank, :], ALU.mult, ALU.mult
                        ).then_inc(nm.f32.sem, 1)
                if k:
                    dve.wait_ge(*nm.hi(k))
                    low(dst_lo[:, n0 + k - 1, :], hf[:, (k - 1) % 2, :], dst_hi[:, n0 + k - 1, :]
                        ).then_inc(nm.lo.sem, 1)

            def apply(nm, src, name, dst_hi, dst_lo, n0=0):
                for k in range(nm.n + 1):
                    apply_one(nm, src, name, dst_hi, dst_lo, k, n0)

            def late_low(nm, name, k):
                dve.wait_ge(*nm.hi(k + 1))
                stt(h_lo[:, k, :], X[:, k, :], gcol(name, k), h_hi[:, k, :].bitcast(f32), ALU.mult, ALU.subtract
                    ).then_inc(nm.lo.sem, 1)

            def scaled(bank, out, scale=None):
                if scale is None:
                    return tt(out, bank, factors_sb[:, :], ALU.mult)
                return stt(out, bank, scale, factors_sb[:, :], ALU.mult, ALU.mult)

            def apply_post(nm, f, name, added, late, late_name):
                dve.wait_ge(*nm.factor(1))
                for k in range(KD + 2):
                    if k < KD:
                        if k >= 2:
                            dve.wait_ge(x_new[0], added + k - 1)
                        stt(hf[:, k % 2, :], f[:, k, :], gcol(name, k), ps[:, R_BANK, :], ALU.mult, ALU.mult
                            ).then_inc(nm.f32.sem, 1)
                    if 1 <= k <= KD:
                        dve.wait_ge(*nm.f32(k))
                        tt(X[:, k - 1, :], X[:, k - 1, :], hf[:, (k - 1) % 2, :], ALU.add).then_inc(x_new[0], 1)
                    if k >= 2:
                        late_low(late, late_name, k - 2)

            dve.wait_ge(p_hi_ready, 1)
            low(p_lo[:, :, :], hf[:, :, :], p_hi[:, :, :]).then_inc(p_lo_ready, 1)
            dve.wait_ge(c0_landed, 32)
            dve.wait_ge(gain_landed, 16)
            variance(n_mix_pre)
            factors(n_mix_pre)
            split(0)
            split(1)
            apply(n_mix_pre, X, "norm_mix_pre", h_hi, h_lo)
            dve.wait_ge(c1_landed, 16)

            def rope(j):
                c = ORDER1[j]
                if c in V1:
                    return
                normed, key = c in NORMED, c in (4, 10)
                cos, sin = (C_COSA, C_SINA) if normed else (C_COSB, C_SINB)
                scale = 1.0 if normed or key else SCALE
                i_roped = ROPED.index(c)
                if i_roped:
                    dve.wait_ge(rope_done, i_roped)
                dve.wait_ge(rot_done, i_roped + 1)
                stt(rt[:, 0, :], y[:, j % 2, :], scale, c1[:, cos:cos + S], ALU.mult, ALU.mult)
                m = mark(stt(rt[:, 1, :], ps[:, 4 + j % 2, :], scale, c1[:, sin:sin + S], ALU.mult, ALU.mult))
                if normed:
                    dve.wait_ge(hsum_done, NORMED.index(c) + 1)
                    ts(rt[:, 3, :], ps[:, 6 + j % 2, :], 1.0 / HD, ALU.mult, EPS, ALU.add).then_inc(hvar_ready, 1)
                dve.wait_ge(dve_self, m)
                if normed:
                    link(tt(rt[:, 2, :], rt[:, 0, :], rt[:, 1, :], ALU.add))
                    dve.wait_ge(hguess_ready, NORMED.index(c) + 1)
                    link(refine(rt[:, 5, :], rt[:, 3, :], rt[:, 4, :]))
                if not key:
                    if normed:
                        last = stt(QA[:, c, :], rt[:, 2, :], SCALE, rt[:, 5, :], ALU.mult, ALU.mult)
                    else:
                        last = tt(QB[:, c - 6, :], rt[:, 0, :], rt[:, 1, :], ALU.add)
                else:
                    for kv in range(2):
                        for half in range(2):
                            i = slice(HD * kv, HD * kv + HD)
                            o = slice(HD * half, HD * half + HD)
                            if normed:
                                last = tt(KDA[o, kv, :], rt[i, 2, :], rt[i, 5, :], ALU.mult)
                            else:
                                last = tt(KDB[o, kv, :], rt[i, 0, :], rt[i, 1, :], ALU.add)
                last.then_inc(rope_done, 1)

            for u in range(UNITS_IN1):
                if u:
                    rope(2 * u - 1)
                split(u + 2)
                rope(2 * u)
            rope(11)

            def negmax(s):
                if s >= 64:
                    return
                kind, h, b, k0, k1 = STEPS[s]
                dve.wait_ge(s_done, s + 1)
                nc.vector.tensor_reduce(nmax[:, s:s + 1], ps[:, s % 3, 0:(k1 - k0) * P + kind], AX.X, ALU.max,
                                        negate=True).then_inc(nmax_ready, 1)

            negmax(0)
            negmax(1)
            for s, (kind, h, b, k0, k1) in enumerate(STEPS):
                w = (k1 - k0) * P
                dve.wait_ge(exp_done, s + 1)
                link(nc.vector.reciprocal(rden[:, s:s + 1], den[:, s:s + 1]))
                ts(prob[:, s % 3, 0:w], prob[:, s % 3, 0:w], rden[:, s:s + 1], ALU.mult).then_inc(pn_ready, 1)
                negmax(s + 2)
                if s == NORM_A_STEP + 5:
                    variance(n_group_a, 4 * P)
                if s == NORM_A_STEP + 7:
                    factors(n_group_a)
                if NORM_A_STEP + 9 <= s < NORM_A_STEP + 14:
                    apply_one(n_group_a, OT[:, 0:4, :], "group_norm_a", h_hi, h_lo, s - (NORM_A_STEP + 9), 0)

            variance(n_group_b, 4 * P)
            factors(n_group_b)
            apply(n_group_b, OT[:, 4:8, :], "group_norm_b", h_hi, h_lo, 4)
            for u in range(UNITS_OUT1):
                split(U_OUT1 + u + 2)
            variance(n_mix_post)
            factors(n_mix_post)
            apply_post(n_mix_post, F1, "norm_mix_post", 0, n_ffn_pre, "norm_ffn_pre")

            def ffn(phase, u_ff, mids0, nm):
                g0, a0, d0 = BASE[phase]

                variance(nm)
                factors(nm)

                def turn(i, last=False):
                    first = isinstance(i, int) and i == 0
                    for half in range(2):
                        if last:
                            split(u_ff + 2 * i + 2 + half)
                        else:
                            dve.wait_ge(hi_ready, i * 2 + (u_ff + 3 + half))
                            low(w_lo[half][:, :], w_raw[half][:, :], w_hi[half][:, :]).then_inc(lo_ready, 1)
                        if half:
                            continue
                        if first:
                            dve.wait_ge(*nm.f32(1))
                        for c in range(2):
                            dve.wait_ge(group_done, i * 4 + (g0 + 1 + c))
                            if not first:
                                dve.wait_ge(prod_ready, i * 2 + (mids0 - 1 + c))
                            scaled(ps[:, c, :], sq[:, c, :]).then_inc(evac_dve, 1)
                        for c in range(2):
                            dve.wait_ge(group_done, i * 4 + (g0 + 3 + c))
                            if not first:
                                dve.wait_ge(prod_lo, i * 2 + (mids0 - 1 + c))
                            scaled(ps[:, 2 + c, :], hf[:, c, :]).then_inc(evac_dve, 1)
                            dve.wait_ge(silu_ready, i * 2 + (mids0 + 1 + c))
                            dve.wait_ge(evac_dve, i * 4 + (d0 + 3 + c))
                            tt(hf[:, c, :], hf[:, c, :], sq[:, c, :], ALU.mult).then_inc(prod_ready, 1)
                        for c in range(2):
                            dve.wait_ge(prod_hi, i * 2 + (mids0 + 1 + c))
                            at = 2 * i + c if isinstance(i, int) else bass.ds(i * 2 + c, 1)
                            low(mid_lo[:, at, :], hf[:, c, :], mid_hi[:, at, :]).then_inc(prod_lo, 1)

                turn(0)
                with dve.Fori(1, KF // 2 - 1) as i:
                    turn(i)
                turn(KF // 2 - 1, True)

            ffn("ff1", U_FF1, 0, n_ffn_pre)
            for u in range(UNITS_DOWN):
                split(U_DOWN1 + u + 2)
            variance(n_ffn_post)
            factors(n_ffn_post)
            apply_post(n_ffn_post, F, "norm_ffn_post", KD, n_mix2, "norm_mix_2")
            variance(n_mix2)
            factors(n_mix2)

            def chunk2(j):
                dve.wait_ge(group_done, GROUP["in2", j])
                if 10 <= j < 12:
                    dve.wait_ge(v2tr_done, j - 9)
                dst = (K2[:, j, :] if j < 4 else Q2[:, j - 4, :] if j < 8 else hf[:, j % 2, :] if j < 12 else
                       UP[:, j - 12, :] if j < 16 else (GA if j < 24 else GB)[:, j % 8, :])
                scaled(ps[:, j % 4, :], dst, SCALE if 4 <= j < 8 else None).then_inc(evac_dve, 1)

            for u in range(8):
                split(U_IN2 + u + 2)
                if u == 0:
                    dve.wait_ge(*n_mix2.f32(1))
                chunk2(2 * u)
                chunk2(2 * u + 1)

            def pool_group(g):
                w, u = POOL_WINDOWS[g], UP[:, g, :]
                src, step, n = u, 1, 0
                if g:
                    dve.wait_ge(pooled, g)
                while step < w:
                    dst = hf[:, n % 2, :]
                    nc.vector.tensor_copy(dst[:, 0:step], src[:, 0:step])
                    link(tt(dst[:, step:S], src[:, step:S], src[:, 0:S - step], ALU.add))
                    src, step, n = dst, 2 * step, n + 1
                tmp = hf[:, n % 2, 0:PADW]
                link(tt(tmp, src[:, 0:PADW], c2[:, 3 * P + g * PADW:3 * P + (g + 1) * PADW], ALU.mult))
                tt(u[:, 0:PADW], tmp, u[:, 0:PADW], ALU.subtract)
                stt(u[:, PADW:S], src[:, PADW:S], 1.0 / w, u[:, PADW:S], ALU.mult, ALU.subtract
                    ).then_inc(pooled, 1)

            dve.wait_ge(evac_dve, EVAC["in2", 15][1])
            dve.wait_ge(v2tr_done, 4)
            dve.wait_ge(c2_landed, 32)
            Z = ps[:, 4:7, :].rearrange("p b s -> p (b s)")[:, 0:1280]
            for h in range(NH):
                dve.wait_ge(ln_done, h + 1)
                stt(E2[:, :], Z, 0.0, E2[:, :], ALU.max, ALU.add).then_inc(sp_ready, 1)
                if h < 4:
                    pool_group(h)
                if h == NH - 1:
                    for i in range(4):
                        dve.wait_ge(pl_hi_ready, i + 1)
                        low(pl_lo[:, i, :], UP[:, i, :], pl_hi[:, i, :]).then_inc(pl_lo_ready, 1)
                chunk2(16 + 2 * h)
                chunk2(17 + 2 * h)
                split(U_IN2 + 8 + h + 2)

            for j in range(4):
                dve.wait_ge(ya_hi, j + 1)
                low(h_lo[:, j, :], hf[:, j % 2, :], h_hi[:, j, :]).then_inc(ya_lo, 1)
                if j % 2:
                    split(U_POOL + j // 2 + 2)
            for i in range(4):
                dve.wait_ge(yb_hi, i + 1)
                low(h_lo[:, 4 + i, :], OB[:, i, :], h_hi[:, 4 + i, :]).then_inc(yb_lo, 1)
            for j in range(KD):
                dve.wait_ge(sig_ready, j // 2 + 1)
                dve.wait_ge(group_done, GROUP["bra", j])
                tt(GA[:, j, :], GA[:, j, :], ps[:, j % 4, :], ALU.mult).then_inc(evac_dve, 1)
                if j % 4 == 3:
                    split(U_BRA + j // 4 + 2)
            for j in range(KD):
                dve.wait_ge(sig_ready, 4 + j // 2 + 1)
                dve.wait_ge(group_done, GROUP["brb", j])
                tt(GB[:, j, :], GB[:, j, :], ps[:, j % 4, :], ALU.mult).then_inc(evac_dve, 1)
                dve.wait_ge(evac_dve, EVAC["brb", j][1])
                tt(GB[:, j, :], GB[:, j, :], GA[:, j, :], ALU.add).then_inc(merged, 1)
                dve.wait_ge(m_hi_ready, j + 1)
                low(m_lo[:, j, :], GB[:, j, :], m_hi[:, j, :]).then_inc(m_lo_ready, 1)
                if j % 4 == 3:
                    split(U_BRB + j // 4 + 2)
            for j in range(KD):
                dve.wait_ge(group_done, GROUP["out2", j])
                tt(X[:, j, :], X[:, j, :], ps[:, j % 4, :], ALU.add).then_inc(evac_dve, 1)
                if j:
                    late_low(n_ffn2, "norm_ffn_2", j - 1)
                if j % 2:
                    split(U_OUT2 + j // 2 + 2)
            late_low(n_ffn2, "norm_ffn_2", KD - 1)
            ffn("ff2", U_FF2, KF, n_ffn2)
            for j in range(KD):
                split(U_DOWN2 + 2 * j + 2)
                dve.wait_ge(group_done, GROUP["down2", j])
                tt(X[:, j, :], X[:, j, :], ps[:, j % 2, :], ALU.add).then_inc(evac_dve, 1)
                split(U_DOWN2 + 2 * j + 3)
            variance(n_ple)
            factors(n_ple)
            apply(n_ple, X, "norm_ple_2", h_hi, h_lo)
            split(U_PLEP + 2)
            for j in range(KD):
                dve.wait_ge(evac_act, EVAC["pleg", j][1])
                link(tt(hf[:, j % 2, :], hf[:, j % 2, :], PP[:, j, :], ALU.mult))
                tt(X[:, j, :], X[:, j, :], hf[:, j % 2, :], ALU.add).then_inc(x_new[1], 1)
                if j % 2 and U_PLEG + j // 2 + 2 < N_UNITS:
                    split(U_PLEG + j // 2 + 2)
            variance(n_final)
            factors(n_final)
            dve.wait_ge(*n_final.factor(1))
            for k in range(KD):
                stt(OUT[:, k, :], X[:, k, :], gcol("norm_final_2", k), ps[:, R_BANK, :], ALU.mult, ALU.mult
                    ).then_inc(out_ready, 1)


def constants():
    import numpy as np

    c = np.zeros((P, C_COLS), np.float32)
    i = np.arange(P)
    c[:, C_ID:C_ID + P] = np.eye(P)
    c[:, C_ONE:C_ONE + P] = 1.0
    c[:, C_HONE:C_HONE + P] = i[:, None] // HD == i[None, :] // HD
    half = HD // 2
    for m in range(P):
        if m % HD < half:
            c[m + half, C_ROT + m] = -1.0
        else:
            c[m - half, C_ROT + m] = 1.0
    c[:, C_TRI:C_TRI + P] = np.where(i[:, None] >= i[None, :], -1.0, 0.0)
    c[:, C_NEG1:C_NEG1 + P] = -1.0
    c[:, C_SMASK:C_SMASK + P] = np.where(i[:, None] >= i[None, :], NEG, 0.0)
    c[:, C_MASK:C_MASK + P] = np.where(i[None, :] >= i[:, None], 0.0, NEG)
    c[:, C_MASK + P:C_MASK + 2 * P] = np.where(i[None, :] <= i[:, None], 0.0, NEG)
    t = np.arange(S, dtype=np.float32)
    row, col = np.floor(t / 64).astype(np.float32), (t % 64).astype(np.float32)
    quarter = HD // 4
    f_ax = np.float32(10000.0) ** (-np.arange(quarter, dtype=np.float32) / np.float32(quarter))
    f_1d = np.float32(10000.0) ** (-np.arange(half, dtype=np.float32) / np.float32(half))
    ang_a = np.concatenate([row[None, :] * f_ax[:, None], col[None, :] * f_ax[:, None]])
    ang_b = t[None, :] * f_1d[:, None]
    for ang, cos, sin in ((ang_a, C_COSA, C_SINA), (ang_b, C_COSB, C_SINB)):
        ang = np.concatenate([ang.astype(np.float32)] * 4).astype(np.float64)
        c[:, cos:cos + S], c[:, sin:sin + S] = np.cos(ang), np.sin(ang)
    for g, w in enumerate(POOL_WINDOWS):
        c[:, C_INVC + g * PADW:C_INVC + (g + 1) * PADW] = 1.0 / np.minimum(np.arange(PADW) + 1.0, w)
    return c


def tiles(w, order=None):
    k, n = w.shape
    t = w.reshape(k // P, P, n // P, P).transpose(2, 0, 1, 3)
    return t if order is None else t[order]


def pack(ts, per):
    import numpy as np

    ts = ts.reshape(-1, per, P, P).transpose(0, 2, 1, 3).reshape(-1, P, per * P)
    return np.pad(ts, ((0, 0), (0, 0), (0, RAW - per * P)))


def pack_pairs(a, b):
    import numpy as np

    return np.stack([pack(tiles(a), 16), pack(tiles(b), 16)], 1).reshape(-1, P, RAW)


def kernel(**inputs):
    import numpy as np
    import concourse.bacc as bacc
    from concourse import mybir
    from concourse.bass_utils import run_bass_kernel_spmd

    a = {n: np.asarray(v) for n, v in inputs.items()}
    weights = np.concatenate([
        pack(tiles(a["w_in"][0], ORDER1), 16),
        pack(tiles(a["w_out"][0]), 16),
        pack_pairs(a["w_gate"][0], a["w_up"][0]),
        pack(tiles(a["w_down"][0]), DOWN_TILES),
        pack(tiles(a["w_in_2"][0], ORDER2), 16),
        pack(a["w_pool_2"][0], 2),
        pack(tiles(a["w_branch_a_2"][0]), 16),
        pack(tiles(a["w_branch_b_2"][0]), 16),
        pack(tiles(a["w_out_2"][0]), 16),
        pack_pairs(a["w_ffn_gate_2"][0], a["w_ffn_up_2"][0]),
        pack(tiles(a["w_ffn_down_2"][0]), DOWN_TILES),
        pack(tiles(a["w_ple_proj_2"][0]), 16),
        pack(tiles(a["w_ple_gate_2"][0]), 16),
    ])
    cols = [a[n].reshape(-1, P).T for n in GAINS]
    cols += [np.concatenate([a[n].reshape(-1)] * 2)[:, None] for n in ("q_norm_a", "k_norm_a")]
    cols.append(np.broadcast_to(a["sink_b"].reshape(1, NH), (P, NH)))
    arrays = {
        "x_t": np.ascontiguousarray(a["x"][0].T),
        "p_t": np.ascontiguousarray(a["p_2"][0, 0].T),
        "weights": np.ascontiguousarray(weights),
        "gains": np.ascontiguousarray(np.concatenate(cols, 1)),
        "constants": constants(),
    }
    nc = bacc.Bacc("TRN2", target_bir_lowering=False, num_devices=1)
    args = [nc.dram_tensor(n, v.shape, mybir.dt.from_np(v.dtype), kind="ExternalInput").ap()
            for n, v in arrays.items()]
    args.append(nc.dram_tensor("out_t", (D, S), mybir.dt.float32, kind="ExternalOutput").ap())
    build(nc, *args)
    r = run_bass_kernel_spmd(nc, [arrays], core_ids=[0])
    return r.results[0]["out_t"].T.reshape(1, S, D)
```

```python
D = 1024
S = 512
P = 128
KD = D // P
FF = 2816
KF = FF // P
HD = 64
NH = 8
NB = S // P
EPS = 1e-6
SCALE = HD ** -0.5
POOL_WINDOWS = (2, 4, 8, 16)
PADW = 16
RAW = 2048
NEG = -3.0e38

DOWN_TILES = KF // 2
UNITS_IN1, UNITS_OUT1 = 6, 4
UNITS_FF, UNITS_DOWN = 2 * (KF // 2), 2 * KD
UNITS_IN2, UNITS_POOL, UNITS_BRANCH, UNITS_OUT2 = 16, 2, 2, 4
U_IN1 = 0
U_OUT1 = U_IN1 + UNITS_IN1
U_FF1 = U_OUT1 + UNITS_OUT1
U_DOWN1 = U_FF1 + UNITS_FF
U_IN2 = U_DOWN1 + UNITS_DOWN
U_POOL = U_IN2 + UNITS_IN2
U_BRA = U_POOL + UNITS_POOL
U_BRB = U_BRA + UNITS_BRANCH
U_OUT2 = U_BRB + UNITS_BRANCH
U_FF2 = U_OUT2 + UNITS_OUT2
U_DOWN2 = U_FF2 + UNITS_FF
U_PLEP = U_DOWN2 + UNITS_DOWN
U_PLEG = U_PLEP + 1
N_UNITS = U_PLEG + 4

NORM_A_STEP = 38

LN_EXP, SILU, SIGMOID = "natural_log_exp_and_others", "silu_and_others", "sigmoid_and_others"

GAINS = ["norm_mix_pre", "norm_mix_post", "norm_ffn_pre", "norm_ffn_post", "norm_mix_2", "norm_ffn_2",
         "norm_ple_2", "norm_final_2", "group_norm_a", "group_norm_b", "pool_scale_2"]
GAIN_W = [KD] * 8 + [4] * 3
GAIN_AT = {n: sum(GAIN_W[:i]) for i, n in enumerate(GAINS)}
G_QN = sum(GAIN_W)
G_KN = G_QN + 1
G_QROT, G_KROT = G_QN + 2, G_QN + 3
G_SINK = G_QN + 4
G_COLS = G_SINK + NH

C_ID, C_ONE, C_TRI, C_NEG1, C_SMASK = (P * i for i in range(5))
C_INVC = 5 * P
C1_AT = C_INVC + 4 * PADW
C_HONE, C_ROT, C_MASK = C1_AT, C1_AT + P, C1_AT + 2 * P
C_COSA, C_SINA, C_COSB, C_SINB = (C1_AT + 4 * P + S * i for i in range(4))
C_COLS = C_SINB + S


ORDER1 = [5, 4, 0, 10, 1, 6, 2, 7, 3, 8, 9, 11]
V1 = [5, 11]
NORMED = [4, 0, 1, 2, 3]
ROPED = [c for c in ORDER1 if c not in V1]
ORDER2 = [*range(8, 12), *range(4, 8), *range(12, 16), *range(0, 4), *range(16, 32)]
STEPS = [(0, h, b, 0, NB) for h in range(NH) for b in range(NB)] + [
    (1, h, b, max(b - 1, 0), min(b + 2, NB)) for h in range(NH) for b in range(NB)]


def build(nc, xT, pT, weights, gains, consts, outT):
    import concourse.bass as bass
    from concourse import mybir
    from contextlib import ExitStack

    f32, f32r = mybir.dt.float32, mybir.dt.float32r
    ACT = mybir.ActivationFunctionType
    ALU = mybir.AluOpType
    AX = mybir.AxisListType

    ctx = ExitStack()
    with ctx:
        def sb(name, shape, dt=f32, stack=ctx):
            return stack.enter_context(nc.sbuf_tensor(name, shape, dt))

        def sem(name):
            return ctx.enter_context(nc.semaphore(name))

        X = sb("X", [P, KD, S])
        w_raw = [sb(f"w_raw{i}", [P, RAW]) for i in range(2)]
        w_hi = [sb(f"w_hi{i}", [P, RAW], f32r) for i in range(2)]
        w_lo = [sb(f"w_lo{i}", [P, RAW], f32r) for i in range(2)]
        p_hi = sb("p_hi", [P, 2, S], f32r)
        p_lo = sb("p_lo", [P, 2, S], f32r)
        ident = sb("ident", [P, P])
        ones = sb("ones", [P, P])
        gain = sb("gain", [P, G_COLS])
        sq = sb("sq", [P, 2, S])
        hf = sb("hf", [P, 2, S])
        sqsum = sb("sqsum", [P, S])
        with ExitStack() as shared:
            diag = sb("diag", [P, NB, P], stack=shared)
        factors_sb = sb("factors_sb", [P, S])
        stat = sb("stat", [P, 5, NB])

        with ExitStack() as lowpart:
            h_lo = sb("h_lo", [P, KD, S], f32r, lowpart)
        F = sb("F", [P, KD, S])
        with ExitStack() as highpart:
            OT = sb("OT", [P, 8, S], stack=highpart)
        h_hi = sb("h_hi", [P, KD, S], f32r)

        with ExitStack() as st:
            with ExitStack() as st2:
                F1 = sb("F1", [P, KD, S], stack=st2)
            QA = sb("QA", [P, NH, S], f32r, st)
            QB = sb("QB", [P, NH, S], f32r, st)
            KA = sb("KA", [P, 2, 2, S], f32r, st)
            KB = sb("KB", [P, 2, 2, S], f32r, st)
            VA = sb("VA", [P, NB, P], stack=st)
            VB = sb("VB", [P, NB, P], stack=st)
            with ExitStack() as st2:
                c1 = sb("c1", [P, C_COLS - C1_AT], stack=st2)
            sb("c1_head", [P, C_COSA - C1_AT], stack=st)
            with ExitStack() as st2:
                prob = sb("prob", [P, 3, S], stack=st2)
            sb("c1_tables", [P, 4 * S], stack=st)
            with ExitStack() as st2:
                PT = sb("PT", [P, 2, NB, S], stack=st2)
            y = sb("y", [P, 3, S], stack=st)
            ysq = sb("ysq", [P, 2, S], stack=st)
            rt = sb("rt", [P, 5, S], stack=st)
            ident_r = sb("ident_r", [P, P], f32r, st)
            mask_r = sb("mask_r", [P, 2, P], f32r, st)
            nmax = sb("nmax", [P, 64], stack=st)
            den = sb("den", [P, 64], stack=st)
            rden = sb("rden", [P, 64], stack=st)
        with ExitStack() as st:
            mid_hi = sb("mid_hi", [P, KF, S], f32r, st)
            mid_lo = sb("mid_lo", [P, KF, S], f32r, st)
        with ExitStack() as st:
            with ExitStack() as st2:
                Q2 = sb("Q2", [P, 4, S], stack=st2)
                K2 = sb("K2", [P, 4, S], stack=st2)
                V2 = sb("V2", [P, NB, S], stack=st2)
                with ExitStack() as st3:
                    E2 = sb("E2", [P, 1280], stack=st3)
                E2_lo = sb("E2_lo", [P, 1280], f32r, st2)
                E2_hi = sb("E2_hi", [P, 1280], f32r, st2)
                A2 = sb("A2", [P, 1280], stack=st2)
            with ExitStack() as st2:
                pl_hi = sb("pl_hi", [P, 4, S], f32r, st2)
                pl_lo = sb("pl_lo", [P, 4, S], f32r, st2)
            with ExitStack() as st2:
                m_hi = sb("m_hi", [P, KD, S], f32r, st2)
                m_lo = sb("m_lo", [P, KD, S], f32r, st2)
            sb("mixer_room", [P, 3 * 4 * S + 3 * 1280], stack=st)
            GA = sb("GA", [P, KD, S], stack=st)
            GB = sb("GB", [P, KD, S], stack=st)
            UP = sb("UP", [P, 4, S], stack=st)
            OB = sb("OB", [P, 4, S], stack=st)
            inv_count = sb("inv_count", [P, 4 * PADW], stack=st)
            c2 = sb("c2", [P, 4 * P], f32r, st)
        with ExitStack() as st:
            PP = sb("PP", [P, KD, S], stack=st)
            OUT = sb("OUT", [P, KD, S], stack=st)

        ps = ctx.enter_context(nc.psum_tensor("ps", [P, 8, S], f32))
        R_BANK, SS_BANK = 4, 5
        GROUP_A_BANK = 7

        raw_landed = [sem(f"raw_landed{i}") for i in range(2)]
        hi_ready, lo_ready = sem("hi_ready"), sem("lo_ready")
        group_done = sem("group_done")
        evac_act, evac_dve = sem("evac_act"), sem("evac_dve")
        x_landed = [sem(f"x_landed{i}") for i in range(4)]
        gain_landed, c0_landed, c1_landed, c2_landed, p_landed = (
            sem(n) for n in ("gain_landed", "c0_landed", "c1_landed", "c2_landed", "p_landed"))
        p_hi_ready, p_lo_ready = sem("p_hi_ready"), sem("p_lo_ready")
        dve_self, act_self, pool_self = sem("dve_self"), sem("act_self"), sem("pool_self")
        ysq_ready, rot_done, hsum_done, hvar_ready, hguess_ready, rope_done, v_ready = (
            sem(n) for n in ("ysq_ready", "rot_done", "hsum_done", "hvar_ready", "hguess_ready", "rope_done",
                             "v_ready"))
        vtr_done, roped, roped_hi = sem("vtr_done"), sem("roped"), sem("roped_hi")
        masks_ready, s_done, nmax_ready, exp_done, pn_ready, tr_done, pt_ready, av_done, ot_ready = (
            sem(n) for n in ("masks_ready", "scores_done", "negmax_ready", "exp_done", "prob_normed", "transposed",
                             "pt_ready", "av_done", "ot_ready"))
        z_done, ln_done, sp_ready, sp_masked, cum_done, a_done, av2_done, ob_ready = (
            sem(n) for n in ("z_done", "ln_done", "sp_ready", "sp_masked", "cum_done", "a_done", "av2_done", "ob_ready"))
        c2_ready, sp_hi, sp_lo = sem("c2_ready"), sem("sp_hi"), sem("sp_lo")
        v2tr_done, v2_ready = sem("v2tr_done"), sem("v2_ready")
        pooled, pl_hi_ready, pl_lo_ready = sem("pooled"), sem("pl_hi_ready"), sem("pl_lo_ready")
        ya_ready, ya_hi, ya_lo, yb_hi, yb_lo = (sem(n) for n in ("ya_ready", "ya_hi", "ya_lo", "yb_hi", "yb_lo"))
        sig_ready, merged, m_hi_ready, m_lo_ready = (sem(n) for n in ("sig_ready", "merged", "m_hi_ready", "m_lo_ready"))
        x_new = [sem(f"x_new{i}") for i in range(3)]
        silu_ready, prod_ready, prod_hi, prod_lo = (
            sem(n) for n in ("silu_ready", "prod_ready", "prod_hi_ready", "prod_lo_ready"))
        out_ready, out_stored = sem("out_ready"), sem("out_stored")

        class Count:

            def __init__(self, sem, base=0):
                self.sem, self.base = sem, base

            def __call__(self, n):
                return self.sem, self.base + n

        NORM_EVENTS = ("squares",
                       "summed",
                       "total",
                       "var",
                       "guess",
                       "diag",
                       "factor",
                       "f32",
                       "hi",
                       "lo")
        norm_sems = {e: sem("norm_" + e) for e in NORM_EVENTS}
        norm_counts = dict.fromkeys(NORM_EVENTS, 0)

        class Norm:

            def __init__(self, n, kind, before):
                self.n, self.before = n, before
                self.r_bank, self.ss_bank = R_BANK, SS_BANK
                (self.squares, self.summed, self.total, self.var, self.guess, self.diag, self.factor, self.f32,
                 self.hi, self.lo) = (Count(norm_sems[e], norm_counts[e]) for e in NORM_EVENTS)
                n_f32 = {"split": n, "late": 1, "added": n, "final": 0}[kind]
                self.factor_used = self.f32(n_f32)
                for e in NORM_EVENTS:
                    norm_counts[e] += (n if e in ("squares", "summed") else n_f32 if e == "f32" else
                                       (n if kind in ("split", "late") else 0) if e in ("hi", "lo") else 1)

        norms = []
        for n, kind in ((KD, "late"), (4, "split"), (4, "split"), (KD, "added"), (KD, "late"), (KD, "added"),
                        (KD, "late"), (KD, "late"), (KD, "split"), (KD, "final")):
            norms.append(Norm(n, kind, norms[-1] if norms else None))
        (n_mix_pre, n_group_a, n_group_b, n_mix_post, n_ffn_pre, n_ffn_post, n_mix2, n_ffn2, n_ple,
         n_final) = norms
        n_group_a.r_bank = n_group_a.ss_bank = GROUP_A_BANK

        PHASES = [("in1", 12, "D", 4, 1), ("out1", KD, "A", 4, 1), ("ff1", 2 * KF, "D", 4, 1),
                  ("down1", KD, "A", 2, 2), ("in2", 32, "D", 4, 1), ("pool", 4, "A", 4, 1),
                  ("bra", KD, "D", 4, 1), ("brb", KD, "D", 4, 1), ("out2", KD, "D", 4, 1),
                  ("ff2", 2 * KF, "D", 4, 1), ("down2", KD, "D", 2, 2), ("plep", KD, "A", 4, 1),
                  ("pleg", KD, "A", 4, 1)]
        GROUP, EVAC, BEFORE, BASE = {}, {}, {}, {}
        counts, groups, users = {"A": 0, "D": 0}, 0, {}
        for phase, n, engines, banks, parts in PHASES:
            BASE[phase] = (groups, counts["A"], counts["D"])
            for j in range(n):
                e = engines[j % len(engines)]
                groups += parts
                counts[e] += 1
                GROUP[phase, j] = groups
                EVAC[phase, j] = (e, counts[e])
                BEFORE[phase, j] = users.get(j % banks)
                users[j % banks] = (e, counts[e])

        USED = []
        for phase, n, engines, banks, parts in PHASES:
            per = {"pool": 2, "bra": 4, "brb": 4, "plep": 8}.get(phase, 2)
            if parts == 2:
                USED += [g for j in range(n) for g in (GROUP[phase, j] - 1, GROUP[phase, j])]
            else:
                USED += [GROUP[phase, j + per - 1] for j in range(0, n, per)]
        assert len(USED) == N_UNITS

        block = ctx.enter_context(nc.Block())

        def gcol(name, k):
            c = GAIN_AT[name] + k
            return gain[:, c:c + 1]

        def tiles_of(u):
            if U_DOWN1 <= u < U_IN2 or U_DOWN2 <= u < U_PLEP:
                return DOWN_TILES
            return 2 if U_POOL <= u < U_BRA else 16

        @block.sync
        def _(sp):
            def load(u, slot, width, first=False):
                if not first:
                    sp.wait_ge(lo_ready, u - 1)
                sp.dma_start(w_raw[slot][:, 0:width * P], weights[bass.ds(u, 1), :, 0:width * P]
                             if not isinstance(u, int) else weights[u, :, 0:width * P]
                             ).then_inc(raw_landed[slot], 16)

            for i in range(4):
                sp.dma_start(X[:, 2 * i:2 * i + 2, :],
                             xT[i * 2 * P:(i + 1) * 2 * P, :].rearrange("(k p) s -> p k s", p=P)
                             ).then_inc(x_landed[i], 16)
                if i == 0:
                    load(0, 0, 16, True)
            load(1, 1, 16, True)

            def run(start, n):
                with sp.Fori(0, n // 2) as i:
                    for slot in range(2):
                        u = i * 2 + (start + slot)
                        sp.wait_ge(lo_ready, u - 1)
                        sp.dma_start(w_raw[slot][:, 0:tiles_of(start) * P],
                                     weights[bass.ds(u, 1), :, 0:tiles_of(start) * P]
                                     ).then_inc(raw_landed[slot], 16)

            run(2, U_DOWN1 - 2)
            run(U_DOWN1, UNITS_DOWN)
            run(U_IN2, UNITS_IN2)
            run(U_POOL, UNITS_POOL)
            run(U_BRA, U_DOWN2 - U_BRA)
            run(U_DOWN2, UNITS_DOWN)
            for u in range(U_PLEP, N_UNITS):
                load(u, u % 2, 16)
            for k in range(KD):
                sp.wait_ge(out_ready, k + 1)
                sp.dma_start(outT[k * P:(k + 1) * P, :], OUT[:, k, :]).then_inc(out_stored, 16)
            sp.wait_ge(out_stored, 16 * KD)

        @block.gpsimd
        def _(pool):
            def sum_squares(nm):
                if nm.before is not None:
                    pool.wait_ge(*nm.before.total(1))
                nc.gpsimd.memset(sqsum[:, :], 0.0).then_inc(nm.summed.sem, 1)
                for j in range(nm.n - 1):
                    pool.wait_ge(*nm.squares(j + 1))
                    pool.wait_ge(*nm.summed(j + 1))
                    nc.gpsimd.tensor_tensor(sqsum[:, :], sqsum[:, :], sq[:, j % 2, :], ALU.add
                                            ).then_inc(nm.summed.sem, 1)

            def zero_masked(t):
                for at in (0, 512, 896, 1024):
                    v = t[:, at:at + P]
                    last = nc.gpsimd.affine_select(out=v, in_=v, compare_op=ALU.is_gt, fill=0.0, base=0,
                                                   pattern=[[1, P]], channel_multiplier=-1)
                return last

            n_self = [0]

            def link(ins):
                n_self[0] += 1
                ins.then_inc(pool_self, 1)
                pool.wait_ge(pool_self, n_self[0])

            def low_qk(j):
                c = ORDER1[j]
                last = None
                for i in range(2):
                    if last is not None:
                        link(last)
                    pool.wait_ge(roped_hi, 2 * ROPED.index(c) + i + 1)
                    rows, other = slice(HD * i, HD * i + HD), slice(HD * (1 - i), HD * (1 - i) + HD)
                    t = y[rows, j % 3, :]
                    if c in (4, 10):
                        k = KA if c == 4 else KB
                        hi = k[rows, 0, i, :]
                        link(nc.gpsimd.tensor_tensor(k[rows, 1, i, :], t, hi.bitcast(f32), ALU.subtract))
                        last = nc.gpsimd.tensor_tensor(k[other, 1, i, :], t, hi.bitcast(f32), ALU.subtract)
                    else:
                        q, h = (QA, 2 * c + i) if c in NORMED else (QB, 2 * (c - 6) + i)
                        last = nc.gpsimd.tensor_tensor(q[other, h, :], t, q[rows, h, :].bitcast(f32), ALU.subtract)
                last.then_inc(rope_done, 1)
                pool.wait_ge(rope_done, ROPED.index(c) + 1)

            sum_squares(n_mix_pre)
            for j in range(len(ORDER1)):
                if ORDER1[j] not in V1:
                    low_qk(j)
            for nm in norms[1:7]:
                sum_squares(nm)
            for h in range(NH):
                pool.wait_ge(sp_ready, h + 1)
                zero_masked(E2[:, :]).then_inc(sp_masked, 1)
            for nm in norms[7:]:
                sum_squares(nm)

        @block.tensor
        def _(pe):
            def mm(out, lhsT, rhs, start=True, stop=True, loose=False):
                return nc.tensor.matmul(out, lhsT, rhs, start=start, stop=stop, skip_group_check=loose)

            def three(bank, slot, t, hi, lo, start, stop):
                whi, wlo = w_hi[slot][:, t * P:(t + 1) * P], w_lo[slot][:, t * P:(t + 1) * P]
                mm(ps[:, bank, :], whi, hi, start, False)
                mm(ps[:, bank, :], whi, lo, False, False)
                return mm(ps[:, bank, :], wlo, hi, False, stop)

            def wait_bank(phase, j):
                if BEFORE[phase, j]:
                    e, n = BEFORE[phase, j]
                    pe.wait_ge(evac_act if e == "A" else evac_dve, n)

            def group(slot, t0, ks, bank, hi, lo, start=True, stop=True, ready=None):
                for n, k in enumerate(ks):
                    if ready is not None:
                        pe.wait_ge(ready[0], ready[1] + k + 1)
                    last = three(bank, slot, t0 + n, hi[:, k, :], lo[:, k, :], start and n == 0,
                                 stop and n == len(ks) - 1)
                last.then_inc(group_done, 1)

            def first_unit(phase, u, ks, hi, lo, readies):
                for j in range(2):
                    wait_bank(phase, j)
                pe.wait_ge(lo_ready, u + 1)
                for n, (k, ready) in enumerate(zip(ks, readies)):
                    pe.wait_ge(*ready)
                    for j in range(2):
                        last = three(j, u % 2, j * len(ks) + n, hi[:, k, :], lo[:, k, :], n == 0, n == len(ks) - 1)
                        if n == len(ks) - 1:
                            last.then_inc(group_done, 1)

            def parts_of(count):
                return [count(k + 1) for k in KS]

            def unit(phase, u, j0, nchunks, ks, hi, lo, after=None):
                pe.wait_ge(lo_ready, u + 1)
                for c in range(nchunks):
                    wait_bank(phase, j0 + c)
                    group(u % 2, c * len(ks), ks, (j0 + c) % 4, hi, lo)
                    if after:
                        after(j0 + c)

            def total(nm):
                for src, ready, n in ((sqsum[:, :], nm.summed, nm.n), (sq[:, (nm.n - 1) % 2, :], nm.squares, nm.n)):
                    pe.wait_ge(*ready(n))
                    for b in range(NB):
                        last = mm(ps[:, nm.ss_bank, b:b + 1], src[:, b * P:(b + 1) * P], ones[:, 0:1],
                                  ready is nm.summed and b == 0, True, loose=True)
                last.then_inc(nm.total.sem, 1)

            def factor(nm):
                pe.wait_ge(*nm.diag(1))
                if nm.before is not None:
                    pe.wait_ge(*nm.before.factor_used)
                mm(ps[:, nm.r_bank, :], ones[:, :], diag[:, :, :]).then_inc(nm.factor.sem, 1)

            KS = range(KD)
            pe.wait_ge(c0_landed, 32)
            def free_item(j):
                if j >= 0:
                    if ORDER1[j] in V1:
                        pe.wait_ge(v_ready, V1.index(ORDER1[j]) + 1)
                    else:
                        pe.wait_ge(roped, ROPED.index(ORDER1[j]) + 1)

            def item(j):
                if j < 0:
                    return
                c = ORDER1[j]
                free_item(j - 2)
                if j == 0:
                    pe.wait_ge(*n_mix_pre.factor_used)
                    pe.wait_ge(c1_landed, 16)
                pe.wait_ge(evac_dve, EVAC["in1", j][1])
                if c in V1:
                    for b in range(NB):
                        last = nc.tensor.transpose(ps[:, 4 + j % 2, b * P:(b + 1) * P],
                                                   y[:, j % 3, b * P:(b + 1) * P], ident[:, :])
                    last.then_inc(vtr_done, 1)
                    return
                mm(ps[:, 4 + j % 2, :], c1[:, C_ROT - C1_AT:C_ROT - C1_AT + P], y[:, j % 3, :]).then_inc(rot_done, 1)
                if c in NORMED:
                    pe.wait_ge(ysq_ready, NORMED.index(c) + 1)
                    mm(ps[:, 6 + j % 2, :], c1[:, C_HONE - C1_AT:C_HONE - C1_AT + P], ysq[:, j % 2, :]).then_inc(hsum_done, 1)

            first_unit("in1", 0, KS, h_hi, h_lo, parts_of(n_mix_pre.lo))
            total(n_mix_pre)

            def beside(j):
                if j == 2:
                    factor(n_mix_pre)
                for i in {3: (0,), 4: (1, 2), 5: (3, 4)}.get(j, (j - 1,) if j > 5 else ()):
                    item(i)

            for u in range(1, UNITS_IN1):
                unit("in1", u, 2 * u, 2, KS, h_hi, h_lo, after=beside)
            item(11)

            pe.wait_ge(roped, len(ROPED))
            pe.wait_ge(rope_done, ROPED.index(NORMED[-1]) + 1)
            pe.wait_ge(v_ready, 1)
            pe.wait_ge(evac_dve, EVAC["in1", 11][1])

            def scores(s):
                if s >= 64:
                    return
                kind, h, b, k0, k1 = STEPS[s]
                if s >= 3:
                    pe.wait_ge(exp_done, s - 2)
                if s == 32:
                    pe.wait_ge(rope_done, len(ROPED))
                    pe.wait_ge(v_ready, 2)
                q, k = (QA, KA) if kind == 0 else (QB, KB)
                w, bank = (k1 - k0) * P, s % 3
                for part in range(2):
                    last = mm(ps[:, bank, 0:w], q[:, h, b * P:(b + 1) * P], k[:, part, h // 4, k0 * P:k1 * P],
                              part == 0, kind == 0 and part == 1, loose=kind == 1)
                if kind:
                    if b:
                        mm(ps[:, bank, 0:P], ident_r[:, :], mask_r[:, 0, :], False, True, loose=True)
                    if b + 1 < NB:
                        mm(ps[:, bank, w - P:w], ident_r[:, :], mask_r[:, 1, :], False, True, loose=True)
                    last = mm(ps[:, bank, w:w + 1], ident[:, :], gain[:, G_SINK + h:G_SINK + h + 1], False, True,
                              loose=True)
                last.then_inc(s_done, 1)

            def weighted(g):
                c = g // 2
                if c >= 2 and g % 2 == 0:
                    pe.wait_ge(ot_ready, c - 1)
                r, v = HD * (g % 2), (VA if g < NH else VB)
                kv = (g % NH) // 4
                pe.wait_ge(pt_ready, 4 * (g + 1))
                order = ([(kb, 0, NB) for kb in range(NB)] if g < NH else
                         [(1, 0, 3), (0, 0, 2), (2, 1, 4), (3, 2, 4)])
                for n, (kb, q0, q1) in enumerate(order):
                    last = mm(ps[r:r + HD, 5 + c % 2, q0 * P:q1 * P], v[:, kb, kv * HD:(kv + 1) * HD],
                              PT[:, g % 2, kb, q0 * P:q1 * P], n == 0, n == len(order) - 1, loose=True)
                last.then_inc(av_done, 1)

            pe.wait_ge(masks_ready, 2)
            scores(0)
            scores(1)
            for s, (kind, h, b, k0, k1) in enumerate(STEPS):
                scores(s + 2)
                pe.wait_ge(pn_ready, s + 1)
                if s >= 2:
                    pe.wait_ge(pt_ready, s - 1)
                for kb in range(k0, k1):
                    last = nc.tensor.transpose(ps[:, 3 + s % 2, (kb - k0) * P:(kb - k0 + 1) * P],
                                               prob[:, s % 3, (kb - k0) * P:(kb - k0 + 1) * P], ident[:, :])
                last.then_inc(tr_done, 1)
                if s % 4 == 2 and s > 2:
                    weighted(s // 4 - 1)
                if s == NORM_A_STEP + 4:
                    total(n_group_a)
                if s == NORM_A_STEP + 8:
                    factor(n_group_a)
            weighted(15)
            pe.wait_ge(ot_ready, 8)
            pe.wait_ge(pt_ready, 64)
            total(n_group_b)
            factor(n_group_b)

            first_unit("out1", U_OUT1, KS, h_hi, h_lo,
                       [nm.lo(k + 1) for nm in (n_group_a, n_group_b) for k in range(4)])
            for u in range(1, UNITS_OUT1):
                unit("out1", U_OUT1 + u, 2 * u, 2, KS, h_hi, h_lo)

            def ffn(phase, down, u_ff, u_down, nm, mids0):
                g0, a0, d0 = BASE[phase]
                first_unit(phase, u_ff, KS, h_hi, h_lo, parts_of(nm.lo))
                total(nm)
                unit(phase, u_ff + 1, 2, 2, KS, h_hi, h_lo, after=lambda j: factor(nm) if j == 2 else None)
                with pe.Fori(1, KF // 2) as i:
                    for half in range(2):
                        for c in range(2):
                            pe.wait_ge(lo_ready, i * 2 + (u_ff + 1 + half))
                            pe.wait_ge(evac_dve, i * 4 + (d0 - 3 + 2 * half + c))
                            group(half, c * KD, KS, 2 * half + c, h_hi, h_lo)
                g0, a0, d0 = BASE[down]
                pe.wait_ge(evac_dve, d0)

                def chunk(j, c, ready=None):
                    for part in range(2):
                        pe.wait_ge(lo_ready, j * 2 + (u_down + part + 1))
                        group(part, 0, range(part * DOWN_TILES, (part + 1) * DOWN_TILES), c, mid_hi, mid_lo,
                              part == 0, part == 1, ready)

                chunk(0, 0, (prod_lo, mids0))
                chunk(1, 1)
                evac, e0 = (evac_act, a0) if down == "down1" else (evac_dve, d0)
                with pe.Fori(1, KD // 2) as i:
                    for c in range(2):
                        pe.wait_ge(evac, i * 2 + (e0 - 1 + c))
                        chunk(i * 2 + c, c)

            total(n_mix_post)
            factor(n_mix_post)
            ffn("ff1", "down1", U_FF1, U_DOWN1, n_ffn_pre, 0)
            total(n_ffn_post)
            factor(n_ffn_post)

            def vee(i):
                pe.wait_ge(evac_dve, EVAC["in2", 8 + i][1])
                if i >= 2:
                    pe.wait_ge(v2_ready, i - 1)
                for b in range(NB):
                    last = nc.tensor.transpose(ps[:, 4 + i % 2, b * P:(b + 1) * P],
                                               hf[:, i % 2, b * P:(b + 1) * P], ident[:, :])
                last.then_inc(v2tr_done, 1)

            first_unit("in2", U_IN2, KS, h_hi, h_lo, parts_of(n_mix2.lo))
            total(n_mix2)
            for u in range(1, 8):
                unit("in2", U_IN2 + u, 2 * u, 2, KS, h_hi, h_lo,
                     after=lambda j: vee(j - 9) if 9 <= j < 13 else factor(n_mix2) if j == 2 else None)
            Z = ps[:, 4:7, :].rearrange("p b s -> p (b s)")
            AHEAD = 6

            def pool_map():
                for u in range(UNITS_POOL):
                    pe.wait_ge(lo_ready, U_POOL + u + 1)
                    for c in range(2):
                        j = 2 * u + c
                        wait_bank("pool", j)
                        pe.wait_ge(pl_lo_ready, j + 1)
                        group(u % 2, c, range(j, j + 1), j % 4, pl_hi, pl_lo)

            def three_rows(slot, t0, bank, k0, k1):
                for k in range(k0, k1):
                    last = three(bank, slot, t0 + k, h_hi[:, k, :], h_lo[:, k, :], k == 0, k == KD - 1)
                return last

            ZAT = [0, 512, 1024, 896]
            pe.wait_ge(v2_ready, 4)
            pe.wait_ge(c2_ready, 2)
            for h in range(NH):
                r = HD * (h % 2)
                if h:
                    pe.wait_ge(a_done, h)
                for kb in range(NB):
                    w = S - kb * P
                    last = mm(Z[:, ZAT[kb]:ZAT[kb] + w], K2[r:r + HD, h // 2, kb * P:(kb + 1) * P],
                              Q2[r:r + HD, h // 2, kb * P:S], kb < 3, True, loose=True)
                last.then_inc(z_done, 1)
                u = 8 + h
                pe.wait_ge(lo_ready, U_IN2 + u + 1)
                wait_bank("in2", 2 * u)
                group(u % 2, 0, KS, (2 * u) % 4, h_hi, h_lo)
                wait_bank("in2", 2 * u + 1)
                three_rows(u % 2, KD, (2 * u + 1) % 4, 0, AHEAD)
                for ready, e in ((sp_hi, E2_hi), (sp_lo, E2_lo)):
                    pe.wait_ge(ready, h + 1)
                    for kb in range(NB):
                        for later in range(kb, NB):
                            w = S - later * P
                            o = ZAT[kb] + (later - kb) * P
                            last = mm(Z[:, o:o + w], c2[:, 0:P] if later == kb else c2[:, P:2 * P],
                                      e[:, ZAT[later]:ZAT[later] + w], False, True, loose=True)
                for kb in range(NB):
                    last = mm(Z[:, ZAT[kb]:ZAT[kb] + P], c2[:, 3 * P:4 * P], c2[:, 2 * P:3 * P], False, True,
                              loose=True)
                last.then_inc(cum_done, 1)
                three_rows(u % 2, KD, (2 * u + 1) % 4, AHEAD, KD).then_inc(group_done, 1)
                if h == NH - 1:
                    pool_map()
                pe.wait_ge(a_done, h + 1)
                if h % 2 == 0 and h:
                    pe.wait_ge(ob_ready, h // 2)
                for kb in range(NB):
                    w = S - kb * P
                    last = mm(ps[r:r + HD, 7, kb * P:S], V2[:, kb, h * HD:(h + 1) * HD],
                              A2[:, ZAT[kb]:ZAT[kb] + w], kb == 0, kb == 3, loose=True)
                last.then_inc(av2_done, 1)

            pe.wait_ge(ya_lo, 4)
            for u in range(UNITS_BRANCH):
                unit("bra", U_BRA + u, 4 * u, 4, range(4), h_hi, h_lo)
            pe.wait_ge(yb_lo, 4)
            for u in range(UNITS_BRANCH):
                unit("brb", U_BRB + u, 4 * u, 4, range(4, 8), h_hi, h_lo)
            first_unit("out2", U_OUT2, KS, m_hi, m_lo, parts_of(Count(m_lo_ready)))
            for u in range(1, UNITS_OUT2):
                unit("out2", U_OUT2 + u, 2 * u, 2, KS, m_hi, m_lo)
            ffn("ff2", "down2", U_FF2, U_DOWN2, n_ffn2, KF)

            total(n_ple)
            pe.wait_ge(p_lo_ready, 1)
            unit("plep", U_PLEP, 0, KD, range(2), p_hi, p_lo)
            factor(n_ple)
            first_unit("pleg", U_PLEG, KS, h_hi, h_lo, parts_of(n_ple.lo))
            for u in range(1, 4):
                unit("pleg", U_PLEG + u, 2 * u, 2, KS, h_hi, h_lo)
            total(n_final)
            factor(n_final)

        @block.scalar
        def _(act):
            n_self = [0]

            def link(ins):
                n_self[0] += 1
                ins.then_inc(act_self, 1)
                act.wait_ge(act_self, n_self[0])

            def af(out, in_, func, **kw):
                return nc.scalar.activation(out, in_, func, **kw)

            def split(u):
                slot, width = u % 2, tiles_of(u)
                act.wait_ge(raw_landed[slot], 16 * (u // 2 + 1))
                if u >= 2:
                    act.wait_ge(group_done, USED[u - 2])
                af(w_hi[slot][:, 0:width * P], w_raw[slot][:, 0:width * P], ACT.Copy).then_inc(hi_ready, 1)

            def square(nm, j, src):
                if j >= 2:
                    act.wait_ge(*nm.summed(j))
                af(sq[:, j % 2, :], src, ACT.Square).then_inc(nm.squares.sem, 1)

            def tables(name):
                nc.scalar.preload_act_table_set(name)

            def guess(nm):
                act.wait_ge(*nm.var(1))
                link(af(stat[:, 1, :], stat[:, 0, :], ACT.Ln))
                af(stat[:, 2, :], stat[:, 1, :], ACT.Exp, scale=-0.5).then_inc(nm.guess.sem, 1)

            def high_one(nm, dst, k, n0):
                act.wait_ge(*nm.f32(k + 1))
                af(dst[:, n0 + k, :], hf[:, k % 2, :], ACT.Copy).then_inc(nm.hi.sem, 1)

            def high(nm, dst, n0=0):
                for k in range(nm.n):
                    high_one(nm, dst, k, n0)

            def late_part(nm, name, k):
                square(nm, k, X[:, k, :])
                af(h_hi[:, k, :], X[:, k, :], ACT.Copy, scale=gcol(name, k)).then_inc(nm.hi.sem, 1)

            def late_factors(nm):
                act.wait_ge(*nm.factor(1))
                af(factors_sb[:, :], ps[:, nm.r_bank, :], ACT.Copy).then_inc(nm.f32.sem, 1)

            tables(LN_EXP)
            act.dma_start(gain[:, :], gains[:, :]).then_inc(gain_landed, 16)
            act.dma_start(ident[:, :], consts[:, C_ID:C_ID + P]).then_inc(c0_landed, 16)
            act.dma_start(ones[:, :], consts[:, C_ONE:C_ONE + P]).then_inc(c0_landed, 16)
            act.wait_ge(gain_landed, 16)
            for k in range(KD):
                act.wait_ge(x_landed[k // 2], 16)
                late_part(n_mix_pre, "norm_mix_pre", k)
                if k == 0:
                    act.dma_start(c1[:, :], consts[:, C1_AT:]).then_inc(c1_landed, 16)
                    split(0)
            act.dma_start(hf[:, :, :], pT.rearrange("(k p) s -> p k s", p=P)).then_inc(p_landed, 16)
            split(1)
            guess(n_mix_pre)
            late_factors(n_mix_pre)
            act.wait_ge(p_landed, 16)
            af(p_hi[:, :, :], hf[:, :, :], ACT.Copy).then_inc(p_hi_ready, 1)

            def finish(j):
                c = ORDER1[j]
                if c in V1:
                    act.wait_ge(vtr_done, V1.index(c) + 1)
                    af((VA if c == 5 else VB)[:, :, :], ps[:, 4 + j % 2, :].rearrange("p (b c) -> p b c", b=NB),
                       ACT.Copy).then_inc(v_ready, 1)
                elif c in NORMED:
                    act.wait_ge(hvar_ready, NORMED.index(c) + 1)
                    link(af(rt[:, 3, :], rt[:, 2, :], ACT.Ln))
                    af(rt[:, 3, :], rt[:, 3, :], ACT.Exp, scale=-0.5).then_inc(hguess_ready, 1)

            def high_qk(j):
                if j < 0 or ORDER1[j] in V1:
                    return
                c = ORDER1[j]
                act.wait_ge(roped, ROPED.index(c) + 1)
                for i in range(2):
                    rows = slice(HD * i, HD * i + HD)
                    if c in (4, 10):
                        dst = (KA if c == 4 else KB)[rows, 0, i, :]
                    else:
                        dst = QA[rows, 2 * c + i, :] if c in NORMED else QB[rows, 2 * (c - 6) + i, :]
                    if c in (4, 10):
                        af((KA if c == 4 else KB)[HD * (1 - i):HD * (1 - i) + HD, 0, i, :], y[rows, j % 3, :],
                           ACT.Copy)
                    af(dst, y[rows, j % 3, :], ACT.Copy).then_inc(roped_hi, 1)

            act.wait_ge(c0_landed, 32)
            act.wait_ge(c1_landed, 16)
            af(ident_r[:, :], ident[:, :], ACT.Copy).then_inc(masks_ready, 1)
            af(mask_r[:, :, :], c1[:, C_MASK - C1_AT:C_MASK - C1_AT + 2 * P].rearrange("p (m c) -> p m c", m=2),
               ACT.Copy).then_inc(masks_ready, 1)
            for j in range(12):
                c = ORDER1[j]
                if c in NORMED:
                    act.wait_ge(evac_dve, EVAC["in1", j][1])
                    if j >= 2:
                        act.wait_ge(roped, sum(o not in V1 for o in ORDER1[:j - 1]))
                    af(ysq[:, j % 2, :], y[:, j % 3, :], ACT.Square).then_inc(ysq_ready, 1)
                high_qk(j - 2)
                if j % 2 and j < 11:
                    split(j // 2 + 2)
                if j:
                    finish(j - 1)
            high_qk(10)
            finish(11)
            split(UNITS_IN1 + 1)

            def copy_pt(s):
                kind, h, b, k0, k1 = STEPS[s]
                g = s // 4
                act.wait_ge(tr_done, s + 1)
                if s == 0:
                    act.wait_ge(rope_done, len(ROPED))
                if g >= 2 and s % 4 == 0:
                    act.wait_ge(av_done, g - 1)
                n = k1 - k0
                af(PT[:, g % 2, k0:k1, b * P:(b + 1) * P],
                   ps[:, 3 + s % 2, 0:n * P].rearrange("p (b c) -> p b c", b=n), ACT.Copy).then_inc(pt_ready, 1)

            def copy_out(c):
                act.wait_ge(av_done, 2 * c + 2)
                af(OT[:, c, :], ps[:, 5 + c % 2, :], ACT.Copy).then_inc(ot_ready, 1)

            def square_group(nm, c0, j):
                act.wait_ge(ot_ready, c0 + j + 1)
                square(nm, j, OT[:, c0 + j, :])

            for s, (kind, h, b, k0, k1) in enumerate(STEPS):
                w = (k1 - k0) * P + kind
                act.wait_ge(nmax_ready, s + 1)
                if s >= 3:
                    act.wait_ge(tr_done, s - 2)
                af(prob[:, s % 3, 0:w], ps[:, s % 3, 0:w], ACT.Exp, bias=nmax[:, s:s + 1],
                   accum_out=den[:, s:s + 1]).then_inc(exp_done, 1)
                if s >= 2:
                    copy_pt(s - 2)
                if s % 8 == 4 and s > 8:
                    copy_out(s // 8 - 1)
                if NORM_A_STEP <= s < NORM_A_STEP + 4:
                    square_group(n_group_a, 0, s - NORM_A_STEP)
                if s == NORM_A_STEP + 6:
                    guess(n_group_a)
                if NORM_A_STEP + 10 <= s < NORM_A_STEP + 14:
                    high_one(n_group_a, h_hi, s - (NORM_A_STEP + 10), 0)
            copy_pt(62)
            copy_pt(63)
            for j in range(3):
                square_group(n_group_b, 4, j)
            copy_out(7)
            square_group(n_group_b, 4, 3)
            guess(n_group_b)
            high(n_group_b, h_hi, 4)

            for j in range(KD):
                act.wait_ge(group_done, GROUP["out1", j])
                square(n_mix_post, j, ps[:, j % 4, :])
                af(F1[:, j, :], ps[:, j % 4, :], ACT.Copy).then_inc(evac_act, 1)
                if j % 2:
                    split(U_OUT1 + j // 2 + 2)
            guess(n_mix_post)
            for k in range(KD):
                act.wait_ge(x_new[0], k + 1)
                late_part(n_ffn_pre, "norm_ffn_pre", k)
            guess(n_ffn_pre)

            def ffn(phase, u_ff, mids0, nm):
                g0, a0, d0 = BASE[phase]

                def turn(i, last=False):
                    first = isinstance(i, int) and i == 0
                    for half in range(2):
                        if last:
                            split(u_ff + 2 * i + 2 + half)
                        else:
                            act.wait_ge(raw_landed[half], i * 16 + 16 * (u_ff // 2 + 2))
                            act.wait_ge(group_done, i * 4 + (g0 + 2 + 2 * half))
                            af(w_hi[half][:, :], w_raw[half][:, :], ACT.Copy).then_inc(hi_ready, 1)
                        if half:
                            continue
                        if first:
                            late_factors(nm)
                        for c in range(2):
                            act.wait_ge(evac_dve, i * 4 + (d0 + 1 + c))
                            af(sq[:, c, :], sq[:, c, :], ACT.Silu).then_inc(silu_ready, 1)
                        for c in range(2):
                            act.wait_ge(prod_ready, i * 2 + (mids0 + 1 + c))
                            af(mid_hi[:, bass.ds(i * 2 + c, 1), :] if not isinstance(i, int)
                               else mid_hi[:, 2 * i + c, :], hf[:, c, :], ACT.Copy).then_inc(prod_hi, 1)

                turn(0)
                with act.Fori(1, KF // 2 - 1) as i:
                    turn(i)
                turn(KF // 2 - 1, True)

            tables(SILU)
            ffn("ff1", U_FF1, 0, n_ffn_pre)
            tables(LN_EXP)

            def down_chunk(phase, u0, j, epilogue):
                act.wait_ge(group_done, GROUP[phase, j] - 1)
                split(u0 + 2 * j + 2)
                act.wait_ge(group_done, GROUP[phase, j])
                epilogue(j)
                split(u0 + 2 * j + 3)

            def down1(j):
                square(n_ffn_post, j, ps[:, j % 2, :])
                af(F[:, j, :], ps[:, j % 2, :], ACT.Copy).then_inc(evac_act, 1)

            for j in range(KD):
                down_chunk("down1", U_DOWN1, j, down1)
            act.dma_start(E2[:, 0:3 * P], consts[:, C_TRI:C_TRI + 3 * P]).then_inc(c2_landed, 16)
            act.dma_start(inv_count[:, :], consts[:, C_INVC:C_INVC + 4 * PADW]).then_inc(c2_landed, 16)
            guess(n_ffn_post)
            for k in range(KD):
                act.wait_ge(x_new[0], KD + k + 1)
                late_part(n_mix2, "norm_mix_2", k)
            guess(n_mix2)

            def finish_vee(i):
                act.wait_ge(v2tr_done, i + 1)
                af(V2[:, :, i * P:(i + 1) * P], ps[:, 4 + i % 2, :].rearrange("p (b c) -> p b c", b=NB),
                   ACT.Copy).then_inc(v2_ready, 1)

            for u in range(8):
                split(U_IN2 + u + 2)
                if u == 0:
                    late_factors(n_mix2)
                if u == 2:
                    act.wait_ge(c2_landed, 32)
                    af(c2[:, 0:3 * P], E2[:, 0:3 * P], ACT.Copy).then_inc(c2_ready, 1)
                    af(c2[:, 3 * P:4 * P], ident[:, :], ACT.Copy).then_inc(c2_ready, 1)
                for i in range(4):
                    if (9 + i) // 2 == u:
                        finish_vee(i)

            Z = ps[:, 4:7, :].rearrange("p b s -> p (b s)")[:, 0:1280]

            def copy_ob(c):
                act.wait_ge(av2_done, 2 * c + 2)
                af(OB[:, c, :], ps[:, 7, :], ACT.Copy).then_inc(ob_ready, 1)

            def pl_high(i):
                act.wait_ge(pooled, i + 1)
                af(pl_hi[:, i, :], UP[:, i, :], ACT.Copy).then_inc(pl_hi_ready, 1)

            for h in range(NH):
                act.wait_ge(z_done, h + 1)
                if h:
                    act.wait_ge(cum_done, h)
                else:
                    act.wait_ge(c2_ready, 2)
                link(af(E2[:, :], Z, ACT.Abs))
                link(af(E2[:, :], E2[:, :], ACT.Exp, scale=-1.0))
                af(E2[:, :], E2[:, :], ACT.Ln, bias=1.0).then_inc(ln_done, 1)
                act.wait_ge(sp_masked, h + 1)
                af(E2_hi[:, :], E2[:, :], ACT.Copy).then_inc(sp_hi, 1)
                if h == NH - 1:
                    for i in range(4):
                        pl_high(i)
                if h % 2 == 0 and h:
                    copy_ob(h // 2 - 1)
                act.wait_ge(cum_done, h + 1)
                if h:
                    act.wait_ge(av2_done, h)
                af(A2[:, :], Z, ACT.Exp).then_inc(a_done, 1)
                split(U_IN2 + 8 + h + 2)

            def yb_high(i):
                act.wait_ge(ob_ready, i + 1)
                act.wait_ge(group_done, GROUP["in2", 31])
                af(h_hi[:, 4 + i, :], OB[:, i, :], ACT.Copy).then_inc(yb_hi, 1)

            for j in range(4):
                act.wait_ge(group_done, GROUP["pool", j])
                if j >= 2:
                    act.wait_ge(ya_lo, j - 1)
                af(hf[:, j % 2, :], ps[:, j % 4, :], ACT.Copy, scale=gcol("pool_scale_2", j)
                   ).then_inc(evac_act, 1)
                act.wait_ge(evac_act, EVAC["pool", j][1])
                af(h_hi[:, j, :], hf[:, j % 2, :], ACT.Copy).then_inc(ya_hi, 1)
                if j % 2:
                    split(U_POOL + j // 2 + 2)
            copy_ob(3)
            for i in range(4):
                yb_high(i)
            tables(SIGMOID)
            act.wait_ge(evac_dve, EVAC["in2", 31][1])
            for j in range(0, KD, 2):
                af(GA[:, j:j + 2, :], GA[:, j:j + 2, :], ACT.Sigmoid).then_inc(sig_ready, 1)
            for j in range(0, KD, 2):
                af(GB[:, j:j + 2, :], GB[:, j:j + 2, :], ACT.Sigmoid).then_inc(sig_ready, 1)
            tables(LN_EXP)
            split(U_BRA + 2)
            split(U_BRA + 3)
            for j in range(KD):
                act.wait_ge(merged, j + 1)
                af(m_hi[:, j, :], GB[:, j, :], ACT.Copy).then_inc(m_hi_ready, 1)
                if j % 4 == 3:
                    split(U_BRB + j // 4 + 2)
            for j in range(KD):
                act.wait_ge(evac_dve, EVAC["out2", j][1])
                late_part(n_ffn2, "norm_ffn_2", j)
                if j % 2:
                    split(U_OUT2 + j // 2 + 2)
            guess(n_ffn2)
            tables(SILU)
            ffn("ff2", U_FF2, KF, n_ffn2)
            tables(LN_EXP)

            def down2(j):
                act.wait_ge(evac_dve, EVAC["down2", j][1])
                square(n_ple, j, X[:, j, :])

            for j in range(KD):
                down_chunk("down2", U_DOWN2, j, down2)
            guess(n_ple)
            for j in range(KD):
                act.wait_ge(group_done, GROUP["plep", j])
                af(PP[:, j, :], ps[:, j % 4, :], ACT.Copy).then_inc(evac_act, 1)
            tables(SIGMOID)
            high(n_ple, h_hi)
            split(U_PLEP + 2)
            for j in range(KD):
                act.wait_ge(group_done, GROUP["pleg", j])
                if j >= 2:
                    act.wait_ge(x_new[1], j - 1)
                af(hf[:, j % 2, :], ps[:, j % 4, :], ACT.Sigmoid).then_inc(evac_act, 1)
                if j % 2 and U_PLEG + j // 2 + 2 < N_UNITS:
                    split(U_PLEG + j // 2 + 2)
                if j:
                    act.wait_ge(x_new[1], j)
                    square(n_final, j - 1, X[:, j - 1, :])
            tables(LN_EXP)
            act.wait_ge(x_new[1], KD)
            square(n_final, KD - 1, X[:, KD - 1, :])
            guess(n_final)

        @block.vector
        def _(dve):
            n_self = [0]

            def mark(ins):
                n_self[0] += 1
                ins.then_inc(dve_self, 1)
                return n_self[0]

            def link(ins):
                dve.wait_ge(dve_self, mark(ins))

            def tt(out, a, b, op):
                return nc.vector.tensor_tensor(out, a, b, op)

            def ts(out, a, s1, op0, s2=None, op1=None):
                return (nc.vector.tensor_scalar(out, a, s1, s2, op0, op1) if op1 is not None
                        else nc.vector.tensor_scalar(out, a, s1, None, op0))

            def stt(out, a, s, b, op0, op1):
                return nc.vector.scalar_tensor_tensor(out=out, in0=a, scalar=s, in1=b, op0=op0, op1=op1)

            def low(out, full, hi):
                return tt(out, full, hi.bitcast(f32), ALU.subtract)

            def split(u):
                slot, width = u % 2, tiles_of(u)
                dve.wait_ge(hi_ready, u + 1)
                low(w_lo[slot][:, 0:width * P], w_raw[slot][:, 0:width * P], w_hi[slot][:, 0:width * P]
                    ).then_inc(lo_ready, 1)

            def refine(out, v, r0):
                link(stt(out, v, -0.5, r0, ALU.mult, ALU.mult))
                link(tt(out, out, r0, ALU.mult))
                return stt(out, out, 1.5, r0, ALU.add, ALU.mult)

            def variance(nm, width=D):
                dve.wait_ge(*nm.total(1))
                ts(stat[:, 0, :], ps[:, nm.ss_bank, 0:NB], 1.0 / width, ALU.mult, EPS, ALU.add
                   ).then_inc(nm.var.sem, 1)

            def factors(nm):
                dve.wait_ge(*nm.guess(1))
                link(refine(stat[:, 3, :], stat[:, 0, :], stat[:, 2, :]))
                for b in range(NB):
                    last = ts(diag[:, b, :], ident[:, :], stat[:, 3, b:b + 1], ALU.mult)
                last.then_inc(nm.diag.sem, 1)

            def apply_one(nm, src, name, dst_hi, dst_lo, k, n0):
                if k < nm.n:
                    if k == 0:
                        dve.wait_ge(*nm.factor(1))
                    if k >= 2:
                        dve.wait_ge(*nm.lo(k - 1))
                    stt(hf[:, k % 2, :], src[:, k, :], gcol(name, k), ps[:, nm.r_bank, :], ALU.mult, ALU.mult
                        ).then_inc(nm.f32.sem, 1)
                if k:
                    dve.wait_ge(*nm.hi(k))
                    low(dst_lo[:, n0 + k - 1, :], hf[:, (k - 1) % 2, :], dst_hi[:, n0 + k - 1, :]
                        ).then_inc(nm.lo.sem, 1)

            def apply(nm, src, name, dst_hi, dst_lo, n0=0):
                for k in range(nm.n + 1):
                    apply_one(nm, src, name, dst_hi, dst_lo, k, n0)

            def late_low(nm, name, k):
                dve.wait_ge(*nm.hi(k + 1))
                stt(h_lo[:, k, :], X[:, k, :], gcol(name, k), h_hi[:, k, :].bitcast(f32), ALU.mult, ALU.subtract
                    ).then_inc(nm.lo.sem, 1)

            def scaled(bank, out, scale=None):
                if scale is None:
                    return tt(out, bank, factors_sb[:, :], ALU.mult)
                return stt(out, bank, scale, factors_sb[:, :], ALU.mult, ALU.mult)

            def apply_post(nm, f, name, added, late, late_name):
                dve.wait_ge(*nm.factor(1))
                for k in range(KD + 2):
                    if k < KD:
                        if k >= 2:
                            dve.wait_ge(x_new[0], added + k - 1)
                        stt(hf[:, k % 2, :], f[:, k, :], gcol(name, k), ps[:, R_BANK, :], ALU.mult, ALU.mult
                            ).then_inc(nm.f32.sem, 1)
                    if 1 <= k <= KD:
                        dve.wait_ge(*nm.f32(k))
                        tt(X[:, k - 1, :], X[:, k - 1, :], hf[:, (k - 1) % 2, :], ALU.add).then_inc(x_new[0], 1)
                    if k >= 2:
                        late_low(late, late_name, k - 2)

            dve.wait_ge(c0_landed, 32)
            dve.wait_ge(gain_landed, 16)
            for k in range(KD):
                late_low(n_mix_pre, "norm_mix_pre", k)
                if k == 0:
                    split(0)
            split(1)
            variance(n_mix_pre)
            factors(n_mix_pre)
            dve.wait_ge(c1_landed, 16)
            dve.wait_ge(*n_mix_pre.f32(1))

            def evacuate(j):
                dve.wait_ge(group_done, GROUP["in1", j])
                if j >= 3:
                    if ORDER1[j - 3] in V1:
                        dve.wait_ge(v_ready, V1.index(ORDER1[j - 3]) + 1)
                    else:
                        dve.wait_ge(rope_done, ROPED.index(ORDER1[j - 3]) + 1)
                scaled(ps[:, j % 4, :], y[:, j % 3, :]).then_inc(evac_dve, 1)

            def rope(j):
                c = ORDER1[j]
                if c in V1:
                    return
                normed, key = c in NORMED, c in (4, 10)
                cos, sin = (at - C1_AT for at in ((C_COSA, C_SINA) if normed else (C_COSB, C_SINB)))
                at = G_KN if key else G_QN
                scale, scale_rot = ((gain[:, at:at + 1], gain[:, at + 2:at + 3]) if normed else
                                    (1.0, 1.0) if key else (SCALE, SCALE))
                i_roped = ROPED.index(c)
                if i_roped:
                    dve.wait_ge(roped, i_roped)
                dve.wait_ge(rot_done, i_roped + 1)
                stt(rt[:, 0, :], y[:, j % 3, :], scale, c1[:, cos:cos + S], ALU.mult, ALU.mult)
                m = mark(stt(rt[:, 1, :], ps[:, 4 + j % 2, :], scale_rot, c1[:, sin:sin + S], ALU.mult, ALU.mult))
                if normed:
                    dve.wait_ge(hsum_done, NORMED.index(c) + 1)
                    ts(rt[:, 2, :], ps[:, 6 + j % 2, :], 1.0 / HD, ALU.mult, EPS, ALU.add).then_inc(hvar_ready, 1)
                dve.wait_ge(dve_self, m)
                out = y[:, j % 3, :]
                if not normed:
                    tt(out, rt[:, 0, :], rt[:, 1, :], ALU.add).then_inc(roped, 1)
                    return
                link(tt(out, rt[:, 0, :], rt[:, 1, :], ALU.add))
                dve.wait_ge(hguess_ready, NORMED.index(c) + 1)
                link(refine(rt[:, 4, :], rt[:, 2, :], rt[:, 3, :]))
                stt(out, out, 1.0 if key else SCALE, rt[:, 4, :], ALU.mult, ALU.mult).then_inc(roped, 1)

            for j in range(12):
                if j > 1 and j % 2 and j < 11:
                    split(j // 2 + 2)
                evacuate(j)
                if j == 1:
                    split(2)
                if j:
                    rope(j - 1)
                if j == 1:
                    dve.wait_ge(p_hi_ready, 1)
                    low(p_lo[:, :, :], hf[:, :, :], p_hi[:, :, :]).then_inc(p_lo_ready, 1)
            split(UNITS_IN1 + 1)

            def negmax(s):
                if s >= 64:
                    return
                kind, h, b, k0, k1 = STEPS[s]
                dve.wait_ge(s_done, s + 1)
                nc.vector.tensor_reduce(nmax[:, s:s + 1], ps[:, s % 3, 0:(k1 - k0) * P + kind], AX.X, ALU.max,
                                        negate=True).then_inc(nmax_ready, 1)

            negmax(0)
            negmax(1)
            for s, (kind, h, b, k0, k1) in enumerate(STEPS):
                w = (k1 - k0) * P
                dve.wait_ge(exp_done, s + 1)
                link(nc.vector.reciprocal(rden[:, s:s + 1], den[:, s:s + 1]))
                ts(prob[:, s % 3, 0:w], prob[:, s % 3, 0:w], rden[:, s:s + 1], ALU.mult).then_inc(pn_ready, 1)
                negmax(s + 2)
                if s == NORM_A_STEP + 5:
                    variance(n_group_a, 4 * P)
                if s == NORM_A_STEP + 7:
                    factors(n_group_a)
                if NORM_A_STEP + 9 <= s < NORM_A_STEP + 14:
                    apply_one(n_group_a, OT[:, 0:4, :], "group_norm_a", h_hi, h_lo, s - (NORM_A_STEP + 9), 0)

            variance(n_group_b, 4 * P)
            factors(n_group_b)
            apply(n_group_b, OT[:, 4:8, :], "group_norm_b", h_hi, h_lo, 4)
            for u in range(UNITS_OUT1):
                split(U_OUT1 + u + 2)
            variance(n_mix_post)
            factors(n_mix_post)
            apply_post(n_mix_post, F1, "norm_mix_post", 0, n_ffn_pre, "norm_ffn_pre")

            def ffn(phase, u_ff, mids0, nm):
                g0, a0, d0 = BASE[phase]

                variance(nm)
                factors(nm)

                def turn(i, last=False):
                    first = isinstance(i, int) and i == 0
                    for half in range(2):
                        if last:
                            split(u_ff + 2 * i + 2 + half)
                        else:
                            dve.wait_ge(hi_ready, i * 2 + (u_ff + 3 + half))
                            low(w_lo[half][:, :], w_raw[half][:, :], w_hi[half][:, :]).then_inc(lo_ready, 1)
                        if half:
                            continue
                        if first:
                            dve.wait_ge(*nm.f32(1))
                        for c in range(2):
                            dve.wait_ge(group_done, i * 4 + (g0 + 1 + c))
                            if not first:
                                dve.wait_ge(prod_ready, i * 2 + (mids0 - 1 + c))
                            scaled(ps[:, c, :], sq[:, c, :]).then_inc(evac_dve, 1)
                        for c in range(2):
                            dve.wait_ge(group_done, i * 4 + (g0 + 3 + c))
                            if not first:
                                dve.wait_ge(prod_lo, i * 2 + (mids0 - 1 + c))
                            scaled(ps[:, 2 + c, :], hf[:, c, :]).then_inc(evac_dve, 1)
                            dve.wait_ge(silu_ready, i * 2 + (mids0 + 1 + c))
                            dve.wait_ge(evac_dve, i * 4 + (d0 + 3 + c))
                            tt(hf[:, c, :], hf[:, c, :], sq[:, c, :], ALU.mult).then_inc(prod_ready, 1)
                        for c in range(2):
                            dve.wait_ge(prod_hi, i * 2 + (mids0 + 1 + c))
                            at = 2 * i + c if isinstance(i, int) else bass.ds(i * 2 + c, 1)
                            low(mid_lo[:, at, :], hf[:, c, :], mid_hi[:, at, :]).then_inc(prod_lo, 1)

                turn(0)
                with dve.Fori(1, KF // 2 - 1) as i:
                    turn(i)
                turn(KF // 2 - 1, True)

            ffn("ff1", U_FF1, 0, n_ffn_pre)
            for u in range(UNITS_DOWN):
                split(U_DOWN1 + u + 2)
            variance(n_ffn_post)
            factors(n_ffn_post)
            apply_post(n_ffn_post, F, "norm_ffn_post", KD, n_mix2, "norm_mix_2")
            variance(n_mix2)
            factors(n_mix2)

            def chunk2(j):
                dve.wait_ge(group_done, GROUP["in2", j])
                if 10 <= j < 12:
                    dve.wait_ge(v2tr_done, j - 9)
                dst = (K2[:, j, :] if j < 4 else Q2[:, j - 4, :] if j < 8 else hf[:, j % 2, :] if j < 12 else
                       UP[:, j - 12, :] if j < 16 else (GA if j < 24 else GB)[:, j % 8, :])
                scaled(ps[:, j % 4, :], dst, SCALE if 4 <= j < 8 else None).then_inc(evac_dve, 1)

            split(U_IN2 + 2)
            dve.wait_ge(*n_mix2.f32(1))
            chunk2(0)
            for u in range(1, 8):
                chunk2(2 * u - 1)
                chunk2(2 * u)
                split(U_IN2 + u + 2)
            chunk2(15)

            def pool_group(g):
                w, u = POOL_WINDOWS[g], UP[:, g, :]
                src, step, n = u, 1, 0
                if g:
                    dve.wait_ge(pooled, g)
                while step < w:
                    dst = hf[:, n % 2, :]
                    nc.vector.tensor_copy(dst[:, 0:step], src[:, 0:step])
                    link(tt(dst[:, step:S], src[:, step:S], src[:, 0:S - step], ALU.add))
                    src, step, n = dst, 2 * step, n + 1
                tmp = hf[:, n % 2, 0:PADW]
                link(tt(tmp, src[:, 0:PADW], inv_count[:, g * PADW:(g + 1) * PADW], ALU.mult))
                tt(u[:, 0:PADW], tmp, u[:, 0:PADW], ALU.subtract)
                stt(u[:, PADW:S], src[:, PADW:S], 1.0 / w, u[:, PADW:S], ALU.mult, ALU.subtract
                    ).then_inc(pooled, 1)

            dve.wait_ge(evac_dve, EVAC["in2", 15][1])
            dve.wait_ge(v2tr_done, 4)
            dve.wait_ge(c2_landed, 32)
            Z = ps[:, 4:7, :].rearrange("p b s -> p (b s)")[:, 0:1280]
            for h in range(NH):
                dve.wait_ge(ln_done, h + 1)
                stt(E2[:, :], Z, 0.0, E2[:, :], ALU.max, ALU.add).then_inc(sp_ready, 1)
                dve.wait_ge(sp_hi, h + 1)
                low(E2_lo[:, :], E2[:, :], E2_hi[:, :]).then_inc(sp_lo, 1)
                if h < 4:
                    pool_group(h)
                if h == NH - 1:
                    for i in range(4):
                        dve.wait_ge(pl_hi_ready, i + 1)
                        low(pl_lo[:, i, :], UP[:, i, :], pl_hi[:, i, :]).then_inc(pl_lo_ready, 1)
                chunk2(16 + 2 * h)
                chunk2(17 + 2 * h)
                split(U_IN2 + 8 + h + 2)

            for j in range(4):
                dve.wait_ge(ya_hi, j + 1)
                low(h_lo[:, j, :], hf[:, j % 2, :], h_hi[:, j, :]).then_inc(ya_lo, 1)
                if j % 2:
                    split(U_POOL + j // 2 + 2)
            for i in range(4):
                dve.wait_ge(yb_hi, i + 1)
                low(h_lo[:, 4 + i, :], OB[:, i, :], h_hi[:, 4 + i, :]).then_inc(yb_lo, 1)
            for j in range(KD):
                dve.wait_ge(sig_ready, j // 2 + 1)
                dve.wait_ge(group_done, GROUP["bra", j])
                tt(GA[:, j, :], GA[:, j, :], ps[:, j % 4, :], ALU.mult).then_inc(evac_dve, 1)
                if j % 4 == 3:
                    split(U_BRA + j // 4 + 2)
            for j in range(KD):
                dve.wait_ge(sig_ready, 4 + j // 2 + 1)
                dve.wait_ge(group_done, GROUP["brb", j])
                tt(GB[:, j, :], GB[:, j, :], ps[:, j % 4, :], ALU.mult).then_inc(evac_dve, 1)
                dve.wait_ge(evac_dve, EVAC["brb", j][1])
                tt(GB[:, j, :], GB[:, j, :], GA[:, j, :], ALU.add).then_inc(merged, 1)
                dve.wait_ge(m_hi_ready, j + 1)
                low(m_lo[:, j, :], GB[:, j, :], m_hi[:, j, :]).then_inc(m_lo_ready, 1)
                if j % 4 == 3:
                    split(U_BRB + j // 4 + 2)
            for j in range(KD):
                dve.wait_ge(group_done, GROUP["out2", j])
                tt(X[:, j, :], X[:, j, :], ps[:, j % 4, :], ALU.add).then_inc(evac_dve, 1)
                if j:
                    late_low(n_ffn2, "norm_ffn_2", j - 1)
                if j % 2:
                    split(U_OUT2 + j // 2 + 2)
            late_low(n_ffn2, "norm_ffn_2", KD - 1)
            ffn("ff2", U_FF2, KF, n_ffn2)
            for j in range(KD):
                split(U_DOWN2 + 2 * j + 2)
                dve.wait_ge(group_done, GROUP["down2", j])
                tt(X[:, j, :], X[:, j, :], ps[:, j % 2, :], ALU.add).then_inc(evac_dve, 1)
                split(U_DOWN2 + 2 * j + 3)
            variance(n_ple)
            factors(n_ple)
            apply(n_ple, X, "norm_ple_2", h_hi, h_lo)
            split(U_PLEP + 2)
            for j in range(KD):
                dve.wait_ge(evac_act, EVAC["pleg", j][1])
                link(tt(hf[:, j % 2, :], hf[:, j % 2, :], PP[:, j, :], ALU.mult))
                tt(X[:, j, :], X[:, j, :], hf[:, j % 2, :], ALU.add).then_inc(x_new[1], 1)
                if j % 2 and U_PLEG + j // 2 + 2 < N_UNITS:
                    split(U_PLEG + j // 2 + 2)
            variance(n_final)
            factors(n_final)
            dve.wait_ge(*n_final.factor(1))
            for k in range(KD):
                stt(OUT[:, k, :], X[:, k, :], gcol("norm_final_2", k), ps[:, R_BANK, :], ALU.mult, ALU.mult
                    ).then_inc(out_ready, 1)


def constants():
    import numpy as np

    c = np.zeros((P, C_COLS), np.float32)
    i = np.arange(P)
    c[:, C_ID:C_ID + P] = np.eye(P)
    c[:, C_ONE:C_ONE + P] = 1.0
    c[:, C_HONE:C_HONE + P] = i[:, None] // HD == i[None, :] // HD
    half = HD // 2
    for m in range(P):
        if m % HD < half:
            c[m + half, C_ROT + m] = -1.0
        else:
            c[m - half, C_ROT + m] = 1.0
    c[:, C_TRI:C_TRI + P] = np.where(i[:, None] >= i[None, :], -1.0, 0.0)
    c[:, C_NEG1:C_NEG1 + P] = -1.0
    c[:, C_SMASK:C_SMASK + P] = np.where(i[:, None] >= i[None, :], NEG, 0.0)
    c[:, C_MASK:C_MASK + P] = np.where(i[None, :] >= i[:, None], 0.0, NEG)
    c[:, C_MASK + P:C_MASK + 2 * P] = np.where(i[None, :] <= i[:, None], 0.0, NEG)
    t = np.arange(S, dtype=np.float32)
    row, col = np.floor(t / 64).astype(np.float32), (t % 64).astype(np.float32)
    quarter = HD // 4
    f_ax = np.float32(10000.0) ** (-np.arange(quarter, dtype=np.float32) / np.float32(quarter))
    f_1d = np.float32(10000.0) ** (-np.arange(half, dtype=np.float32) / np.float32(half))
    ang_a = np.concatenate([row[None, :] * f_ax[:, None], col[None, :] * f_ax[:, None]])
    ang_b = t[None, :] * f_1d[:, None]
    for ang, cos, sin in ((ang_a, C_COSA, C_SINA), (ang_b, C_COSB, C_SINB)):
        ang = np.concatenate([ang.astype(np.float32)] * 4).astype(np.float64)
        c[:, cos:cos + S], c[:, sin:sin + S] = np.cos(ang), np.sin(ang)
    for g, w in enumerate(POOL_WINDOWS):
        c[:, C_INVC + g * PADW:C_INVC + (g + 1) * PADW] = 1.0 / np.minimum(np.arange(PADW) + 1.0, w)
    return c


def tiles(w, order=None):
    k, n = w.shape
    t = w.reshape(k // P, P, n // P, P).transpose(2, 0, 1, 3)
    return t if order is None else t[order]


def pack(ts, per):
    import numpy as np

    ts = ts.reshape(-1, per, P, P).transpose(0, 2, 1, 3).reshape(-1, P, per * P)
    return np.pad(ts, ((0, 0), (0, 0), (0, RAW - per * P)))


def pack_pairs(a, b):
    import numpy as np

    return np.stack([pack(tiles(a), 16), pack(tiles(b), 16)], 1).reshape(-1, P, RAW)


def kernel(**inputs):
    import numpy as np
    import concourse.bacc as bacc
    from concourse import mybir
    from concourse.bass_utils import run_bass_kernel_spmd

    a = {n: np.asarray(v) for n, v in inputs.items()}
    weights = np.concatenate([
        pack(tiles(a["w_in"][0], ORDER1), 16),
        pack(tiles(a["w_out"][0]), 16),
        pack_pairs(a["w_gate"][0], a["w_up"][0]),
        pack(tiles(a["w_down"][0]), DOWN_TILES),
        pack(tiles(a["w_in_2"][0], ORDER2), 16),
        pack(a["w_pool_2"][0], 2),
        pack(tiles(a["w_branch_a_2"][0]), 16),
        pack(tiles(a["w_branch_b_2"][0]), 16),
        pack(tiles(a["w_out_2"][0]), 16),
        pack_pairs(a["w_ffn_gate_2"][0], a["w_ffn_up_2"][0]),
        pack(tiles(a["w_ffn_down_2"][0]), DOWN_TILES),
        pack(tiles(a["w_ple_proj_2"][0]), 16),
        pack(tiles(a["w_ple_gate_2"][0]), 16),
    ])
    cols = [a[n].reshape(-1, P).T for n in GAINS]
    cols += [np.concatenate([a[n].reshape(-1)] * 2)[:, None] for n in ("q_norm_a", "k_norm_a")]
    cols += [np.roll(c, HD // 2, axis=0) for c in cols[-2:]]
    cols.append(np.broadcast_to(a["sink_b"].reshape(1, NH), (P, NH)))
    arrays = {
        "x_t": np.ascontiguousarray(a["x"][0].T),
        "p_t": np.ascontiguousarray(a["p_2"][0, 0].T),
        "weights": np.ascontiguousarray(weights),
        "gains": np.ascontiguousarray(np.concatenate(cols, 1)),
        "constants": constants(),
    }
    nc = bacc.Bacc("TRN2", target_bir_lowering=False, num_devices=1)
    args = [nc.dram_tensor(n, v.shape, mybir.dt.from_np(v.dtype), kind="ExternalInput").ap()
            for n, v in arrays.items()]
    args.append(nc.dram_tensor("out_t", (D, S), mybir.dt.float32, kind="ExternalOutput").ap())
    build(nc, *args)
    r = run_bass_kernel_spmd(nc, [arrays], core_ids=[0])
    return r.results[0]["out_t"].T.reshape(1, S, D)
```
